# Optimizing a Trainium2 kernel written in Bass

```python
import jax, jax.numpy as jnp
from jax import lax
import numpy as np

D_MODEL = 1024
BATCH = 1
SEQ = 512
DEPTH = 1
DEC_BATCH = 8
DEC_SEQ = 8
PAST_LEN = 4096
PAGE_SIZE = 128

CONV_WIDTH = 3
CONV_DIM = D_MODEL
GLA_HEADS = 4
GLA_DK = D_MODEL // 2 // GLA_HEADS
GLA_DV = D_MODEL // GLA_HEADS
GLA_RANK = 16
GLA_TAU = 16.0
GLA_CHUNK = 16
D_FF = 2816
EPS = 1e-6
IN_SIZES = (CONV_DIM, CONV_DIM, CONV_DIM,
            GLA_HEADS * GLA_DK, GLA_HEADS * GLA_DK, GLA_HEADS * GLA_DV, GLA_HEADS * GLA_DV, GLA_RANK,
            D_MODEL, D_MODEL)
IN_COLS = sum(IN_SIZES)

kernel_name = "hybrid_conv_gla_convffn_step"

def rmsnorm(x, g):
    x32 = x.astype(jnp.float32)
    y = x32 * lax.rsqrt(jnp.mean(x32 * x32, axis=-1, keepdims=True) + EPS)
    return (y * g.astype(jnp.float32)).astype(x.dtype)

def causal_dwconv(u, buf, w, b):
    T = u.shape[1]
    ext = jnp.concatenate([buf.astype(u.dtype), u], axis=1)
    y = b + sum(w[j] * ext[:, j:j + T] for j in range(CONV_WIDTH))
    return y, ext[:, -(CONV_WIDTH - 1):]

def gla_recurrence(q, k, v, log_a, s0):
    B, T = q.shape[:2]
    L = GLA_CHUNK
    n = -(-T // L)
    pad = n * L - T

    def prep(t):
        t = jnp.pad(t, ((0, 0), (0, pad), (0, 0), (0, 0)))
        return t.reshape(B, n, L, t.shape[2], t.shape[3]).transpose(1, 0, 3, 2, 4)

    qc, kc, vc, ac = prep(q), prep(k), prep(v), prep(log_a)
    mask = jnp.tril(jnp.ones((L, L), dtype=bool))[None, None, :, :, None]

    def step(S, inp):
        qi, ki, vi, ai = inp
        qi = qi.astype(jnp.float32); ki = ki.astype(jnp.float32); vi = vi.astype(jnp.float32)
        bcum = jnp.cumsum(ai.astype(jnp.float32), axis=2)
        diff = bcum[:, :, :, None, :] - bcum[:, :, None, :, :]
        decay = jnp.exp(jnp.where(mask, diff, -jnp.inf))
        scores = jnp.einsum('bhtd,bhsd,bhtsd->bhts', qi, ki, decay)
        intra = jnp.einsum('bhts,bhsv->bhtv', scores, vi)
        inter = jnp.einsum('bhtd,bhdv->bhtv', qi * jnp.exp(bcum), S)
        b_last = bcum[:, :, -1:, :]
        S_new = jnp.exp(b_last[:, :, 0, :])[..., None] * S + jnp.einsum(
            'bhsd,bhsv->bhdv', ki * jnp.exp(b_last - bcum), vi)
        return S_new, intra + inter

    S_fin, o = lax.scan(step, s0.astype(jnp.float32), (qc, kc, vc, ac))
    o = o.transpose(1, 0, 3, 2, 4).reshape(B, n * L, GLA_HEADS, GLA_DV)[:, :T]
    return o, S_fin

def layer(x, c, conv_buf, gla_state, ffn_buf,
          w_ada, b_ada, norm_pre1, norm_post1, norm_pre2, norm_post2,
          w_in, conv_w, conv_b, w_a2, b_a, gla_norm, w_out,
          w_up, ffn_conv_w, ffn_conv_b, w_down):
    Bn, T = x.shape[:2]
    mod = jax.nn.silu(c) @ w_ada + b_ada
    sh1, sc1, g1, sh2, sc2, g2 = jnp.split(mod, 6, axis=-1)

    h = rmsnorm(x, norm_pre1) * (1 + sc1[:, None]) + sh1[:, None]
    proj = h @ w_in
    split_idx = [int(s) for s in np.cumsum(IN_SIZES)[:-1]]
    bg, cg, ua, q, k, v, r, lr, ga, gb = jnp.split(proj, split_idx, axis=-1)

    conv_out, conv_buf_new = causal_dwconv(cg * ua, conv_buf, conv_w, conv_b)
    y_a = bg * conv_out

    q = q.reshape(Bn, T, GLA_HEADS, GLA_DK) * (GLA_DK ** -0.5)
    k = k.reshape(Bn, T, GLA_HEADS, GLA_DK)
    v = v.reshape(Bn, T, GLA_HEADS, GLA_DV)
    log_a = jax.nn.log_sigmoid((lr @ w_a2 + b_a).astype(jnp.float32)) / GLA_TAU
    log_a = log_a.reshape(Bn, T, GLA_HEADS, GLA_DK)
    o, gla_state_new = gla_recurrence(q, k, v, log_a, gla_state)
    o = rmsnorm(o.astype(x.dtype), gla_norm)
    y_b = o.reshape(Bn, T, GLA_HEADS * GLA_DV) * jax.nn.silu(r)

    merged = jax.nn.sigmoid(ga) * y_a + jax.nn.sigmoid(gb) * y_b
    x = x + g1[:, None] * rmsnorm(merged @ w_out, norm_post1)

    h2 = rmsnorm(x, norm_pre2) * (1 + sc2[:, None]) + sh2[:, None]
    a, gt = jnp.split(h2 @ w_up, 2, axis=-1)
    a_conv, ffn_buf_new = causal_dwconv(a, ffn_buf, ffn_conv_w, ffn_conv_b)
    f = (jax.nn.gelu(a_conv) * gt) @ w_down
    x = x + g2[:, None] * rmsnorm(f, norm_post2)
    return x, conv_buf_new, gla_state_new.astype(gla_state.dtype), ffn_buf_new

def setup_inputs(seed: int = 0) -> dict:
    key = jax.random.key(seed)
    ks = jax.random.split(key, 32)
    nrm = jax.random.normal
    f32 = jnp.float32
    d = D_MODEL
    hk = GLA_HEADS * GLA_DK
    return {
        "x_prompt": nrm(ks[0], (BATCH, SEQ, d), f32),
        "x_sample": nrm(ks[1], (DEC_BATCH, DEC_SEQ, d), f32),
        "c_prompt": nrm(ks[2], (BATCH, d), f32),
        "c_sample": nrm(ks[3], (DEC_BATCH, d), f32),
        "state_conv_mix": nrm(ks[4], (DEPTH, DEC_BATCH, CONV_WIDTH - 1, CONV_DIM), f32),
        "state_gla": 0.3 * nrm(ks[5], (DEPTH, DEC_BATCH, GLA_HEADS, GLA_DK, GLA_DV), f32),
        "state_conv_ffn": nrm(ks[6], (DEPTH, DEC_BATCH, CONV_WIDTH - 1, D_FF), f32),
        "w_ada": 0.5 * d ** -0.5 * nrm(ks[7], (DEPTH, d, 6 * d), f32),
        "b_ada": 0.01 * nrm(ks[8], (DEPTH, 6 * d), f32),
        "norm_pre1": 1.0 + 0.1 * nrm(ks[9], (DEPTH, d), f32),
        "norm_post1": 1.0 + 0.1 * nrm(ks[10], (DEPTH, d), f32),
        "norm_pre2": 1.0 + 0.1 * nrm(ks[11], (DEPTH, d), f32),
        "norm_post2": 1.0 + 0.1 * nrm(ks[12], (DEPTH, d), f32),
        "w_in": d ** -0.5 * nrm(ks[13], (DEPTH, d, IN_COLS), f32),
        "conv_w": CONV_WIDTH ** -0.5 * nrm(ks[14], (DEPTH, CONV_WIDTH, CONV_DIM), f32),
        "conv_b": 0.01 * nrm(ks[15], (DEPTH, CONV_DIM), f32),
        "w_a2": GLA_RANK ** -0.5 * nrm(ks[16], (DEPTH, GLA_RANK, hk), f32),
        "b_a": 0.1 * nrm(ks[17], (DEPTH, hk), f32),
        "gla_norm": 1.0 + 0.1 * nrm(ks[18], (DEPTH, GLA_HEADS, GLA_DV), f32),
        "w_out": d ** -0.5 * nrm(ks[19], (DEPTH, d, d), f32),
        "w_up": d ** -0.5 * nrm(ks[20], (DEPTH, d, 2 * D_FF), f32),
        "ffn_conv_w": CONV_WIDTH ** -0.5 * nrm(ks[21], (DEPTH, CONV_WIDTH, D_FF), f32),
        "ffn_conv_b": 0.01 * nrm(ks[22], (DEPTH, D_FF), f32),
        "w_down": D_FF ** -0.5 * nrm(ks[23], (DEPTH, D_FF, d), f32),
    }

def reference(x_prompt, x_sample, c_prompt, c_sample, state_conv_mix, state_gla, state_conv_ffn,
              w_ada, b_ada, norm_pre1, norm_post1, norm_pre2, norm_post2,
              w_in, conv_w, conv_b, w_a2, b_a, gla_norm, w_out,
              w_up, ffn_conv_w, ffn_conv_b, w_down):
    xp, xs = x_prompt, x_sample
    pc, pg, pf, sc, sg, sf = [], [], [], [], [], []
    for l in range(DEPTH):
        weights = (w_ada[l], b_ada[l], norm_pre1[l], norm_post1[l], norm_pre2[l], norm_post2[l],
                   w_in[l], conv_w[l], conv_b[l], w_a2[l], b_a[l], gla_norm[l], w_out[l],
                   w_up[l], ffn_conv_w[l], ffn_conv_b[l], w_down[l])
        zc = jnp.zeros((xp.shape[0], CONV_WIDTH - 1, CONV_DIM), xp.dtype)
        zg = jnp.zeros((xp.shape[0], GLA_HEADS, GLA_DK, GLA_DV), state_gla.dtype)
        zf = jnp.zeros((xp.shape[0], CONV_WIDTH - 1, D_FF), xp.dtype)
        xp, c1, g1, f1 = layer(xp, c_prompt, zc, zg, zf, *weights)
        xs, c2, g2, f2 = layer(xs, c_sample, state_conv_mix[l], state_gla[l], state_conv_ffn[l], *weights)
        pc.append(c1); pg.append(g1); pf.append(f1)
        sc.append(c2); sg.append(g2); sf.append(f2)
    return (xp, xs,
            jnp.stack(pc), jnp.stack(pg), jnp.stack(pf),
            jnp.stack(sc), jnp.stack(sg), jnp.stack(sf))


_drawn_inputs = setup_inputs


def setup_inputs(seed=0):
    import zlib

    import numpy as np

    out = dict(_drawn_inputs(seed))
    spreads = {}
    factors = {'conv_b': 45.381, 'gla_norm': 3.847, 'ffn_conv_b': 22.245}
    for name, (base, spread) in spreads.items():
        noise = np.random.default_rng([zlib.crc32(name.encode()), seed]).standard_normal(out[name].shape)
        drawn = base * np.exp(spread * noise) if base else spread * noise
        out[name] = __import__('jax').numpy.asarray(drawn.astype(out[name].dtype))
    for name, factor in factors.items():
        out[name] = (out[name] * factor).astype(out[name].dtype)
    return out
```

```python
import numpy as np
import concourse.bass as bass
from concourse import mybir

F32 = mybir.dt.float32
F32R = mybir.dt.float32r
I32 = mybir.dt.int32
ALU = mybir.AluOpType
ACT = mybir.ActivationFunctionType

P = 128
D = 1024
KT = D // P
SEQ = 512
NS, TS = 8, 8
T = SEQ + NS * TS
HALF = T // 2
TT = 5
ROWS = [P, P, P, P, NS * TS]
HEADS, DK, DV = 4, 128, 256
RANK = 16
FF = 2816
FT = FF // P
EPS = 1e-6
TAU_INV = 1.0 / 16.0
NCH = SEQ // P
EXT = 2 + SEQ + NS * (2 + TS)
S0E = 2 + SEQ
CONV = EXT - 2

IN_BG, IN_CG, IN_UA = 0, D, 2 * D
IN_Q, IN_K, IN_V = 3 * D, 3 * D + HEADS * DK, 3 * D + 2 * HEADS * DK
IN_R = IN_V + HEADS * DV
IN_LR = IN_R + HEADS * DV
IN_GA = IN_LR + RANK
IN_GB = IN_GA + D

TILE_K, TILE_Q, TILE_V = 0, HEADS, 2 * HEADS
TILE_C1 = TILE_V + 8
TILE_C2 = TILE_C1 + 4 * KT
TILE_WO = TILE_C2 + 2 * KT
TILE_UP = TILE_WO + KT
TILE_DN = TILE_UP + 2 * FT
TILES = TILE_DN + FT
LEVELS = [0, 1, 2, 4, 8, 16, 32, 64]


def freed(n):
    return n + 1 if n < TILE_WO else n - 3


def layer_program(nc, a):
    base = 1152
    at = base

    def place(name, shape, dtype=F32, offset=None):
        nonlocal at
        size = int(np.prod(shape[1:])) * 4
        if offset is None:
            offset = at
            at += -(-size // 32) * 32
        return nc.alloc_sbuf_tensor_at(name, shape, dtype, offset=offset)

    raw = [place(f"raw{i}", [P, 1024]) for i in range(2)]
    w_hi = [place(f"w_hi{i}", [P, 1024], F32R) for i in range(4)]
    w_lo = [place(f"w_lo{i}", [P, 1024], F32R) for i in range(4)]
    x_at = at
    x_tok = place("x_tok", [P, TT, D])
    v_tok = place("v_tok", [P, TT, D], offset=x_at)
    h_at = at
    h_hi = place("h_hi", [P, KT, T], F32R)
    h_lo = place("h_lo", [P, KT, T], F32R)
    g_at = at
    at += 106496
    ada_first = place("ada_first", [P, KT, 2 * D], offset=g_at)
    q = place("q", [P, HEADS, T], offset=g_at)
    k = place("k", [P, HEADS, T], offset=g_at + 9216)
    pre = place("pre", [P, HEADS, T], offset=g_at + 18432)
    suf = place("suf", [P, HEADS, T], offset=g_at + 27648)
    kd = place("kd", [P, HEADS, T], offset=g_at + 36864)
    qd = place("qd", [P, HEADS * T // 2], offset=g_at + 46080)
    score = place("score", [P, TT * HEADS, P], offset=g_at + 50688)
    state = [place(f"state{i}", [P, HEADS, DV], offset=g_at + 60928 + 4096 * i) for i in range(2)]
    y_a = place("y_a", [P, KT, T], offset=g_at + 69632)
    h32 = place("h32", [P, KT, T], offset=g_at + 69632)
    o = place("o", [P, KT, T], offset=g_at + 88064)
    ada_next = place("ada_next", [P, KT, 512], offset=g_at + 88064)
    k_tok = [place(f"k_tok{i}", [P, HEADS * DK], offset=g_at + 27648 + 2048 * i) for i in range(2)]
    k_own = place("k_own", [NS * TS, NS, DK], offset=g_at + 31744)
    s_in = [place(f"s_in{i}", [P, 4, DV], offset=g_at + 36864 + 4096 * i) for i in range(3)]
    m_hi = place("m_hi", [P, KT, T], F32R, offset=g_at)
    m_lo = place("m_lo", [P, KT, T], F32R, offset=g_at + 18432)
    wo_hi = place("wo_hi", [P, 4, D], F32R, offset=g_at + 36864)
    wo_lo = place("wo_lo", [P, 4, D], F32R, offset=g_at + 53248)
    gate1 = place("gate1", [P, 2, D], offset=g_at + 69632)
    xn = place("xn", [P, D], offset=g_at + 77824)
    y_tmp = place("y_tmp", [P, D], offset=g_at + 81920)
    h2_32 = place("h2_32", [P, KT, P], offset=g_at + 86016)
    sq_tok = place("sq_tok", [P, D], offset=g_at + 90112)
    f_hi = place("f_hi", [P, FT, T], F32R, offset=g_at)
    f_lo = place("f_lo", [P, FT, T], F32R, offset=g_at + FT * T * 4)
    gate2 = place("gate2", [P, 2, D], offset=h_at)
    y_half = place("y_half", [P, TT, 512], offset=h_at + 8192)
    sq_half = place("sq_half", [P, 512], offset=h_at + 18432)
    t_at = at
    ext = place("ext", [P, EXT])
    cv = place("cv", [P, CONV])
    buf_a = place("buf_a", [P, T])
    buf_b = place("buf_b", [P, T])
    rows = place("rows", [P, P], offset=t_at)
    rows_ffn = place("rows_ffn", [P, P], offset=t_at + 512)
    rows_c = place("rows_c", [P, P], offset=t_at + 1024)
    rows_mix = place("rows_mix", [P, P], offset=t_at + 1536)
    rows_ff0 = place("rows_ff0", [P, 3, P], offset=t_at + 2048)
    w_lr = place("w_lr", [P, KT, RANK], offset=t_at + 3584)
    w_a2 = place("w_a2", [RANK, HEADS * DK], offset=t_at + 4096)
    lr = place("lr", [RANK, T], offset=t_at + 6144)
    sq0 = place("sq0", [P, D], offset=g_at + 88064)
    tails_out = place("tails_out", [P, 2, P], offset=t_at + 0)
    ftails_out = place("ftails_out", [P, 4, P], offset=h_at + 20480)
    buf_fin = place("buf_fin", [P, 512], offset=t_at)
    prm = place("prm", [P, 124])
    ffp = place("ffp", [P, 88])
    c_t = place("c_t", [P, 72])
    c_sig = place("c_sig", [P, 72])
    mix0 = place("mix0", [P, 16, KT])
    ff0 = place("ff0", [P, 16, FT])
    mod = place("mod", [P, 48, 9])
    ident = place("ident", [P, P])
    ones = place("ones", [P, P])
    mask = place("mask", [P, 7, 64])
    own = place("own", [NS * TS, NS])
    mul1 = place("mul1", [P, KT, 9])
    mul2 = place("mul2", [P, KT, 9])
    g1n = place("g1n", [P, KT, 9])
    g2n = place("g2n", [P, KT, 9])
    gx = place("gx", [P, KT, NS * TS])
    eps = place("eps", [P, 1])
    one = place("one", [P, 1])
    st_x = place("st_x", [P, 3, TT])
    st_y = place("st_y", [P, 3, TT])
    st_h = place("st_h", [P, 3, TT])
    st_f = place("st_f", [P, 4, TT])
    tail_mix = place("tail_mix", [P, 18, KT])
    tail_ff = place("tail_ff", [P, 18, FT])
    assert at <= 229368, at
    bank = [nc.alloc_psum_tensor(f"pair{i}", [P, 2, 512], F32) for i in range(4)]

    def one_bank(b):
        return bank[b // 2][:, b % 2, :]

    B_ADA, PRE1, POST1, PRE2, POST2, CW, CB, B_A, GN = 0, 48, 56, 64, 72, 80, 104, 112, 116
    FW, FB = 0, 66

    sems = {}

    def S(name):
        if name not in sems:
            sems[name] = nc.alloc_semaphore(name)
        return sems[name]

    w_in, w_up, w_down, w_out, w_ada = (a[n][0] for n in ("w_in", "w_up", "w_down", "w_out", "w_ada"))

    def in_cols(c0):
        return w_in[:, c0:c0 + P].rearrange("(k p) c -> p k c", p=P)

    def spread(v, n):
        if len(v.shape) == 2:
            return v.rearrange("p (m o) -> p m o", o=1).to_broadcast([v.shape[0], v.shape[1], n])
        return v.rearrange("p k (m o) -> p k m o", o=1).to_broadcast([v.shape[0], v.shape[1], v.shape[2], n])

    def row(buf, j):
        if isinstance(j, int):
            return buf[:, j, :]
        return buf[:, bass.ds(j, 1), :].rearrange("p o n -> p (o n)")

    def kc(tile):
        return tile[:, :].rearrange("p (k c) -> p k c", c=P)

    def k2(tile):
        return tile[:, :].rearrange("p (k c) -> p k c", c=512)

    def halves(buf):
        return buf.rearrange("p (a t) -> p a t", a=2)

    def out2(pair):
        return bank[pair][:, :, 0:HALF]

    def conv_pieces(pair, buf, first, s_step, s_skip):
        s_at = first + SEQ
        smp = buf[:, s_at:s_at + NS * s_step].rearrange("p (s w) -> p s w", w=s_step)[:, :, s_skip:s_skip + TS]
        return [
            (bank[pair][:, 0, 0:HALF], buf[:, first:first + HALF], 0, HALF),
            (bank[pair][:, 1, 0:SEQ - HALF], buf[:, first + HALF:first + SEQ], HALF, SEQ),
            (bank[pair][:, 1, SEQ - HALF:HALF].rearrange("p (s w) -> p s w", w=TS), smp, SEQ, T),
        ]

    def piece(buf, lo, hi):
        v = buf[:, lo:hi]
        return v.rearrange("p (s w) -> p s w", w=TS) if lo == SEQ else v

    def c1_pair(n):
        return n % 3

    C2_PAIR = [0, 1, 2, 0]

    items = []
    for lv, B in enumerate(LEVELS):
        groups = [[0], [1], [2], [3]] if B == 0 else [[0, 1], [2, 3]]
        for n, g in enumerate(groups):
            items.append((lv, g, False, n))
        items.append((lv, [4] if B < 8 else [], True, len(groups)))
    per_level = [[i for i, it in enumerate(items) if it[0] == lv] for lv in range(8)]

    def block_view(buf, B, ch_tokens, side):
        return buf.rearrange("p (n s b) -> p n s b", s=2, b=B)[:, :, side, :]

    def store_state(sp, u):
        h, g = u // 2, u % 2
        sp.wait_ge(S("s_done"), 4 * (u + 1))
        sp.dma_start(a["new_gla_sample"][0, 4 * g:4 * g + 4, h].rearrange("s d v -> d s v"), s_in[u % 3][:, :, :]) \
          .then_inc(S(f"s_stored{u % 3}"), 16)

    def level_exps(act, lv):
        B = LEVELS[lv]
        act.wait_ge(S("level_set"), lv)
        act.wait_ge(S("item"), per_level[lv - 1][-1] + 1)
        if B < 8:
            src = block_view(pre[:, :, :].rearrange("p h t -> p (h t)"), B, T, 1)
            dst = qd[:, :].rearrange("p (n b) -> p n b", b=B)
        else:
            src = pre[:, :, 0:SEQ].rearrange("p h (n s b) -> p h n s b", s=2, b=B)[:, :, :, 1, :]
            dst = qd[:, 0:HEADS * SEQ // 2].rearrange("p (h n b) -> p h n b", h=HEADS, b=B)
        act.activation(dst, src, ACT.Exp, scale=TAU_INV).then_inc(S("qd_exp"), 1)
        if B > 1:
            w = T if B < 8 else SEQ
            act.activation(kd[:, :, 0:w], suf[:, :, 0:w], ACT.Exp, scale=TAU_INV).then_inc(S("kd_exp"), 1)

    def act_out(act):
        for t in range(TT):
            m = ROWS[t]
            act.wait_ge(S("wo_mm"), t + 1)
            act.activation(sq_tok[0:m, :], bank[t % 3][0:m, :, :].rearrange("p a c -> p (a c)"), ACT.Square,
                           accum_out=st_y[0:m, 0, t:t + 1]).then_inc(S("y_sq"), 1)
            act.wait_ge(S("y_sq"), t + 1)
            act.activation(st_y[0:m, 1, t:t + 1], st_y[0:m, 0, t:t + 1], ACT.Sqrt, bias=eps[0:m, :], scale=1.0 / D) \
               .then_inc(S("y_root"), 1)
            act.wait_ge(S("x1_done"), t + 1)
            act.activation(sq_tok[0:m, :], x_tok[0:m, t, :], ACT.Square, accum_out=st_h[0:m, 0, t:t + 1]) \
               .then_inc(S("x1_sq"), 1)
            act.wait_ge(S("x1_sq"), t + 1)
            act.activation(st_h[0:m, 1, t:t + 1], st_h[0:m, 0, t:t + 1], ACT.Sqrt, bias=eps[0:m, :], scale=1.0 / D) \
               .then_inc(S("x1_root"), 1)
            act.wait_ge(S("h2_done"), t + 1)
            act.activation(h_hi[:, :, P * t:P * t + m], h2_32[:, :, 0:m], ACT.Copy).then_inc(S("h2_hi_done"), 1)

    def conv(dve, src, dst, w, b, name, count):
        dve.tensor_scalar(dst[:, :], src[:, 2:EXT], w[2], b, ALU.mult, ALU.add).then_inc(S(name), 1)
        for i, tap in enumerate((1, 0)):
            dve.wait_ge(S(name), count + (i + 1))
            dve.scalar_tensor_tensor(dst[:, :], src[:, tap:tap + CONV], w[tap], dst[:, :], ALU.mult, ALU.add) \
               .then_inc(S(name), 1)

    def tails(dve, dst, name):
        dve.tensor_copy(dst[:, 0:2], ext[:, SEQ:SEQ + 2]).then_inc(S(name), 1)
        last = ext[:, S0E:EXT].rearrange("p (s w) -> p s w", w=TS + 2)[:, :, TS:TS + 2]
        dve.tensor_copy(dst[:, 2:18].rearrange("p (s w) -> p s w", w=2), last).then_inc(S(name), 1)

    def dve_level(dve, lv):
        B = LEVELS[lv]
        if B:
            dve.wait_ge(S("level_set"), lv)
            dve.wait_ge(S("qd_exp"), lv)
            if B < 8:
                src = block_view(q[:, :, :].rearrange("p h t -> p (h t)"), B, T, 1)
                dst = qd[:, :].rearrange("p (n b) -> p n b", b=B)
            else:
                src = q[:, :, 0:SEQ].rearrange("p h (n s b) -> p h n s b", s=2, b=B)[:, :, :, 1, :]
                dst = qd[:, 0:HEADS * SEQ // 2].rearrange("p (h n b) -> p h n b", h=HEADS, b=B)
            dve.tensor_tensor(dst, dst, src, ALU.mult).then_inc(S("qd_done"), 1)
            if B > 1:
                w = T if B < 8 else SEQ
                dve.wait_ge(S("kd_exp"), lv - 1)
                dve.tensor_tensor(kd[:, :, 0:w], kd[:, :, 0:w], k[:, :, 0:w], ALU.mult).then_inc(S("kd_done"), 1)
            w = T if B < 8 else SEQ

            def side(buf, s, last=False):
                if B < 8:
                    v = buf[:, :, :].rearrange("p h t -> p (h t)").rearrange("p (n s b) -> p n s b", s=2, b=B)
                    v = v[:, :, s, B - 1:B] if last else v[:, :, s, :]
                    return v.to_broadcast([P, HEADS * T // (2 * B), B]) if last else v
                v = buf[:, :, 0:SEQ].rearrange("p h (n s b) -> p h n s b", s=2, b=B)
                v = v[:, :, :, s, B - 1:B] if last else v[:, :, :, s, :]
                return v.to_broadcast([P, HEADS, SEQ // (2 * B), B]) if last else v

            dve.tensor_tensor(side(suf, 0), side(suf, 0), side(pre, 1, True), ALU.add).then_inc(S("suf_add"), 1)
            dve.wait_ge(S("suf_add"), lv)
            dve.tensor_tensor(side(pre, 1), side(pre, 1), side(pre, 0, True), ALU.add).then_inc(S("level_set"), 1)

    def take_item(dve, i):
        lv, chunks, last, _ = items[i]
        B = LEVELS[lv]
        src = one_bank(6 + i % 2)
        dve.wait_ge(S("item"), i + 1)
        if chunks:
            ch, nch = chunks[0] * HEADS, len(chunks) * HEADS
            w = 64 if last else P
            m = 64 if last else P
            if B == 0:
                dst = score[0:m, ch:ch + nch, 0:w]
                msk = ident[0:m, 0:w].bitcast(I32).rearrange("p (o t) -> p o t", o=1).to_broadcast([m, nch, w])
                data = src[0:m, 0:nch * w].rearrange("p (c t) -> p c t", t=w)
            else:
                dst = score[0:m, ch:ch + nch, 0:w].rearrange("p c (n s b) -> p c n s b", s=2, b=B)[:, :, :, 1, :]
                msk = mask[0:m, lv - 1, 0:w // 2].bitcast(I32).rearrange("p (o n b) -> p o n b", o=1, b=B) \
                    .to_broadcast([m, nch, w // 2 // B, B])
                data = src[0:m, 0:nch * w // 2].rearrange("p (c n b) -> p c n b", c=nch, b=B)
            ins = dve.copy_predicated(dst, msk, data)
            if not last:
                ins.then_inc(S("item_taken"), 1)
            else:
                ins.then_inc(S("smp_scores"), 1)
        if last:
            dve.tensor_tensor(mod[:, 16 + 4 * lv:20 + 4 * lv, :], src[:, 256:292].rearrange("p (m s) -> p m s", s=9),
                              spread(prm[:, 16 + 4 * lv:20 + 4 * lv], 9), ALU.add) \
               .then_inc(S("mod_done"), 1)

    def dve_out(dve, t):
        m, g = ROWS[t], t // 4
        dve.wait_ge(S("y_root"), t + 1)
        dve.reciprocal(st_y[0:m, 2, t:t + 1], st_y[0:m, 1, t:t + 1]).then_inc(S("y_rstd"), 1)
        dve.wait_ge(S("y_rstd"), t + 1)
        if t > 0:
            dve.wait_ge(S("x1_done"), t)
        dve.scalar_tensor_tensor(y_tmp[0:m, :], bank[t % 3][0:m, :, :].rearrange("p a c -> p (a c)"),
                                 st_y[0:m, 2, t:t + 1], gate1[0:m, g, :], ALU.mult, ALU.mult).then_inc(S("y_scaled"), 1)
        dve.wait_ge(S("y_scaled"), t + 1)
        dve.tensor_tensor(x_tok[0:m, t, :], x_tok[0:m, t, :], y_tmp[0:m, :], ALU.add).then_inc(S("x1_done"), 1)
        dve.wait_ge(S("x1_root"), t + 1)
        dve.reciprocal(st_h[0:m, 2, t:t + 1], st_h[0:m, 1, t:t + 1]).then_inc(S("x1_rstd"), 1)
        dve.wait_ge(S("x1_rstd"), t + 1)
        if t > 0:
            dve.wait_ge(S("h_tr"), t)
        dve.tensor_scalar(xn[0:m, :], x_tok[0:m, t, :], st_h[0:m, 2, t:t + 1], None, ALU.mult).then_inc(S("xn2_done"), 1)
        dve.wait_ge(S("h_tr"), t + 1)
        if t > 0:
            dve.wait_ge(S("h2_hi_done"), t)
            dve.wait_ge(S("h2_lo_done"), t)
        src = bank[3][:, :, :].rearrange("p a (k t) -> p (a k) t", t=P)[:, :, 0:m]
        dst = h2_32[:, :, 0:m]
        if g == 0:
            mul, add = (v.to_broadcast([P, KT, P]) for v in (mul2[:, :, 0:1], mod[:, 24:32, 0:1]))
        else:
            src = src.rearrange("p k (s t) -> p k s t", t=TS)
            dst = dst.rearrange("p k (s t) -> p k s t", t=TS)
            mul, add = (spread(v, TS) for v in (mul2[:, :, 1:9], mod[:, 24:32, 1:9]))
        dve.tensor_tensor(dst, src, mul, ALU.mult).then_inc(S("h2_mul"), 1)
        dve.wait_ge(S("h2_mul"), t + 1)
        dve.tensor_tensor(dst, dst, add, ALU.add).then_inc(S("h2_done"), 1)
        dve.wait_ge(S("h2_hi_done"), t + 1)
        dve.tensor_tensor(h_lo[:, :, P * t:P * t + m], h2_32[:, :, 0:m], h_hi[:, :, P * t:P * t + m].bitcast(F32),
                          ALU.subtract).then_inc(S("h2_lo_done"), 1)

    with nc.Block() as block:

        @block.sync
        def _(sp):
            def load_raw(n, src, view=None):
                if n >= 2:
                    sp.wait_ge(S("w_lo_done"), n - 1)
                dst = raw[n % 2][:, :]
                if len(src.shape) == 3:
                    dst = dst.rearrange("p (k c) -> p k c", k=src.shape[1])
                sp.dma_start(dst, src).then_inc(S(f"raw_in{n % 2}"), 16)

            def row_load(dst, src, sem):
                sp.dma_start(dst, src).then_inc(S(sem), 16)

            row_load(rows_c[0:8, :], a["c_prompt"].rearrange("b (j p) -> (b j) p", p=P), "c_in")
            row_load(rows_c[8:72, :], a["c_sample"].rearrange("b (j p) -> (b j) p", p=P), "c_in")
            sp.dma_start(x_tok[:, 0:4, :], a["x_prompt"][0].rearrange("(t p) d -> p t d", p=P)).then_inc(S("x_in"), 16)
            sp.dma_start(x_tok[0:64, 4, :], a["x_sample"].rearrange("b t d -> (b t) d")).then_inc(S("x_in"), 16)
            r = 0
            for name in ("b_ada", "norm_pre1", "norm_post1", "norm_pre2", "norm_post2"):
                n = a[name].shape[1] // P
                row_load(rows[r:r + n, :], a[name].rearrange("o (j p) -> (o j) p", p=P), "rows_in")
                r += n
            row_load(rows[r:r + 24, :], a["conv_w"][0].rearrange("w (j p) -> (w j) p", p=P), "rows_in")
            row_load(rows[r + 24:r + 32, :], a["conv_b"].rearrange("o (j p) -> (o j) p", p=P), "rows_in")
            row_load(rows[r + 32:r + 36, :], a["b_a"].rearrange("o (j p) -> (o j) p", p=P), "rows_in")
            row_load(rows[r + 36:r + 44, :], a["gla_norm"][0].rearrange("h (j p) -> (h j) p", p=P), "rows_in")
            row_load(rows_ffn[0:66, :], a["ffn_conv_w"][0].rearrange("w (j p) -> (w j) p", p=P), "rows_in")
            row_load(rows_ffn[66:88, :], a["ffn_conv_b"].rearrange("o (j p) -> (o j) p", p=P), "rows_in")
            row_load(rows_mix[:, :], a["state_conv_mix"][0].rearrange("s w (j p) -> (s w j) p", p=P), "rows_in")
            ffr = a["state_conv_ffn"][0].rearrange("s w (j p) -> (s w j) p", p=P)
            for i in range(3):
                n = min(P, 352 - P * i)
                row_load(rows_ff0[0:n, i, :], ffr[P * i:P * i + n, :], "rows_in")
            ada_v = w_ada.rearrange("(k p) c -> p k c", p=P)
            for i in range(4):
                sp.dma_start(ada_first[:, :, 512 * i:512 * i + 512], ada_v[:, :, 512 * i:512 * i + 512]) \
                  .then_inc(S(f"ada_in{i}"), 16)
            sp.dma_start(w_lr[:, :, :], w_in[:, IN_LR:IN_LR + RANK].rearrange("(k p) c -> p k c", p=P)) \
              .then_inc(S("lr_in"), 16)
            sp.dma_start(w_a2[:, :], a["w_a2"][0]).then_inc(S("lr_in"), 16)
            for h in range(HEADS):
                load_raw(TILE_K + h, in_cols(IN_K + h * DK))
            for h in range(HEADS):
                load_raw(TILE_Q + h, in_cols(IN_Q + h * DK))
            v_w = w_in[:, IN_V:IN_V + D].rearrange("(g k p) c -> g p k c", p=P, k=2)
            for n in range(8):
                load_raw(TILE_V + n, v_w[n % 4, :, :, 512 * (n // 4):512 * (n // 4) + 512])
            def load_c2(n):
                load_raw(TILE_C2 + n, in_cols((IN_R, IN_GB)[n % 2] + P * (n // 2)))

            def load_ada(j):
                c0 = 2 * D + 512 * j
                sp.dma_start(ada_next[:, :, :], ada_v[:, :, c0:c0 + 512]).then_inc(S("ada_next_in"), 16)

            for j in range(KT):
                if j == 0:
                    sp.wait_ge(S("x_sq"), TT)
                    load_ada(0)
                for i, c0 in enumerate((IN_CG, IN_UA, IN_BG, IN_GA)):
                    load_raw(TILE_C1 + 4 * j + i, in_cols(c0 + P * j))
                if j > 0:
                    sp.wait_ge(S("item"), per_level[j - 1][-1] + 1)
                    load_ada(j)
            for n in range(3):
                load_c2(n)
            for u in range(8):
                h, g = u // 2, u % 2
                if u == 0:
                    sp.wait_ge(S("item"), len(items))
                if u >= 3:
                    sp.wait_ge(S(f"s_stored{u % 3}"), 16 * (u // 3))
                sp.dma_start(s_in[u % 3][:, :, :], a["state_gla"][0, 4 * g:4 * g + 4, h].rearrange("s d v -> d s v")) \
                  .then_inc(S(f"s_in{u % 3}"), 16)
                if u >= 1:
                    store_state(sp, u - 1)
            store_state(sp, 7)
            sp.wait_ge(S("state_done"), NCH)
            sp.dma_start(a["new_gla_prompt"][0, 0].rearrange("h d v -> d h v"), state[(NCH - 1) % 2][:, :, :]) \
              .then_inc(S("state_stored"), 16)
            sp.wait_ge(S("tails_out"), 2)
            tm = a["new_conv_mix_prompt"][0, 0].rearrange("w (j p) -> (w j) p", p=P)
            sp.dma_start(tm, tails_out[0:16, 0, :]).then_inc(S("tails_stored"), 16)
            ts = a["new_conv_mix_sample"][0].rearrange("s w (j p) -> (s w j) p", p=P)
            sp.dma_start(ts, tails_out[:, 1, :]).then_inc(S("tails_stored"), 16)
            for n in range(3, 2 * KT):
                load_c2(n)
                if n == 3:
                    sp.wait_ge(S("ds_mm"), 8)
                    sp.dma_start(x_tok[:, 0:4, :], a["x_prompt"][0].rearrange("(t p) d -> p t d", p=P)) \
                      .then_inc(S("x_in"), 16)
                    sp.dma_start(x_tok[0:64, 4, :], a["x_sample"].rearrange("b t d -> (b t) d")).then_inc(S("x_in"), 16)
            for n in range(KT):
                load_raw(TILE_WO + n, w_out[P * n:P * n + P, :])
            with sp.Fori(0, FT) as j:
                for i in range(2):
                    sp.wait_ge(S("w_lo_done"), j * 2 + (TILE_UP + i - 1))
                    src = w_up[:, bass.ds(j * P + i * FF, P)].rearrange("(k p) c -> p k c", p=P)
                    sp.dma_start(kc(raw[i]), src).then_inc(S(f"raw_in{i}"), 16)
            dn = w_down.rearrange("(g k p) c -> g p k c", p=P, k=2)
            for n in range(FT):
                load_raw(TILE_DN + n, dn[n % 11, :, :, 512 * (n // 11):512 * (n // 11) + 512])
            sp.wait_ge(S("ftails_out"), 4)
            fp = a["new_conv_ffn_prompt"][0, 0].rearrange("w (j p) -> (w j) p", p=P)
            sp.dma_start(fp, ftails_out[0:44, 3, :]).then_inc(S("out_stored"), 16)
            fs = a["new_conv_ffn_sample"][0].rearrange("s w (j p) -> (s w j) p", p=P)
            for i in range(3):
                n = min(P, 352 - P * i)
                sp.dma_start(fs[P * i:P * i + n, :], ftails_out[0:n, i, :]).then_inc(S("out_stored"), 16)
            for t in range(TT):
                sp.wait_ge(S("y_out"), t + 1)
                if t < 4:
                    dst = a["y_prompt"][0, P * t:P * t + P, :]
                else:
                    dst = a["y_sample"].rearrange("b t d -> (b t) d")
                sp.dma_start(dst, x_tok[0:ROWS[t], t, :]).then_inc(S("out_stored"), 16)
            sp.wait_ge(S("out_stored"), 16 * (4 + TT))
            sp.wait_ge(S("state_stored"), 16)
            sp.wait_ge(S("tails_stored"), 32)
            for u in range(3):
                sp.wait_ge(S(f"s_stored{u}"), 16 * ((7 - u) // 3 + 1))

        @block.gpsimd
        def _(pool):
            pool.memset(ident[:, :], 0.0).then_inc(S("p_set"), 1)
            pool.memset(mask[:, :, :], 1.0).then_inc(S("p_set"), 1)
            pool.memset(own[:, :], 1.0).then_inc(S("p_set"), 1)
            pool.memset(ones[:, :], 1.0).then_inc(S("p_set"), 1)
            pool.memset(eps[:, :], EPS).then_inc(S("p_set"), 1)
            pool.memset(one[:, :], 1.0).then_inc(S("p_set"), 1)
            pool.wait_ge(S("p_set"), 6)
            pool.affine_select(out=ident[:, :], in_=ident[:, :], compare_op=ALU.not_equal, fill=1.0, base=0,
                               pattern=[[-1, P]], channel_multiplier=1).then_inc(S("consts"), 1)
            for i, B in enumerate(LEVELS[1:]):
                m = mask[:, i, :].rearrange("p (n b) -> p n b", b=B)
                pool.affine_select(out=m, in_=m, compare_op=ALU.is_ge, fill=0.0, base=0,
                                   pattern=[[-2 * B, 64 // B], [0, B]], channel_multiplier=1).then_inc(S("p_sel"), 1)
                pool.wait_ge(S("p_sel"), i + 1)
                pool.affine_select(out=m, in_=m, compare_op=ALU.is_ge, fill=0.0, base=B - 1,
                                   pattern=[[2 * B, 64 // B], [0, B]], channel_multiplier=-1).then_inc(S("consts"), 1)
            pool.affine_select(out=own[:, :], in_=own[:, :], compare_op=ALU.is_ge, fill=0.0, base=0,
                               pattern=[[-TS, NS]], channel_multiplier=1).then_inc(S("p_sel"), 1)
            pool.wait_ge(S("p_sel"), 8)
            pool.affine_select(out=own[:, :], in_=own[:, :], compare_op=ALU.is_ge, fill=0.0, base=TS - 1,
                               pattern=[[TS, NS]], channel_multiplier=-1).then_inc(S("consts"), 1)

            def low(r, hi, lo, done):
                pool.wait_ge(S("w_hi_done"), done)
                pool.tensor_tensor(lo, raw[r % 2][:, :], hi.bitcast(F32), ALU.subtract).then_inc(S("w_lo_done"), 1)

            with pool.Fori(0, TILE_WO // 4) as g:
                for r in range(4):
                    low(r, w_hi[r][:, :], w_lo[r][:, :], g * 4 + (r + 1))
            for r in range(4):
                low(r, wo_hi[:, r, :], wo_lo[:, r, :], TILE_WO + r + 1)
            with pool.Fori(TILE_WO // 4 + 1, TILES // 4) as g:
                for r in range(4):
                    low(r, w_hi[r][:, :], w_lo[r][:, :], g * 4 + (r + 1))
            for n in range(TILES // 4 * 4, TILES):
                low(n, w_hi[n % 4][:, :], w_lo[n % 4][:, :], n + 1)

        @block.scalar
        def _(act):
            def high(n, turn=0):
                if isinstance(turn, int):
                    n, turn = n + 4 * turn, 0
                if n >= TILES:
                    return
                act.wait_ge(S(f"raw_in{n % 2}"), turn * 32 + 16 * (n // 2 + 1))
                if TILE_WO <= n < TILE_WO + 4:
                    if n == TILE_WO:
                        for u in range(3):
                            act.wait_ge(S(f"s_stored{u}"), 16 * ((7 - u) // 3 + 1))
                        act.wait_ge(S("state_stored"), 16)
                    dst = wo_hi[:, n - TILE_WO, :]
                else:
                    if n >= 4:
                        act.wait_ge(S("ring_free"), turn * 4 + (freed(n) - 4))
                    dst = w_hi[n % 4][:, :]
                act.activation(dst, raw[n % 2][:, :], ACT.Copy).then_inc(S("w_hi_done"), 1)

            act.wait_ge(S("c_tr"), 1)
            act.activation(c_sig[:, :], one_bank(2)[:, 0:72], ACT.Sigmoid).then_inc(S("c_sig"), 1)
            act.wait_ge(S("x_in"), 32)
            act.wait_ge(S("p_set"), 6)
            for t in range(TT):
                n = ROWS[t]
                if t > 0:
                    act.wait_ge(S("x_sq"), t)
                act.activation(sq0[0:n, :], x_tok[0:n, t, :], ACT.Square, accum_out=st_x[0:n, 0, t:t + 1]) \
                   .then_inc(S("x_sq"), 1)
            for t in range(TT):
                n = ROWS[t]
                act.wait_ge(S("x_sq"), t + 1)
                act.activation(st_x[0:n, 1, t:t + 1], st_x[0:n, 0, t:t + 1], ACT.Sqrt, bias=eps[0:n, :],
                               scale=1.0 / D).then_inc(S("x_root"), 1)
            for t in range(TT):
                n = ROWS[t]
                act.wait_ge(S("x_tr"), t + 1)
                src = bank[2 + t % 2][:, :, :].rearrange("p a (k t) -> p (a k) t", t=P)[:, :, 0:n]
                act.activation(h32[:, :, P * t:P * t + n], src, ACT.Copy).then_inc(S("x_ch"), 1)
            for n in range(3):
                high(n)
            for i in range(KT):
                act.wait_ge(S("h32_done"), i + 1)
                act.activation(h_hi[:, i, :], h32[:, i, :], ACT.Copy).then_inc(S("h_hi_done"), 1)
            act.wait_ge(S("lr_mm"), 1)
            act.activation(halves(lr[:, :]), bank[3][0:RANK, :, 0:HALF], ACT.Copy).then_inc(S("lr_done"), 1)
            for n in range(8):
                high(n + 3)
                dst = (k if n < 4 else q)[:, n % 4, :]
                act.wait_ge(S("ring_free"), n + 1)
                act.activation(halves(dst), out2(n % 3), ACT.Copy, scale=1.0 if n < 4 else DK ** -0.5) \
                   .then_inc(S("kq_done"), 1)
                if n < 4:
                    act.wait_ge(S("z_mm"), n + 1)
                    act.activation(halves(suf[:, n, :]), out2(3), ACT.Abs, bias=prm[:, B_A + n:B_A + n + 1]) \
                       .then_inc(S("z_abs"), 1)
            act.wait_ge(S("z_abs"), 4)
            act.activation(suf[:, :, :], suf[:, :, :], ACT.Exp, scale=-1.0).then_inc(S("z_exp"), 1)
            act.wait_ge(S("z_exp"), 1)
            act.activation(suf[:, :, :], suf[:, :, :], ACT.Ln, bias=one[:, :]).then_inc(S("z_ln"), 1)
            for n in range(TILE_V, TILE_C1):
                high(n + 3)
                if n % 4 == 3:
                    for t in range(TT):
                        m, c = ROWS[t], (n - TILE_V) // 4
                        if t < TT - 1:
                            act.wait_ge(S("v_mm"), (TT - 1) * c + t + 1)
                        else:
                            act.wait_ge(S("ring_free"), n + 1)
                        act.activation(v_tok[0:m, t, 512 * c:512 * c + 512], one_bank((TT * c + t) % 8)[0:m, :], ACT.Copy) \
                           .then_inc(S("v_done"), 1)
            for j in range(KT):
                n = TILE_C1 + 4 * j
                high(n + 3)
                act.wait_ge(S("ring_free"), n + 1)
                if j > 0:
                    act.wait_ge(S("u_done"), 3 * j)
                act.activation(halves(buf_a[:, :]), out2(c1_pair(n)), ACT.Copy).then_inc(S("cg_done"), 1)
                high(n + 4)
                high(n + 5)
                if j + 1 < KT:
                    level_exps(act, j + 1)
                high(n + 6)
                act.wait_ge(S("ring_free"), n + 4)
                if j > 0:
                    act.wait_ge(S("ya_done"), j)
                act.activation(halves(buf_b[:, :]), out2(c1_pair(n + 3)), ACT.Sigmoid).then_inc(S("sga_done"), 1)
            act.wait_ge(S("level_set"), 8)
            act.activation(suf[:, :, :], suf[:, :, :], ACT.Exp, scale=TAU_INV).then_inc(S("exp_suf"), 1)
            act.activation(pre[:, :, :], pre[:, :, :], ACT.Exp, scale=TAU_INV).then_inc(S("exp_pre"), 1)
            act.wait_ge(S("tails_tr"), 1)
            act.activation(tails_out[0:16, 0, :], one_bank(6)[0:16, 0:P], ACT.Copy).then_inc(S("tails_out"), 1)
            act.activation(tails_out[:, 1, :], one_bank(6)[:, P:2 * P], ACT.Copy).then_inc(S("tails_out"), 1)
            for c in range(NCH):
                act.wait_ge(S("k_tr"), c + 1)
                if c == 0:
                    act.wait_ge(S("k_dec"), 1)
                if c >= 2:
                    act.wait_ge(S("delta_mm"), c - 1)
                act.activation(k_tok[c % 2][:, :], one_bank(0)[:, :], ACT.Copy).then_inc(S("k_tok_done"), 1)
                act.wait_ge(S("o_mm"), c + 1)
                act.activation(o[:, :, P * c:P * c + P], bank[2][:, :, :].rearrange("p a (m t) -> p (a m) t", t=P),
                               ACT.Copy).then_inc(S("o_done"), 1)
            act.wait_ge(S("ds_mm"), 8)
            for half in range(2):
                dst = o[:, :, SEQ:T].rearrange("p (h e) t -> p h e t", e=2)[:, :, half, :]
                act.activation(dst, bank[3][:, half, 0:256].rearrange("p (h t) -> p h t", t=64), ACT.Copy) \
                   .then_inc(S("o_done"), 1)
            def gates_b(i):
                for e in range(2):
                    if e == 1:
                        act.wait_ge(S("ssq_mm"), i * 2 + 1)
                    elif not isinstance(i, int) or i > 0:
                        act.wait_ge(S("silu_r"), i * 2)
                    act.activation(buf_a[:, :], row(o, i * 2 + e), ACT.Square).then_inc(S("o_sq"), 1)
                act.wait_ge(S("ssq_mm"), i * 2 + 2)
                if not isinstance(i, int) or i > 0:
                    act.wait_ge(S("gb_used"), i * 2)
                act.activation(halves(buf_b[:, :]), out2(3), ACT.Sqrt, bias=eps[:, :], scale=1.0 / DV) \
                   .then_inc(S("o_root"), 1)
                for e in range(2):
                    n = TILE_C2 + 2 * e
                    high(n + 3, i)
                    act.wait_ge(S("ring_free"), i * 4 + (n + 1))
                    if e == 1:
                        act.wait_ge(S("silu_r"), i * 2 + 1)
                    act.activation(halves(buf_a[:, :]), out2(C2_PAIR[2 * e]), ACT.Sigmoid).then_inc(S("sr_done"), 1)
                    high(n + 4, i)
                    act.wait_ge(S("ring_free"), i * 4 + (n + 2))
                    if e == 0:
                        act.wait_ge(S("o_recip"), i + 1)
                    else:
                        act.wait_ge(S("gb_used"), i * 2 + 1)
                    act.activation(halves(buf_b[:, :]), out2(C2_PAIR[2 * e + 1]), ACT.Sigmoid).then_inc(S("sgb_done"), 1)
                    act.wait_ge(S("m_done"), i * 2 + (e + 1))
                    act.activation(row(m_hi, i * 2 + e), cv[:, 0:T], ACT.Copy).then_inc(S("m_hi_done"), 1)

            act.wait_ge(S("o_done"), NCH + 2)
            gates_b(0)
            with act.Fori(1, HEADS - 1) as i:
                gates_b(i)
            gates_b(HEADS - 1)
            for n in range(TILE_WO + 3, TILE_UP):
                high(n)
            act_out(act)
            for n in range(TILE_UP, TILE_UP + 3):
                high(n)
            def ffn_up(i):
                for e in range(2):
                    n = TILE_UP + 2 * e
                    high(n + 3, i)
                    act.wait_ge(S("ring_free"), i * 4 + freed(n))
                    if e == 1 or not isinstance(i, int) or i > 0:
                        act.wait_ge(S("ftail_done"), i * 4 + 2 * e)
                    for src, dst, _, _ in conv_pieces(2 * e, ext, 2, TS + 2, 2):
                        act.activation(dst, src, ACT.Copy).then_inc(S("a_done"), 1)
                    high(n + 4, i)
                    act.wait_ge(S("fconv"), i * 6 + (3 * e + 3))
                    act.activation(cv[:, :], cv[:, :], ACT.Gelu_apprx_tanh).then_inc(S("gelu_done"), 1)
                    act.wait_ge(S("f_done"), i * 6 + (3 * e + 3))
                    act.activation(row(f_hi, i * 2 + e), buf_b[:, :], ACT.Copy).then_inc(S("f_hi_done"), 1)

            act.wait_ge(S("ext_zero"), 2)
            ffn_up(0)
            with act.Fori(1, FT // 2) as i:
                ffn_up(i)
            for n in range(TILE_DN, TILES):
                high(n + 3)
                if n == TILE_DN + 2:
                    act.wait_ge(S("ftails_tr"), 1)
                    for i in range(4):
                        m = (P, P, 96, 44)[i]
                        act.activation(ftails_out[0:m, i, :], one_bank(5)[0:m, P * i:P * i + P], ACT.Copy) \
                           .then_inc(S("ftails_out"), 1)
                if n == TILE_DN + 10:
                    for t in range(TT):
                        m = ROWS[t]
                        if t < TT - 1:
                            act.wait_ge(S("dn_mm"), t + 1)
                        else:
                            act.wait_ge(S("ring_free"), freed(n))
                        if t > 0:
                            act.wait_ge(S("f_sq"), t)
                        act.activation(sq_half[0:m, :], one_bank(t)[0:m, :], ACT.Square, accum_out=st_f[0:m, 0, t:t + 1]) \
                           .then_inc(S("f_sq"), 1)
                        act.activation(y_half[0:m, t, :], one_bank(t)[0:m, :], ACT.Copy).then_inc(S("yh_done"), 1)
            for t in range(TT):
                m = ROWS[t]
                if t < TT - 1:
                    act.wait_ge(S("dn_mm"), TT - 1 + t + 1)
                else:
                    act.wait_ge(S("ring_free"), freed(TILES - 1))
                act.wait_ge(S("f_sq"), TT + t)
                act.activation(sq_half[0:m, :], one_bank((TT + t) % 8)[0:m, :], ACT.Square, accum_out=st_f[0:m, 1, t:t + 1]) \
                   .then_inc(S("f_sq"), 1)
                act.wait_ge(S("f_sum"), t + 1)
                act.activation(st_f[0:m, 3, t:t + 1], st_f[0:m, 2, t:t + 1], ACT.Sqrt, bias=eps[0:m, :], scale=1.0 / D) \
                   .then_inc(S("f_root"), 1)

        @block.vector
        def _(dve):
            dve.wait_ge(S("c_sig"), 1)
            dve.tensor_tensor(c_t[:, :], one_bank(2)[:, 0:72], c_sig[:, :], ALU.mult).then_inc(S("c_done"), 1)
            dve.wait_ge(S("rows_tr"), 4)
            dve.tensor_copy(prm[:, :], one_bank(0)[:, 0:124]).then_inc(S("prm_done"), 1)
            dve.tensor_copy(ffp[:, :], one_bank(1)[:, 0:88]).then_inc(S("prm_done"), 1)
            dve.tensor_copy(mix0[:, :, :].rearrange("p a j -> p (a j)"), one_bank(3)[:, 0:P]).then_inc(S("prm_done"), 1)
            dve.tensor_copy(ff0[:, :, :].rearrange("p a j -> p (a j)"), one_bank(4)[:, 0:352]).then_inc(S("prm_done"), 1)
            for t in range(TT):
                n = ROWS[t]
                dve.wait_ge(S("x_root"), t + 1)
                dve.reciprocal(st_x[0:n, 2, t:t + 1], st_x[0:n, 1, t:t + 1]).then_inc(S("x_rstd"), 1)
                dve.wait_ge(S("x_rstd"), t + 1)
                dve.tensor_scalar(x_tok[0:n, t, :], x_tok[0:n, t, :], st_x[0:n, 2, t:t + 1], None, ALU.mult) \
                   .then_inc(S("xn_done"), 1)
            dve.wait_ge(S("ada0_mm"), 1)
            dve.wait_ge(S("prm_done"), 4)
            dve.tensor_tensor(mod[:, 0:16, :], one_bank(0)[:, 0:144].rearrange("p (m s) -> p m s", s=9),
                              spread(prm[:, 0:16], 9),
                              ALU.add).then_inc(S("mod_done"), 1)
            dve.wait_ge(S("mod_done"), 1)
            dve.scalar_tensor_tensor(mul1[:, :, :], mod[:, 8:16, :], 1.0, spread(prm[:, PRE1:PRE1 + 8], 9),
                                     ALU.add, ALU.mult).then_inc(S("mul1_done"), 1)
            dve.wait_ge(S("mul1_done"), 1)
            dve.wait_ge(S("x_ch"), TT)
            for i in range(KT):
                smp = h32[:, i, SEQ:T].rearrange("p (s t) -> p s t", t=TS)
                dve.tensor_scalar(h32[:, i, 0:SEQ], h32[:, i, 0:SEQ], mul1[:, i, 0:1], mod[:, i, 0:1], ALU.mult, ALU.add) \
                   .then_inc(S("h_prompt"), 1)
                dve.tensor_tensor(smp, smp, spread(mul1[:, i, 1:9], TS), ALU.mult) \
                   .then_inc(S("h_smp"), 1)
                if i > 0:
                    dve.wait_ge(S("h_hi_done"), i)
                    dve.tensor_tensor(h_lo[:, i - 1, :], h32[:, i - 1, :], h_hi[:, i - 1, :].bitcast(F32), ALU.subtract) \
                       .then_inc(S("h_lo_done"), 1)
                dve.wait_ge(S("h_smp"), i + 1)
                dve.wait_ge(S("h_prompt"), i + 1)
                dve.tensor_tensor(smp, smp, spread(mod[:, i, 1:9], TS), ALU.add) \
                   .then_inc(S("h32_done"), 1)
            dve.wait_ge(S("h_hi_done"), KT)
            dve.wait_ge(S("h32_done"), KT)
            dve.tensor_tensor(h_lo[:, KT - 1, :], h32[:, KT - 1, :], h_hi[:, KT - 1, :].bitcast(F32), ALU.subtract) \
               .then_inc(S("h_lo_done"), 1)
            for h in range(HEADS):
                dve.wait_ge(S("z_mm"), h + 1)
                dve.wait_ge(S("z_abs"), h + 1)
                dve.tensor_scalar(halves(pre[:, h, :]), out2(3), prm[:, B_A + h:B_A + h + 1], 0.0, ALU.add, ALU.min) \
                   .then_inc(S("z_min"), 1)
            dve.memset(score[:, :, :], 0.0).then_inc(S("score_zero"), 1)
            dve.wait_ge(S("z_ln"), 1)
            dve.wait_ge(S("z_min"), 4)
            dve.tensor_tensor(pre[:, :, :], pre[:, :, :], suf[:, :, :], ALU.subtract).then_inc(S("log_a"), 1)
            dve.wait_ge(S("log_a"), 1)
            dve.memset(suf[:, :, :], 0.0).then_inc(S("level_set"), 1)
            dve.memset(ext[:, 0:2], 0.0).then_inc(S("ext_zero"), 1)
            dve.wait_ge(S("ext_zero"), 1)
            dve.wait_ge(S("level_set"), 1)
            dve.wait_ge(S("score_zero"), 1)
            dve.wait_ge(S("consts"), 9)
            for j in range(KT):
                dve_level(dve, j)
                mine = per_level[j]
                n = TILE_C1 + 4 * j
                for i in mine[:1]:
                    take_item(dve, i)
                if j > 0:
                    dve.wait_ge(S("tail_done"), 2 * j)
                    dve.wait_ge(S("conv"), 3 * j)
                hist = ext[:, S0E:EXT].rearrange("p (s w) -> p s w", w=TS + 2)[:, :, 0:2]
                dve.tensor_copy(hist, mix0[:, :, j].rearrange("p (s w) -> p s w", w=2)).then_inc(S("hist"), 1)
                dve.wait_ge(S("cg_done"), j + 1)
                dve.wait_ge(S("ring_free"), n + 2)
                for src, dst, lo, hi in conv_pieces(c1_pair(n + 1), ext, 2, TS + 2, 2):
                    dve.tensor_tensor(dst, src, piece(buf_a, lo, hi), ALU.mult).then_inc(S("u_done"), 1)
                for i in mine[1:2]:
                    take_item(dve, i)
                dve.wait_ge(S("u_done"), 3 * (j + 1))
                dve.wait_ge(S("hist"), j + 1)
                if j > 0:
                    dve.wait_ge(S("t_done"), 3 * j)
                conv(dve, ext, cv, [prm[:, CW + 8 * w + j:CW + 8 * w + j + 1] for w in range(3)],
                     prm[:, CB + j:CB + j + 1], "conv", 3 * j)
                tails(dve, tail_mix[:, :, j], "tail_done")
                dve.wait_ge(S("conv"), 3 * j + 3)
                dve.wait_ge(S("ring_free"), n + 3)
                for src, cvp, lo, hi in conv_pieces(c1_pair(n + 2), cv, 0, TS + 2, 2):
                    dve.tensor_tensor(piece(y_a[:, j, :], lo, hi), src, cvp, ALU.mult).then_inc(S("t_done"), 1)
                for i in mine[2:]:
                    take_item(dve, i)
                dve.wait_ge(S("t_done"), 3 * (j + 1))
                dve.wait_ge(S("sga_done"), j + 1)
                dve.tensor_tensor(y_a[:, j, :], y_a[:, j, :], buf_b[:, :], ALU.mult).then_inc(S("ya_done"), 1)
            dve.wait_ge(S("mod_done"), 9)
            dve.scalar_tensor_tensor(mul2[:, :, :], mod[:, 32:40, :], 1.0, spread(prm[:, PRE2:PRE2 + 8], 9),
                                     ALU.add, ALU.mult).then_inc(S("scales"), 1)
            dve.tensor_tensor(g1n[:, :, :], mod[:, 16:24, :], spread(prm[:, POST1:POST1 + 8], 9),
                              ALU.mult).then_inc(S("scales"), 1)
            dve.tensor_tensor(g2n[:, :, :], mod[:, 40:48, :], spread(prm[:, POST2:POST2 + 8], 9),
                              ALU.mult).then_inc(S("scales"), 1)
            dve.wait_ge(S("scales"), 3)
            dve.tensor_copy(gx[:, :, :].rearrange("p k (s t) -> p k s t", t=TS), spread(g1n[:, :, 1:9], TS)) \
               .then_inc(S("gx_done"), 1)
            dve.wait_ge(S("exp_suf"), 1)
            dve.wait_ge(S("item"), len(items))
            dve.tensor_tensor(k[:, :, :], k[:, :, :], suf[:, :, :], ALU.mult).then_inc(S("k_dec"), 1)
            dve.wait_ge(S("exp_pre"), 1)
            dve.tensor_tensor(q[:, :, :], q[:, :, :], pre[:, :, :], ALU.mult).then_inc(S("q_dec"), 1)
            for c in range(NCH):
                dve.wait_ge(S("delta_mm"), c + 1)
                if c >= 2:
                    dve.wait_ge(S("o_mm"), c)
                new, old = state[c % 2], state[(c - 1) % 2]
                for h in range(HEADS):
                    delta = bank[1][:, :, :].rearrange("p a (h v) -> p (a h) v", v=DV)[:, h, :]
                    if c == 0:
                        ins = dve.tensor_copy(new[:, h, :], delta)
                    else:
                        if h == 0:
                            dve.wait_ge(S("state_done"), c)
                        ins = dve.scalar_tensor_tensor(new[:, h, :], old[:, h, :], pre[:, h, P * c + P - 1:P * c + P],
                                                       delta, ALU.mult, ALU.add)
                    if h == HEADS - 1:
                        ins.then_inc(S("state_done"), 1)
                    else:
                        ins.then_inc(S("state_part"), 1)
            for u in range(8):
                h, g = u // 2, u % 2
                if g == 0:
                    dve.wait_ge(S("ks_tr"), 1)
                    if h > 0:
                        dve.wait_ge(S("ds_mm"), 2 * h)
                    src = one_bank(1)[0:64, DK * h:DK * h + DK].rearrange("p (o d) -> p o d", o=1)
                    dve.tensor_tensor(k_own[:, :, :], src.to_broadcast([64, NS, DK]),
                                      spread(own[:, :], DK), ALU.mult).then_inc(S("k_own"), 1)
                dve.wait_ge(S("ds_mm"), u + 1)
                dve.wait_ge(S(f"s_in{u % 3}"), 16 * (u // 3 + 1))
                for s in range(4):
                    tok = SEQ + (4 * g + s) * TS + TS - 1
                    delta = bank[1 + u % 2][:, :, :].rearrange("p a (s v) -> p (a s) v", v=DV)[:, s, :]
                    dve.scalar_tensor_tensor(s_in[u % 3][:, s, :], s_in[u % 3][:, s, :], pre[:, h, tok:tok + 1], delta,
                                             ALU.mult, ALU.add).then_inc(S("s_done"), 1)
            dve.wait_ge(S("o_done"), NCH + 2)
            dve.wait_ge(S("tails_stored"), 32)
            dve.wait_ge(S("t_done"), 3 * KT)

            def merge(i):
                dve.wait_ge(S("o_root"), i + 1)
                dve.reciprocal(ext[:, 0:T], buf_b[:, :]).then_inc(S("o_recip"), 1)
                for e in range(2):
                    j = i * 2 + e
                    if e == 0:
                        dve.wait_ge(S("o_recip"), i + 1)
                    dve.tensor_tensor(row(o, j), row(o, j), ext[:, 0:T], ALU.mult).then_inc(S("o_norm"), 1)
                    dve.wait_ge(S("sr_done"), i * 2 + (e + 1))
                    if e == 1 or not isinstance(i, int) or i > 0:
                        dve.wait_ge(S("m_hi_done"), i * 2 + e)
                        dve.wait_ge(S("m_lo_done"), i * 2 + e)
                    dve.tensor_tensor(halves(cv[:, 0:T]), out2(C2_PAIR[2 * e]), halves(buf_a[:, :]), ALU.mult) \
                       .then_inc(S("silu_r"), 1)
                    dve.wait_ge(S("silu_r"), i * 2 + (e + 1))
                    dve.wait_ge(S("sgb_done"), i * 2 + (e + 1))
                    dve.tensor_tensor(cv[:, 0:T], cv[:, 0:T], buf_b[:, :], ALU.mult).then_inc(S("gb_used"), 1)
                    dve.wait_ge(S("gb_used"), i * 2 + (e + 1))
                    dve.wait_ge(S("o_norm"), i * 2 + (e + 1))
                    norm = prm[:, GN + j:GN + j + 1] if isinstance(j, int) else prm[:, bass.ds(j + GN, 1)]
                    dve.scalar_tensor_tensor(row(o, j), row(o, j), norm, cv[:, 0:T], ALU.mult, ALU.mult) \
                       .then_inc(S("y_b"), 1)
                    dve.wait_ge(S("y_b"), i * 2 + (e + 1))
                    dve.tensor_tensor(cv[:, 0:T], row(o, j), row(y_a, j), ALU.add).then_inc(S("m_done"), 1)
                    dve.wait_ge(S("m_done"), i * 2 + (e + 1))
                    dve.wait_ge(S("m_hi_done"), i * 2 + (e + 1))
                    dve.tensor_tensor(row(m_lo, j), cv[:, 0:T], row(m_hi, j).bitcast(F32), ALU.subtract) \
                       .then_inc(S("m_lo_done"), 1)

            merge(0)
            with dve.Fori(1, HEADS) as i:
                merge(i)
            dve.memset(ext[:, 0:2], 0.0).then_inc(S("ext_zero"), 1)
            for g in range(2):
                dve.wait_ge(S("gate1_mm"), g + 1)
                dve.wait_ge(S("m_lo_done"), KT)
                m = P if g == 0 else 64
                dve.tensor_copy(gate1[0:m, g, :], bank[3][0:m, :, :].rearrange("p a c -> p (a c)")) \
                   .then_inc(S("gate1_done"), 1)
            dve.wait_ge(S("x_in"), 64)
            dve.wait_ge(S("gate1_done"), 2)
            for t in range(TT):
                dve_out(dve, t)
            def ffn_mid(i):
                for e in range(2):
                    j = i * 2 + e
                    col = (lambda x: ffp[:, j + x:j + x + 1]) if isinstance(i, int) else (lambda x: ffp[:, bass.ds(j + x, 1)])
                    n = TILE_UP + 2 * e
                    later = e == 1 or not isinstance(i, int) or i > 0
                    if later:
                        dve.wait_ge(S("ftail_done"), i * 4 + 2 * e)
                    hist = ext[:, S0E:EXT].rearrange("p (s w) -> p s w", w=TS + 2)[:, :, 0:2]
                    if isinstance(i, int):
                        old = ff0[:, :, j].rearrange("p (s w) -> p s w", w=2)
                        new = tail_ff[:, :, j]
                    else:
                        old = ff0[:, :, bass.ds(j, 1)].rearrange("p (s w) o -> p s (w o)", w=2)
                        new = tail_ff[:, :, bass.ds(j, 1)].rearrange("p a o -> p (a o)")
                    dve.tensor_copy(hist, old).then_inc(S("fhist"), 1)
                    dve.wait_ge(S("a_done"), i * 6 + (3 * e + 3))
                    dve.wait_ge(S("fhist"), i * 2 + (e + 1))
                    if later:
                        dve.wait_ge(S("f_done"), i * 6 + 3 * e)
                    conv(dve, ext, cv, [col(FW + FT * w) for w in range(3)], col(FB), "fconv", i * 6 + 3 * e)
                    tails(dve, new, "ftail_done")
                    dve.wait_ge(S("gelu_done"), i * 2 + (e + 1))
                    dve.wait_ge(S("ring_free"), i * 4 + freed(n + 1))
                    for src, cvp, lo, hi in conv_pieces(2 * e + 1, cv, 0, TS + 2, 2):
                        dve.tensor_tensor(piece(buf_b, lo, hi), src, cvp, ALU.mult).then_inc(S("f_done"), 1)
                    dve.wait_ge(S("f_done"), i * 6 + (3 * e + 3))
                    dve.wait_ge(S("f_hi_done"), i * 2 + (e + 1))
                    dve.tensor_tensor(row(f_lo, j), buf_b[:, :], row(f_hi, j).bitcast(F32), ALU.subtract) \
                       .then_inc(S("f_lo_done"), 1)

            dve.wait_ge(S("ext_zero"), 2)
            ffn_mid(0)
            with dve.Fori(1, FT // 2) as i:
                ffn_mid(i)
            dve.tensor_copy(gx[:, :, :].rearrange("p k (s t) -> p k s t", t=TS), spread(g2n[:, :, 1:9], TS)) \
               .then_inc(S("gx_done"), 1)
            for g in range(2):
                dve.wait_ge(S("gate2_mm"), g + 1)
                m = P if g == 0 else 64
                dve.tensor_copy(gate2[0:m, g, :], bank[3][0:m, :, :].rearrange("p a c -> p (a c)")) \
                   .then_inc(S("gate2_done"), 1)
            for t in range(TT):
                m, g = ROWS[t], t // 4
                dve.wait_ge(S("f_sq"), TT + t + 1)
                dve.wait_ge(S("gate2_done"), 2)
                dve.tensor_tensor(st_f[0:m, 2, t:t + 1], st_f[0:m, 0, t:t + 1], st_f[0:m, 1, t:t + 1], ALU.add) \
                   .then_inc(S("f_sum"), 1)
                dve.wait_ge(S("f_root"), t + 1)
                dve.reciprocal(st_f[0:m, 2, t:t + 1], st_f[0:m, 3, t:t + 1]).then_inc(S("f_rstd"), 1)
                dve.wait_ge(S("f_rstd"), t + 1)
                dve.wait_ge(S("yh_done"), t + 1)
                dve.scalar_tensor_tensor(y_half[0:m, t, :], y_half[0:m, t, :], st_f[0:m, 2, t:t + 1],
                                         gate2[0:m, g, 0:512], ALU.mult, ALU.mult).then_inc(S("fin_a"), 1)
                if t > 0:
                    dve.wait_ge(S("y_out"), t)
                dve.scalar_tensor_tensor(buf_fin[0:m, :], one_bank((TT + t) % 8)[0:m, :], st_f[0:m, 2, t:t + 1],
                                         gate2[0:m, g, 512:1024], ALU.mult, ALU.mult).then_inc(S("fin_a"), 1)
                dve.wait_ge(S("fin_a"), 2 * t + 1)
                dve.tensor_tensor(x_tok[0:m, t, 0:512], x_tok[0:m, t, 0:512], y_half[0:m, t, :], ALU.add) \
                   .then_inc(S("fin_b"), 1)
                dve.wait_ge(S("fin_a"), 2 * t + 2)
                dve.tensor_tensor(x_tok[0:m, t, 512:1024], x_tok[0:m, t, 512:1024], buf_fin[0:m, :], ALU.add) \
                   .then_inc(S("y_out"), 1)

        @block.tensor
        def _(pe):
            pe.wait_ge(S("consts"), 9)
            pe.wait_ge(S("c_in"), 32)
            pe.transpose(one_bank(2)[:, 0:72], rows_c[0:72, :], ident[0:72, 0:72]).then_inc(S("c_tr"), 1)
            pe.wait_ge(S("rows_in"), 16 * 15)
            pe.transpose(one_bank(0)[:, 0:124], rows[0:124, :], ident[0:124, 0:124]).then_inc(S("rows_tr"), 1)
            pe.transpose(one_bank(1)[:, 0:88], rows_ffn[0:88, :], ident[0:88, 0:88]).then_inc(S("rows_tr"), 1)
            pe.transpose(one_bank(3)[:, 0:P], rows_mix[:, :], ident[:, :]).then_inc(S("rows_tr"), 1)
            for i in range(3):
                n = min(P, 352 - P * i)
                ins = pe.transpose(one_bank(4)[:, P * i:P * i + n], rows_ff0[0:n, i, :], ident[0:n, 0:n])
            ins.then_inc(S("rows_tr"), 1)
            pe.wait_ge(S("prm_done"), 4)
            for t in range(TT):
                n = ROWS[t]
                pe.wait_ge(S("xn_done"), t + 1)
                if t >= 2:
                    pe.wait_ge(S("x_ch"), t - 1)
                for i in range(KT):
                    dst = bank[2 + t % 2][:, i // 4, P * (i % 4):P * (i % 4) + n]
                    ins = pe.transpose(dst, x_tok[0:n, t, P * i:P * i + P], ident[0:n, 0:n])
                ins.then_inc(S("x_tr"), 1)
            pe.wait_ge(S("c_done"), 1)
            cond = c_t[:, :].rearrange("p (s j) -> p j s", j=KT)

            def ada(dst, weights, cols):
                for i in range(KT):
                    ins = pe.matmul(dst, weights[:, i, cols:cols + P], cond[:, i, :], start=i == 0, stop=i == KT - 1)
                return ins

            for m in range(16):
                if m % 4 == 0:
                    pe.wait_ge(S(f"ada_in{m // 4}"), 16)
                ins = ada(one_bank(0)[:, 9 * m:9 * m + 9], ada_first, P * m)
            ins.then_inc(S("ada0_mm"), 1)

            def channel_tile(hi, lo, pair, xs, last_sem=True, first=False):
                x_hi, x_lo = xs
                for i in range(KT):
                    if first:
                        pe.wait_ge(S("h_lo_done"), i + 1)
                    for w, x, p in ((hi, x_hi, 0), (hi, x_lo, 1), (lo, x_hi, 2)):
                        for half in range(2):
                            ins = pe.matmul(bank[pair][:, half, 0:HALF], w[:, i, :],
                                            x[:, i, HALF * half:HALF * half + HALF],
                                            start=i == 0 and p == 0, stop=i == KT - 1 and p == 2)
                ins.then_inc(S("ring_free"), 1)

            pe.wait_ge(S("lr_in"), 32)
            for half in range(2):
                for i in range(KT):
                    pe.wait_ge(S("h32_done"), i + 1) if half == 0 else None
                    ins = pe.matmul(bank[3][0:RANK, half, 0:HALF], w_lr[:, i, :],
                                    h32[:, i, HALF * half:HALF * half + HALF], start=i == 0, stop=i == KT - 1)
            ins.then_inc(S("lr_mm"), 1)
            for n in range(8):
                pe.wait_ge(S("w_lo_done"), n + 1)
                if n >= 3:
                    pe.wait_ge(S("kq_done"), n - 2)
                channel_tile(kc(w_hi[n % 4]), kc(w_lo[n % 4]), n % 3, (h_hi, h_lo), first=n == 0)
                if n < 4:
                    pe.wait_ge(S("lr_done"), 1)
                    if n > 0:
                        pe.wait_ge(S("z_min"), n)
                    for half in range(2):
                        ins = pe.matmul(bank[3][:, half, 0:HALF], w_a2[:, DK * n:DK * n + DK],
                                        lr[:, HALF * half:HALF * half + HALF], start=True, stop=True)
                    ins.then_inc(S("z_mm"), 1)
                if n == 3:
                    pass

            def token_tiles(n, g, banks, x_hi, x_lo, first, last, done):
                wh, wl = k2(w_hi[n % 4]), k2(w_lo[n % 4])
                for t in range(TT):
                    m = ROWS[t]
                    for i in range(2):
                        xh = x_hi[:, 2 * g + i, P * t:P * t + m]
                        xl = x_lo[:, 2 * g + i, P * t:P * t + m]
                        for p, (x, w) in enumerate(((xh, wh), (xh, wl), (xl, wh))):
                            ins = pe.matmul(one_bank(banks[t])[0:m, :], x, w[:, i, :],
                                            start=first and i == 0 and p == 0, stop=last and i == 1 and p == 2)
                    if last and t < TT - 1:
                        ins.then_inc(S(done), 1)
                return ins

            for n in range(8):
                c = n // 4
                pe.wait_ge(S("w_lo_done"), TILE_V + n + 1)
                if n == 0:
                    pe.wait_ge(S("kq_done"), 8)
                if n == 4:
                    pe.wait_ge(S("z_min"), 4)
                    pe.wait_ge(S("v_done"), 2)
                ins = token_tiles(TILE_V + n, n % 4, [(TT * c + t) % 8 for t in range(TT)], h_hi, h_lo,
                                  n % 4 == 0, n % 4 == 3, "v_mm")
                ins.then_inc(S("ring_free"), 1)
            pe.wait_ge(S("v_done"), 2 * TT)

            def score_item(i):
                lv, chunks, last, _ = items[i]
                B = LEVELS[lv]
                dst = one_bank(6 + i % 2)
                if B:
                    pe.wait_ge(S("qd_done"), lv)
                    if B > 1:
                        pe.wait_ge(S("kd_done"), lv - 1)
                if i >= 2:
                    before = [items[x] for x in range(i - 1)]
                    taken = sum(1 for x in before if not x[2])
                    pe.wait_ge(S("item_taken"), taken)
                    if any(x[2] for x in before):
                        pe.wait_ge(S("mod_done"), 1 + sum(1 for x in before if x[2]))
                kk = kd if B > 1 else k
                col = 0
                ins = None
                for c in chunks:
                    w = 64 if last else P
                    for h in range(HEADS):
                        lhs = kk[:, h, P * c:P * c + w]
                        if B == 0:
                            rhs, n = q[:, h, P * c:P * c + w], w
                        else:
                            at_ = (h * T + P * c) // 2 if B < 8 else (h * SEQ + P * c) // 2
                            rhs, n = qd[:, at_:at_ + w // 2], w // 2
                        ins = pe.matmul(dst[0:w, col:col + n], lhs, rhs, start=True, stop=True)
                        col += n
                if last:
                    pe.wait_ge(S("ada_next_in"), 16 * (lv + 1))
                    for m in range(4):
                        ins = ada(dst[:, 256 + 9 * m:265 + 9 * m], ada_next, P * m)
                ins.then_inc(S("item"), 1)
                return

            for j in range(KT):
                mine = per_level[j]
                for e in range(4):
                    n = TILE_C1 + 4 * j + e
                    pe.wait_ge(S("w_lo_done"), n + 1)
                    if n - TILE_C1 >= 3:
                        m = n - 3
                        jj, ee = (m - TILE_C1) // 4, (m - TILE_C1) % 4
                        name, per = (("cg_done", 1), ("u_done", 3), ("t_done", 3), ("sga_done", 1))[ee]
                        pe.wait_ge(S(name), per * (jj + 1))
                    channel_tile(kc(w_hi[n % 4]), kc(w_lo[n % 4]), c1_pair(n), (h_hi, h_lo))
                    for i in (mine[:1], mine[1:2], mine[2:], [])[e]:
                        score_item(i)
            pe.wait_ge(S("tail_done"), 2 * KT)
            pe.wait_ge(S("mod_done"), 9)
            pe.wait_ge(S("item_taken"), sum(1 for x in items if not x[2]))
            pe.transpose(one_bank(6)[0:16, 0:P], tail_mix[:, 0:2, :].rearrange("p a j -> p (a j)"), ident[:, :])
            pe.transpose(one_bank(6)[:, P:2 * P], tail_mix[:, 2:18, :].rearrange("p a j -> p (a j)"), ident[:, :]) \
              .then_inc(S("tails_tr"), 1)
            pe.wait_ge(S("k_dec"), 1)
            pe.wait_ge(S("cg_done"), KT)
            pe.wait_ge(S("u_done"), 3 * KT)
            pe.wait_ge(S("t_done"), 3 * KT)
            pe.wait_ge(S("sga_done"), KT)
            for h in range(HEADS):
                ins = pe.transpose(one_bank(1)[0:64, DK * h:DK * h + DK], k[:, h, SEQ:T], ident[:, :])
            ins.then_inc(S("ks_tr"), 1)
            for c in range(NCH):
                if c >= 1:
                    pe.wait_ge(S("k_tok_done"), c)
                for h in range(HEADS):
                    ins = pe.transpose(one_bank(0)[:, DK * h:DK * h + DK], k[:, h, P * c:P * c + P], ident[:, :])
                ins.then_inc(S("k_tr"), 1)
                if c == 0:
                    pe.wait_ge(S("smp_scores"), 4)
                    pe.wait_ge(S("q_dec"), 1)
                else:
                    pe.wait_ge(S("o_done"), c)
                    pe.wait_ge(S("state_done"), c)
                for h in range(HEADS):
                    for e in range(2):
                        mt = 2 * h + e
                        dst = bank[2][:, mt // 4, P * (mt % 4):P * (mt % 4) + P]
                        cols = DV * h + P * e
                        ins = pe.matmul(dst, v_tok[:, c, cols:cols + P], score[:, HEADS * c + h, :], start=True, stop=c == 0)
                        if c > 0:
                            ins = pe.matmul(dst, state[(c - 1) % 2][:, h, P * e:P * e + P], q[:, h, P * c:P * c + P],
                                            start=False, stop=True)
                ins.then_inc(S("o_mm"), 1)
                pe.wait_ge(S("k_tok_done"), c + 1)
                if c >= 1:
                    pe.wait_ge(S("state_done"), c)
                for h in range(HEADS):
                    dst = bank[1][:, h // 2, DV * (h % 2):DV * (h % 2) + DV]
                    ins = pe.matmul(dst, k_tok[c % 2][:, DK * h:DK * h + DK], v_tok[:, c, DV * h:DV * h + DV],
                                    start=True, stop=True)
                ins.then_inc(S("delta_mm"), 1)
            pe.wait_ge(S("tails_out"), 2)
            pe.wait_ge(S("o_done"), NCH)
            pe.wait_ge(S("state_done"), NCH)
            for u in range(8):
                h, g = u // 2, u % 2
                if g == 0:
                    for e in range(2):
                        pe.matmul(bank[3][:, e, 64 * h:64 * h + 64], v_tok[0:64, 4, DV * h + P * e:DV * h + P * e + P],
                                  score[0:64, HEADS * NCH + h, 0:64], start=True, stop=True)
                pe.wait_ge(S(f"s_in{u % 3}"), 16 * (u // 3 + 1))
                for e in range(2):
                    for s in range(4):
                        tok = (4 * g + s) * TS
                        pe.matmul(bank[3][:, e, 64 * h + tok:64 * h + tok + TS], s_in[u % 3][:, s, P * e:P * e + P],
                                  q[:, h, SEQ + tok:SEQ + tok + TS], start=False, stop=True,
                                  skip_group_check=True)
                pe.wait_ge(S("k_own"), h + 1)
                if u >= 2:
                    pe.wait_ge(S("s_done"), 4 * (u - 1))
                for s in range(4):
                    dst = bank[1 + u % 2][:, s // 2, DV * (s % 2):DV * (s % 2) + DV]
                    ins = pe.matmul(dst, k_own[:, 4 * g + s, :], v_tok[0:64, 4, DV * h:DV * h + DV], start=True, stop=True)
                ins.then_inc(S("ds_mm"), 1)
            pe.wait_ge(S("s_done"), 32)
            pe.wait_ge(S("o_done"), NCH + 2)
            def branch_b(i):
                later = not isinstance(i, int) or i > 0
                if later:
                    pe.wait_ge(S("o_root"), i)
                for e in range(2):
                    pe.wait_ge(S("o_sq"), i * 2 + (e + 1))
                    for half in range(2):
                        ins = pe.matmul(bank[3][:, half, 0:HALF], ones[:, :], buf_a[:, HALF * half:HALF * half + HALF],
                                        start=e == 0, stop=e == 1)
                    ins.then_inc(S("ssq_mm"), 1)
                for e in range(4):
                    n = TILE_C2 + e
                    pe.wait_ge(S("w_lo_done"), i * 4 + (n + 1))
                    if e == 3:
                        pe.wait_ge(S("silu_r"), i * 2 + 1)
                    elif later:
                        pe.wait_ge(S("silu_r" if e == 2 else "sgb_done"), i * 2)
                    channel_tile(kc(w_hi[n % 4]), kc(w_lo[n % 4]), C2_PAIR[e], (h_hi, h_lo))

            branch_b(0)
            with pe.Fori(1, HEADS) as i:
                branch_b(i)

            def gate_rows(src, g, done, name):
                m = P if g == 0 else 64
                if g == 1:
                    pe.wait_ge(S(done), 1)
                    pe.wait_ge(S("gx_done"), 1 if src is g1n else 2)
                for i in range(KT):
                    lhs = src[:, i, 0:1].to_broadcast([P, P]) if g == 0 else gx[:, i, :]
                    ins = pe.matmul(bank[3][0:m, i // 4, P * (i % 4):P * (i % 4) + P], lhs, ident[:, :],
                                    start=True, stop=True)
                ins.then_inc(S(name), 1)

            pe.wait_ge(S("scales"), 3)
            pe.wait_ge(S("o_root"), HEADS)
            for g in range(2):
                gate_rows(g1n, g, "gate1_done", "gate1_mm")
            pe.wait_ge(S("w_lo_done"), TILE_UP)
            pe.wait_ge(S("m_lo_done"), KT)
            pe.wait_ge(S("sgb_done"), KT)
            pe.wait_ge(S("silu_r"), KT)
            pe.wait_ge(S("gate1_done"), 2)

            def to_channels(t):
                m = ROWS[t]
                pe.wait_ge(S("xn2_done"), t + 1)
                if t > 0:
                    pe.wait_ge(S("h2_mul"), t)
                for i in range(KT):
                    ins = pe.transpose(bank[3][:, i // 4, P * (i % 4):P * (i % 4) + m], xn[0:m, P * i:P * i + P],
                                       ident[0:m, 0:m])
                ins.then_inc(S("h_tr"), 1)

            for t in range(TT):
                m = ROWS[t]
                if t >= 3:
                    pe.wait_ge(S("y_scaled"), t - 2)
                order = list(range(KT)) if t < TT - 1 else list(range(4, 8)) + list(range(4))
                for x, i in enumerate(order):
                    wh, wl = (wo_hi[:, i, :], wo_lo[:, i, :]) if i < 4 else (w_hi[i - 4][:, :], w_lo[i - 4][:, :])
                    xh, xl = m_hi[:, i, P * t:P * t + m], m_lo[:, i, P * t:P * t + m]
                    for c in range(2):
                        for p, (xx, w) in enumerate(((xh, wh), (xh, wl), (xl, wh))):
                            ins = pe.matmul(bank[t % 3][0:m, c, :], xx, w[:, 512 * c:512 * c + 512],
                                            start=x == 0 and p == 0, stop=x == KT - 1 and p == 2)
                    if t == TT - 1 and i >= 4:
                        ins.then_inc(S("ring_free"), 1)
                ins.then_inc(S("wo_mm"), 1)
                if t > 0:
                    to_channels(t - 1)
            to_channels(TT - 1)
            pe.wait_ge(S("h2_lo_done"), TT)
            def ffn_up(i):
                for e in range(4):
                    n = TILE_UP + e
                    pe.wait_ge(S("w_lo_done"), i * 4 + (n + 1))
                    if not isinstance(i, int) or i > 0:
                        if e < 2:
                            pe.wait_ge(S("f_done" if e % 2 else "a_done"), i * 6 - 3)
                        else:
                            pe.wait_ge(S("f_done" if e % 2 else "a_done"), i * 6)
                    channel_tile(kc(w_hi[n % 4]), kc(w_lo[n % 4]), e, (h_hi, h_lo))

            ffn_up(0)
            with pe.Fori(1, FT // 2) as i:
                ffn_up(i)
            pe.wait_ge(S("f_done"), 3 * FT)
            pe.wait_ge(S("a_done"), 3 * FT)
            pe.wait_ge(S("ftail_done"), 2 * FT)
            for i in range(4):
                lo, m = ((P * i, (P, P, 96)[i]) if i < 3 else (0, 44))
                src = (tail_ff[:, 2:18, :] if i < 3 else tail_ff[:, 0:2, :]).rearrange("p a j -> p (a j)")
                ins = pe.transpose(one_bank(5)[0:m, P * i:P * i + P], src[:, lo:lo + m], ident[:, :])
            ins.then_inc(S("ftails_tr"), 1)
            for n in range(FT):
                c, g = n // 11, n % 11
                pe.wait_ge(S("w_lo_done"), TILE_DN + n + 1)
                if c == 0:
                    pe.wait_ge(S("f_lo_done"), 2 * g + 2)
                if n == 0:
                    gate_rows(g2n, 0, "gate2_done", "gate2_mm")
                if n == 1:
                    gate_rows(g2n, 1, "gate2_done", "gate2_mm")
                if n == 11:
                    pe.wait_ge(S("ftails_out"), 4)
                    pe.wait_ge(S("gate2_done"), 2)
                    pe.wait_ge(S("yh_done"), 2)
                token_tiles(TILE_DN + n, g, [(TT * c + t) % 8 for t in range(TT)], f_hi, f_lo, g == 0, g == 10, "dn_mm") \
                    .then_inc(S("ring_free"), 1)


_INS = ["x_prompt", "x_sample", "c_prompt", "c_sample", "state_conv_mix", "state_gla", "state_conv_ffn",
        "w_ada", "b_ada", "norm_pre1", "norm_post1", "norm_pre2", "norm_post2", "w_in", "conv_w", "conv_b",
        "w_a2", "b_a", "gla_norm", "w_out", "w_up", "ffn_conv_w", "ffn_conv_b", "w_down"]
_OUTS = [("y_prompt", (1, SEQ, D)), ("y_sample", (NS, TS, D)),
         ("new_conv_mix_prompt", (1, 1, 2, D)), ("new_gla_prompt", (1, 1, HEADS, DK, DV)),
         ("new_conv_ffn_prompt", (1, 1, 2, FF)),
         ("new_conv_mix_sample", (1, NS, 2, D)), ("new_gla_sample", (1, NS, HEADS, DK, DV)),
         ("new_conv_ffn_sample", (1, NS, 2, FF))]


def kernel(**inputs):
    import concourse.bacc as _bacc
    from concourse.bass_utils import run_bass_kernel_spmd as _run

    nc = _bacc.Bacc("TRN2", target_bir_lowering=False, num_devices=1, dynamic_dma_scratch_size=1024)
    arrays, aps = {}, {}
    for name in _INS:
        arr = np.ascontiguousarray(inputs[name])
        arrays[f"in_{name}"] = arr
        aps[name] = nc.dram_tensor(f"in_{name}", arr.shape, mybir.dt.from_np(arr.dtype), kind="ExternalInput").ap()
    for name, shape in _OUTS:
        aps[name] = nc.dram_tensor(f"out_{name}", shape, F32, kind="ExternalOutput").ap()
    layer_program(nc, aps)
    r = _run(nc, [arrays], core_ids=[0])
    return tuple(r.results[0][f"out_{name}"] for name, _ in _OUTS)
```

```python
import numpy as np
import concourse.bass as bass
from concourse import mybir

F32 = mybir.dt.float32
F32R = mybir.dt.float32r
I32 = mybir.dt.int32
ALU = mybir.AluOpType
ACT = mybir.ActivationFunctionType

P = 128
D = 1024
KT = D // P
SEQ = 512
NS, TS = 8, 8
T = SEQ + NS * TS
HALF = T // 2
TT = 5
ROWS = [P, P, P, P, NS * TS]
HEADS, DK, DV = 4, 128, 256
RANK = 16
FF = 2816
FT = FF // P
EPS = 1e-6
TAU_INV = 1.0 / 16.0
NCH = SEQ // P
EXT = 2 + SEQ + NS * (2 + TS)
S0E = 2 + SEQ
CONV = EXT - 2

IN_BG, IN_CG, IN_UA = 0, D, 2 * D
IN_Q, IN_K, IN_V = 3 * D, 3 * D + HEADS * DK, 3 * D + 2 * HEADS * DK
IN_R = IN_V + HEADS * DV
IN_LR = IN_R + HEADS * DV
IN_GA = IN_LR + RANK
IN_GB = IN_GA + D

TILE_K, TILE_Q, TILE_V = 0, HEADS, 2 * HEADS
TILE_C1 = TILE_V + 8
TILE_C2 = TILE_C1 + 8 * KT
TILE_WO = TILE_C2 + 2 * KT
TILE_UP = TILE_WO + KT
TILE_DN = TILE_UP + 2 * FT
TILES = TILE_DN + FT
LEVELS = [0, 1, 2, 4, 8, 16, 32, 64]


def freed(n):
    return n + 1 if n < TILE_WO else n - 3


def layer_program(nc, a):
    base = 1152
    at = base

    def place(name, shape, dtype=F32, offset=None):
        nonlocal at
        size = int(np.prod(shape[1:])) * 4
        if offset is None:
            offset = at
            at += -(-size // 32) * 32
        return nc.alloc_sbuf_tensor_at(name, shape, dtype, offset=offset)

    raw = [place(f"raw{i}", [P, 1024]) for i in range(2)]
    w_hi = [place(f"w_hi{i}", [P, 1024], F32R) for i in range(4)]
    w_lo = [place(f"w_lo{i}", [P, 1024], F32R) for i in range(4)]
    x_at = at
    x_tok = place("x_tok", [P, TT, D])
    v_tok = place("v_tok", [P, TT, D], offset=x_at)
    h_at = at
    h_hi = place("h_hi", [P, KT, T], F32R)
    h_lo = place("h_lo", [P, KT, T], F32R)
    g_at = at
    at += 106496
    ada_first = place("ada_first", [P, KT, 2 * D], offset=g_at)
    q = place("q", [P, HEADS, T], offset=g_at)
    k = place("k", [P, HEADS, T], offset=g_at + 9216)
    pre = place("pre", [P, HEADS, T], offset=g_at + 18432)
    suf = place("suf", [P, HEADS, T], offset=g_at + 27648)
    kd = place("kd", [P, HEADS, T], offset=g_at + 36864)
    qd = place("qd", [P, HEADS * T // 2], offset=g_at + 46080)
    score = place("score", [P, TT * HEADS, P], offset=g_at + 50688)
    state = [place(f"state{i}", [P, HEADS, DV], offset=g_at + 60928 + 4096 * i) for i in range(2)]
    y_a = place("y_a", [P, KT, T], offset=g_at + 69632)
    h32 = place("h32", [P, KT, T], offset=g_at + 69632)
    o = place("o", [P, KT, T], offset=g_at + 88064)
    rows_ada = place("rows_ada", [18, 512], offset=g_at + 88064)
    rows_ada0 = place("rows_ada0", [18, 4, 512], offset=g_at + 96256)
    ada_hi = [place(f"ada_hi{i}", [P, 2 * D], F32R, offset=h_at + 8192 * i) for i in range(2)]
    ada_lo = [place(f"ada_lo{i}", [P, 2 * D], F32R, offset=h_at + 16384 + 8192 * i) for i in range(2)]
    k_tok = [place(f"k_tok{i}", [P, HEADS * DK], offset=g_at + 27648 + 2048 * i) for i in range(2)]
    k_own = place("k_own", [NS * TS, NS, DK], offset=g_at + 31744)
    s_in = [place(f"s_in{i}", [P, 4, DV], offset=g_at + 36864 + 4096 * i) for i in range(3)]
    m_hi = place("m_hi", [P, KT, T], F32R, offset=g_at)
    m_lo = place("m_lo", [P, KT, T], F32R, offset=g_at + 18432)
    wo_hi = place("wo_hi", [P, 4, D], F32R, offset=g_at + 36864)
    wo_lo = place("wo_lo", [P, 4, D], F32R, offset=g_at + 53248)
    gate1 = place("gate1", [P, 2, D], offset=g_at + 69632)
    xn = place("xn", [P, D], offset=g_at + 77824)
    y_tmp = place("y_tmp", [P, D], offset=g_at + 81920)
    h2_32 = place("h2_32", [P, KT, P], offset=g_at + 86016)
    sq_tok = place("sq_tok", [P, D], offset=g_at + 90112)
    f_hi = place("f_hi", [P, FT, T], F32R, offset=g_at)
    f_lo = place("f_lo", [P, FT, T], F32R, offset=g_at + FT * T * 4)
    gate2 = place("gate2", [P, 2, D], offset=h_at)
    y_half = place("y_half", [P, TT, 512], offset=h_at + 8192)
    sq_half = place("sq_half", [P, 512], offset=h_at + 18432)
    t_at = at
    ext = place("ext", [P, EXT])
    cv = place("cv", [P, CONV])
    buf_a = place("buf_a", [P, T])
    buf_b = place("buf_b", [P, T])
    rows = place("rows", [P, P], offset=t_at)
    rows_ffn = place("rows_ffn", [P, P], offset=t_at + 512)
    rows_c = place("rows_c", [P, P], offset=t_at + 1024)
    rows_mix = place("rows_mix", [P, P], offset=t_at + 1536)
    rows_ff0 = place("rows_ff0", [P, 3, P], offset=t_at + 2048)
    w_lr = place("w_lr", [P, KT, RANK], offset=t_at + 3584)
    w_a2 = place("w_a2", [RANK, HEADS * DK], offset=t_at + 4096)
    lr = place("lr", [RANK, T], offset=t_at + 6144)
    sq0 = place("sq0", [P, D], offset=g_at + 90112)
    tails_out = place("tails_out", [P, 2, P], offset=t_at + 0)
    ftails_out = place("ftails_out", [P, 4, P], offset=h_at + 20480)
    buf_fin = place("buf_fin", [P, 512], offset=t_at)
    prm = place("prm", [P, 124])
    ffp = place("ffp", [P, 88])
    c_t = place("c_t", [P, 72], offset=t_at + 8736)
    c_sig = place("c_sig", [P, 72], offset=t_at + 8448)
    c_hl = place("c_hl", [P, KT, 18], F32R)
    fold = place("fold", [18, 9])
    mix0 = place("mix0", [P, 16, KT])
    ff0 = place("ff0", [P, 16, FT])
    mod = place("mod", [P, 48, 9])
    ident = place("ident", [P, P])
    ones = place("ones", [P, P])
    mask = place("mask", [P, 7, 64])
    own = place("own", [NS * TS, NS])
    mul1 = place("mul1", [P, KT, 9])
    mul2 = place("mul2", [P, KT, 9])
    g1n = place("g1n", [P, KT, 9])
    g2n = place("g2n", [P, KT, 9])
    gx = place("gx", [P, KT, NS * TS])
    eps = place("eps", [P, 1])
    one = place("one", [P, 1])
    st_x = place("st_x", [P, 3, TT])
    st_y = place("st_y", [P, 3, TT])
    st_h = place("st_h", [P, 3, TT])
    st_f = place("st_f", [P, 4, TT])
    tail_mix = place("tail_mix", [P, 18, KT])
    tail_ff = place("tail_ff", [P, 18, FT])
    assert at <= 229368, at
    bank = [nc.alloc_psum_tensor(f"pair{i}", [P, 2, 512], F32) for i in range(4)]

    def one_bank(b):
        return bank[b // 2][:, b % 2, :]

    B_ADA, PRE1, POST1, PRE2, POST2, CW, CB, B_A, GN = 0, 48, 56, 64, 72, 80, 104, 112, 116
    FW, FB = 0, 66

    sems = {}

    def S(name):
        if name not in sems:
            sems[name] = nc.alloc_semaphore(name)
        return sems[name]

    w_in, w_up, w_down, w_out, w_ada = (a[n][0] for n in ("w_in", "w_up", "w_down", "w_out", "w_ada"))

    def in_cols(c0):
        return w_in[:, c0:c0 + P].rearrange("(k p) c -> p k c", p=P)

    def spread(v, n):
        if len(v.shape) == 2:
            return v.rearrange("p (m o) -> p m o", o=1).to_broadcast([v.shape[0], v.shape[1], n])
        return v.rearrange("p k (m o) -> p k m o", o=1).to_broadcast([v.shape[0], v.shape[1], v.shape[2], n])

    def row(buf, j):
        if isinstance(j, int):
            return buf[:, j, :]
        return buf[:, bass.ds(j, 1), :].rearrange("p o n -> p (o n)")

    def kc(tile):
        return tile[:, :].rearrange("p (k c) -> p k c", c=P)

    def k2(tile):
        return tile[:, :].rearrange("p (k c) -> p k c", c=512)

    def halves(buf):
        return buf.rearrange("p (a t) -> p a t", a=2)

    def out2(pair):
        return bank[pair][:, :, 0:HALF]

    def conv_pieces(pair, buf, first, s_step, s_skip):
        s_at = first + SEQ
        smp = buf[:, s_at:s_at + NS * s_step].rearrange("p (s w) -> p s w", w=s_step)[:, :, s_skip:s_skip + TS]
        return [
            (bank[pair][:, 0, 0:HALF], buf[:, first:first + HALF], 0, HALF),
            (bank[pair][:, 1, 0:SEQ - HALF], buf[:, first + HALF:first + SEQ], HALF, SEQ),
            (bank[pair][:, 1, SEQ - HALF:HALF].rearrange("p (s w) -> p s w", w=TS), smp, SEQ, T),
        ]

    def piece(buf, lo, hi):
        v = buf[:, lo:hi]
        return v.rearrange("p (s w) -> p s w", w=TS) if lo == SEQ else v

    def c1_pair(j, i):
        return (4 * j + i) % 3

    C2_PAIR = [0, 1, 2, 0]

    items = []
    for lv, B in enumerate(LEVELS):
        items += [(lv, g) for g in ([[0], [1], [2], [3]] if B == 0 else [[0, 1], [2, 3]])]
        items += [(lv, [4])] if B < 8 else []

    def after_tile(j, e):
        level = [i for i, it in enumerate(items) if it[0] == j]
        slots = (0, 2, 4, 6, 7) if j == 0 else (0, 2, 4)
        return [i for i, slot in zip(level, slots) if slot == e]

    def items_to(lv):
        return sum(1 for it in items if it[0] <= lv)

    def block_view(buf, B, ch_tokens, side):
        return buf.rearrange("p (n s b) -> p n s b", s=2, b=B)[:, :, side, :]

    def store_state(sp, u):
        h, g = u // 2, u % 2
        sp.wait_ge(S("s_done"), 4 * (u + 1))
        sp.dma_start(a["new_gla_sample"][0, 4 * g:4 * g + 4, h].rearrange("s d v -> d s v"), s_in[u % 3][:, :, :]) \
          .then_inc(S(f"s_stored{u % 3}"), 16)

    def qd_exp(act, lv):
        B = LEVELS[lv]
        act.wait_ge(S("level_set"), lv)
        if lv > 1:
            act.wait_ge(S("item"), items_to(lv - 1))
        if B < 8:
            src = block_view(pre[:, :, :].rearrange("p h t -> p (h t)"), B, T, 1)
            dst = qd[:, :].rearrange("p (n b) -> p n b", b=B)
        else:
            src = pre[:, :, 0:SEQ].rearrange("p h (n s b) -> p h n s b", s=2, b=B)[:, :, :, 1, :]
            dst = qd[:, 0:HEADS * SEQ // 2].rearrange("p (h n b) -> p h n b", h=HEADS, b=B)
        act.activation(dst, src, ACT.Exp, scale=TAU_INV).then_inc(S("qd_exp"), 1)

    def kd_exp(act, lv):
        w = T if LEVELS[lv] < 8 else SEQ
        act.activation(kd[:, :, 0:w], suf[:, :, 0:w], ACT.Exp, scale=TAU_INV).then_inc(S("kd_exp"), 1)

    def act_out(act):
        for t in range(TT):
            m = ROWS[t]
            act.wait_ge(S("wo_mm"), t + 1)
            act.activation(sq_tok[0:m, :], bank[t % 3][0:m, :, :].rearrange("p a c -> p (a c)"), ACT.Square,
                           accum_out=st_y[0:m, 0, t:t + 1]).then_inc(S("y_sq"), 1)
            act.wait_ge(S("y_sq"), t + 1)
            act.activation(st_y[0:m, 1, t:t + 1], st_y[0:m, 0, t:t + 1], ACT.Sqrt, bias=eps[0:m, :], scale=1.0 / D) \
               .then_inc(S("y_root"), 1)
            act.wait_ge(S("x1_done"), t + 1)
            act.activation(sq_tok[0:m, :], x_tok[0:m, t, :], ACT.Square, accum_out=st_h[0:m, 0, t:t + 1]) \
               .then_inc(S("x1_sq"), 1)
            act.wait_ge(S("x1_sq"), t + 1)
            act.activation(st_h[0:m, 1, t:t + 1], st_h[0:m, 0, t:t + 1], ACT.Sqrt, bias=eps[0:m, :], scale=1.0 / D) \
               .then_inc(S("x1_root"), 1)
            act.wait_ge(S("h2_done"), t + 1)
            act.activation(h_hi[:, :, P * t:P * t + m], h2_32[:, :, 0:m], ACT.Copy).then_inc(S("h2_hi_done"), 1)

    def conv(dve, src, dst, w, b, name, count):
        dve.tensor_scalar(dst[:, :], src[:, 2:EXT], w[2], b, ALU.mult, ALU.add).then_inc(S(name), 1)
        for i, tap in enumerate((1, 0)):
            dve.wait_ge(S(name), count + (i + 1))
            dve.scalar_tensor_tensor(dst[:, :], src[:, tap:tap + CONV], w[tap], dst[:, :], ALU.mult, ALU.add) \
               .then_inc(S(name), 1)

    def tails(dve, dst, name):
        dve.tensor_copy(dst[:, 0:2], ext[:, SEQ:SEQ + 2]).then_inc(S(name), 1)
        last = ext[:, S0E:EXT].rearrange("p (s w) -> p s w", w=TS + 2)[:, :, TS:TS + 2]
        dve.tensor_copy(dst[:, 2:18].rearrange("p (s w) -> p s w", w=2), last).then_inc(S(name), 1)

    def dve_level(dve, lv):
        B = LEVELS[lv]
        if B:
            dve.wait_ge(S("level_set"), lv)
            dve.wait_ge(S("qd_exp"), lv)
            if B < 8:
                src = block_view(q[:, :, :].rearrange("p h t -> p (h t)"), B, T, 1)
                dst = qd[:, :].rearrange("p (n b) -> p n b", b=B)
            else:
                src = q[:, :, 0:SEQ].rearrange("p h (n s b) -> p h n s b", s=2, b=B)[:, :, :, 1, :]
                dst = qd[:, 0:HEADS * SEQ // 2].rearrange("p (h n b) -> p h n b", h=HEADS, b=B)
            dve.tensor_tensor(dst, dst, src, ALU.mult).then_inc(S("qd_done"), 1)
            if B > 1:
                w = T if B < 8 else SEQ
                dve.wait_ge(S("kd_exp"), lv - 1)
                dve.tensor_tensor(kd[:, :, 0:w], kd[:, :, 0:w], k[:, :, 0:w], ALU.mult).then_inc(S("kd_done"), 1)
            w = T if B < 8 else SEQ

            def side(buf, s, last=False):
                if B < 8:
                    v = buf[:, :, :].rearrange("p h t -> p (h t)").rearrange("p (n s b) -> p n s b", s=2, b=B)
                    v = v[:, :, s, B - 1:B] if last else v[:, :, s, :]
                    return v.to_broadcast([P, HEADS * T // (2 * B), B]) if last else v
                v = buf[:, :, 0:SEQ].rearrange("p h (n s b) -> p h n s b", s=2, b=B)
                v = v[:, :, :, s, B - 1:B] if last else v[:, :, :, s, :]
                return v.to_broadcast([P, HEADS, SEQ // (2 * B), B]) if last else v

            dve.tensor_tensor(side(suf, 0), side(suf, 0), side(pre, 1, True), ALU.add).then_inc(S("suf_add"), 1)
            dve.wait_ge(S("suf_add"), lv)
            dve.tensor_tensor(side(pre, 1), side(pre, 1), side(pre, 0, True), ALU.add).then_inc(S("level_set"), 1)

    def take_item(dve, i):
        lv, chunks = items[i]
        B = LEVELS[lv]
        src = one_bank(7)
        ch, nch = chunks[0] * HEADS, len(chunks) * HEADS
        m = ROWS[chunks[0]]
        dve.wait_ge(S("item"), i + 1)
        if B == 0:
            dst = score[0:m, ch:ch + nch, 0:m]
            msk = ident[0:m, 0:m].bitcast(I32).rearrange("p (o t) -> p o t", o=1).to_broadcast([m, nch, m])
            data = src[0:m, 0:nch * m].rearrange("p (c t) -> p c t", t=m)
        else:
            dst = score[0:m, ch:ch + nch, 0:m].rearrange("p c (n s b) -> p c n s b", s=2, b=B)[:, :, :, 1, :]
            msk = mask[0:m, lv - 1, 0:m // 2].bitcast(I32).rearrange("p (o n b) -> p o n b", o=1, b=B) \
                .to_broadcast([m, nch, m // 2 // B, B])
            data = src[0:m, 0:nch * m // 2].rearrange("p (c n b) -> p c n b", c=nch, b=B)
        dve.copy_predicated(dst, msk, data).then_inc(S("item_taken"), 1)

    def take_mod(dve, j):
        dve.wait_ge(S("back"), j + 1)
        dve.tensor_tensor(mod[:, 16 + 4 * j:20 + 4 * j, :], one_bank(7)[:, 0:36].rearrange("p (m s) -> p m s", s=9),
                          spread(prm[:, 16 + 4 * j:20 + 4 * j], 9), ALU.add).then_inc(S("mod_done"), 1)

    def dve_out(dve, t):
        m, g = ROWS[t], t // 4
        dve.wait_ge(S("y_root"), t + 1)
        dve.reciprocal(st_y[0:m, 2, t:t + 1], st_y[0:m, 1, t:t + 1]).then_inc(S("y_rstd"), 1)
        dve.wait_ge(S("y_rstd"), t + 1)
        if t > 0:
            dve.wait_ge(S("x1_done"), t)
        dve.scalar_tensor_tensor(y_tmp[0:m, :], bank[t % 3][0:m, :, :].rearrange("p a c -> p (a c)"),
                                 st_y[0:m, 2, t:t + 1], gate1[0:m, g, :], ALU.mult, ALU.mult).then_inc(S("y_scaled"), 1)
        dve.wait_ge(S("y_scaled"), t + 1)
        dve.tensor_tensor(x_tok[0:m, t, :], x_tok[0:m, t, :], y_tmp[0:m, :], ALU.add).then_inc(S("x1_done"), 1)
        dve.wait_ge(S("x1_root"), t + 1)
        dve.reciprocal(st_h[0:m, 2, t:t + 1], st_h[0:m, 1, t:t + 1]).then_inc(S("x1_rstd"), 1)
        dve.wait_ge(S("x1_rstd"), t + 1)
        if t > 0:
            dve.wait_ge(S("h_tr"), t)
        dve.tensor_scalar(xn[0:m, :], x_tok[0:m, t, :], st_h[0:m, 2, t:t + 1], None, ALU.mult).then_inc(S("xn2_done"), 1)
        dve.wait_ge(S("h_tr"), t + 1)
        if t > 0:
            dve.wait_ge(S("h2_hi_done"), t)
            dve.wait_ge(S("h2_lo_done"), t)
        src = bank[3][:, :, :].rearrange("p a (k t) -> p (a k) t", t=P)[:, :, 0:m]
        dst = h2_32[:, :, 0:m]
        if g == 0:
            mul, add = (v.to_broadcast([P, KT, P]) for v in (mul2[:, :, 0:1], mod[:, 24:32, 0:1]))
        else:
            src = src.rearrange("p k (s t) -> p k s t", t=TS)
            dst = dst.rearrange("p k (s t) -> p k s t", t=TS)
            mul, add = (spread(v, TS) for v in (mul2[:, :, 1:9], mod[:, 24:32, 1:9]))
        dve.tensor_tensor(dst, src, mul, ALU.mult).then_inc(S("h2_mul"), 1)
        dve.wait_ge(S("h2_mul"), t + 1)
        dve.tensor_tensor(dst, dst, add, ALU.add).then_inc(S("h2_done"), 1)
        dve.wait_ge(S("h2_hi_done"), t + 1)
        dve.tensor_tensor(h_lo[:, :, P * t:P * t + m], h2_32[:, :, 0:m], h_hi[:, :, P * t:P * t + m].bitcast(F32),
                          ALU.subtract).then_inc(S("h2_lo_done"), 1)

    with nc.Block() as block:

        @block.sync
        def _(sp):
            def load_raw(n, src, view=None):
                if n >= 2:
                    sp.wait_ge(S("w_lo_done"), n - 1)
                dst = raw[n % 2][:, :]
                if len(src.shape) == 3:
                    dst = dst.rearrange("p (k c) -> p k c", k=src.shape[1])
                sp.dma_start(dst, src).then_inc(S(f"raw_in{n % 2}"), 16)

            for t in range(NCH):
                sp.dma_start(x_tok[:, t, :], a["x_prompt"][0, P * t:P * t + P, :]).then_inc(S(f"x_in{t}"), 16)
            sp.dma_start(x_tok[0:64, 4, :], a["x_sample"].rearrange("b t d -> (b t) d")).then_inc(S(f"x_in{NCH}"), 16)
            small = []
            r = 0
            for name in ("b_ada", "norm_pre1", "norm_post1", "norm_pre2", "norm_post2"):
                n = a[name].shape[1] // P
                small.append((rows[r:r + n, :], a[name].rearrange("o (j p) -> (o j) p", p=P)))
                r += n
            small.append((rows[r:r + 24, :], a["conv_w"][0].rearrange("w (j p) -> (w j) p", p=P)))
            small.append((rows[r + 24:r + 32, :], a["conv_b"].rearrange("o (j p) -> (o j) p", p=P)))
            small.append((rows[r + 32:r + 36, :], a["b_a"].rearrange("o (j p) -> (o j) p", p=P)))
            small.append((rows[r + 36:r + 44, :], a["gla_norm"][0].rearrange("h (j p) -> (h j) p", p=P)))
            small.append((rows_ffn[0:66, :], a["ffn_conv_w"][0].rearrange("w (j p) -> (w j) p", p=P)))
            small.append((rows_ffn[66:88, :], a["ffn_conv_b"].rearrange("o (j p) -> (o j) p", p=P)))
            small.append((rows_mix[:, :], a["state_conv_mix"][0].rearrange("s w (j p) -> (s w j) p", p=P)))
            ffr = a["state_conv_ffn"][0].rearrange("s w (j p) -> (s w j) p", p=P)
            for i in range(3):
                n = min(P, 352 - P * i)
                small.append((rows_ff0[0:n, i, :], ffr[P * i:P * i + n, :]))
            for i in range(KT):
                sp.dma_start(ada_first[:, i, :], w_ada[P * i:P * i + P, 0:2 * D]).then_inc(S(f"ada_in{i}"), 16)
                for dst, src in small[3 * i:3 * i + 3]:
                    sp.dma_start(dst, src).then_inc(S("rows_in"), 16)
            sp.dma_start(w_lr[:, :, :], w_in[:, IN_LR:IN_LR + RANK].rearrange("(k p) c -> p k c", p=P)) \
              .then_inc(S("lr_in"), 16)
            sp.dma_start(w_a2[:, :], a["w_a2"][0]).then_inc(S("lr_in"), 16)
            for h in range(HEADS):
                load_raw(TILE_K + h, in_cols(IN_K + h * DK))
            for h in range(HEADS):
                load_raw(TILE_Q + h, in_cols(IN_Q + h * DK))
            v_w = w_in[:, IN_V:IN_V + D].rearrange("(g k p) c -> g p k c", p=P, k=2)
            for n in range(8):
                load_raw(TILE_V + n, v_w[n % 4, :, :, 512 * (n // 4):512 * (n // 4) + 512])
            def load_c2(n):
                load_raw(TILE_C2 + n, in_cols((IN_R, IN_GB)[n % 2] + P * (n // 2)))

            ada_v = w_ada.rearrange("(g k p) c -> g p k c", p=P, k=2)
            for j in range(KT):
                for i, c0 in enumerate((IN_CG, IN_UA, IN_BG, IN_GA)):
                    load_raw(TILE_C1 + 8 * j + 2 * i, in_cols(c0 + P * j))
                    load_raw(TILE_C1 + 8 * j + 2 * i + 1, ada_v[i, :, :, 2 * D + 512 * j:2 * D + 512 * j + 512])
            for n in range(3):
                load_c2(n)
            for u in range(8):
                h, g = u // 2, u % 2
                if u == 0:
                    sp.wait_ge(S("item"), len(items))
                if u >= 3:
                    sp.wait_ge(S(f"s_stored{u % 3}"), 16 * (u // 3))
                sp.dma_start(s_in[u % 3][:, :, :], a["state_gla"][0, 4 * g:4 * g + 4, h].rearrange("s d v -> d s v")) \
                  .then_inc(S(f"s_in{u % 3}"), 16)
                if u >= 1:
                    store_state(sp, u - 1)
            store_state(sp, 7)
            sp.wait_ge(S("state_done"), NCH)
            sp.dma_start(a["new_gla_prompt"][0, 0].rearrange("h d v -> d h v"), state[(NCH - 1) % 2][:, :, :]) \
              .then_inc(S("state_stored"), 16)
            sp.wait_ge(S("tails_out"), 2)
            tm = a["new_conv_mix_prompt"][0, 0].rearrange("w (j p) -> (w j) p", p=P)
            sp.dma_start(tm, tails_out[0:16, 0, :]).then_inc(S("tails_stored"), 16)
            ts = a["new_conv_mix_sample"][0].rearrange("s w (j p) -> (s w j) p", p=P)
            sp.dma_start(ts, tails_out[:, 1, :]).then_inc(S("tails_stored"), 16)
            for n in range(3, 2 * KT):
                load_c2(n)
                if n == 3:
                    sp.wait_ge(S("ds_mm"), 8)
                    sp.dma_start(x_tok[:, 0:4, :], a["x_prompt"][0].rearrange("(t p) d -> p t d", p=P)) \
                      .then_inc(S("x_back"), 16)
                    sp.dma_start(x_tok[0:64, 4, :], a["x_sample"].rearrange("b t d -> (b t) d")).then_inc(S("x_back"), 16)
            for n in range(KT):
                load_raw(TILE_WO + n, w_out[P * n:P * n + P, :])
            with sp.Fori(0, FT) as j:
                for i in range(2):
                    sp.wait_ge(S("w_lo_done"), j * 2 + (TILE_UP + i - 1))
                    src = w_up[:, bass.ds(j * P + i * FF, P)].rearrange("(k p) c -> p k c", p=P)
                    sp.dma_start(kc(raw[i]), src).then_inc(S(f"raw_in{i}"), 16)
            dn = w_down.rearrange("(g k p) c -> g p k c", p=P, k=2)
            for n in range(FT):
                load_raw(TILE_DN + n, dn[n % 11, :, :, 512 * (n // 11):512 * (n // 11) + 512])
            sp.wait_ge(S("ftails_out"), 4)
            fp = a["new_conv_ffn_prompt"][0, 0].rearrange("w (j p) -> (w j) p", p=P)
            sp.dma_start(fp, ftails_out[0:44, 3, :]).then_inc(S("out_stored"), 16)
            fs = a["new_conv_ffn_sample"][0].rearrange("s w (j p) -> (s w j) p", p=P)
            for i in range(3):
                n = min(P, 352 - P * i)
                sp.dma_start(fs[P * i:P * i + n, :], ftails_out[0:n, i, :]).then_inc(S("out_stored"), 16)
            for t in range(TT):
                sp.wait_ge(S("y_out"), t + 1)
                if t < 4:
                    dst = a["y_prompt"][0, P * t:P * t + P, :]
                else:
                    dst = a["y_sample"].rearrange("b t d -> (b t) d")
                sp.dma_start(dst, x_tok[0:ROWS[t], t, :]).then_inc(S("out_stored"), 16)
            sp.wait_ge(S("out_stored"), 16 * (4 + TT))
            sp.wait_ge(S("state_stored"), 16)
            sp.wait_ge(S("tails_stored"), 32)
            for u in range(3):
                sp.wait_ge(S(f"s_stored{u}"), 16 * ((7 - u) // 3 + 1))

        @block.gpsimd
        def _(pool):
            pool.memset(ident[:, :], 0.0).then_inc(S("p_set"), 1)
            pool.memset(mask[:, :, :], 1.0).then_inc(S("p_set"), 1)
            pool.memset(own[:, :], 1.0).then_inc(S("p_set"), 1)
            pool.memset(ones[:, :], 1.0).then_inc(S("p_set"), 1)
            pool.memset(eps[:, :], EPS).then_inc(S("p_set"), 1)
            pool.memset(one[:, :], 1.0).then_inc(S("p_set"), 1)
            pool.wait_ge(S("p_set"), 6)
            pool.affine_select(out=ident[:, :], in_=ident[:, :], compare_op=ALU.not_equal, fill=1.0, base=0,
                               pattern=[[-1, P]], channel_multiplier=1).then_inc(S("consts"), 1)
            for i, B in enumerate(LEVELS[1:]):
                m = mask[:, i, :].rearrange("p (n b) -> p n b", b=B)
                pool.affine_select(out=m, in_=m, compare_op=ALU.is_ge, fill=0.0, base=0,
                                   pattern=[[-2 * B, 64 // B], [0, B]], channel_multiplier=1).then_inc(S("p_sel"), 1)
                pool.wait_ge(S("p_sel"), i + 1)
                pool.affine_select(out=m, in_=m, compare_op=ALU.is_ge, fill=0.0, base=B - 1,
                                   pattern=[[2 * B, 64 // B], [0, B]], channel_multiplier=-1).then_inc(S("consts"), 1)
            pool.affine_select(out=own[:, :], in_=own[:, :], compare_op=ALU.is_ge, fill=0.0, base=0,
                               pattern=[[-TS, NS]], channel_multiplier=1).then_inc(S("p_sel"), 1)
            pool.wait_ge(S("p_sel"), 8)
            pool.affine_select(out=own[:, :], in_=own[:, :], compare_op=ALU.is_ge, fill=0.0, base=TS - 1,
                               pattern=[[TS, NS]], channel_multiplier=-1).then_inc(S("consts"), 1)

            def low(r, hi, lo, done):
                pool.wait_ge(S("w_hi_done"), done)
                pool.tensor_tensor(lo, raw[r % 2][:, :], hi.bitcast(F32), ALU.subtract).then_inc(S("w_lo_done"), 1)

            with pool.Fori(0, TILE_WO // 4) as g:
                for r in range(4):
                    low(r, w_hi[r][:, :], w_lo[r][:, :], g * 4 + (r + 1))
            for r in range(4):
                low(r, wo_hi[:, r, :], wo_lo[:, r, :], TILE_WO + r + 1)
            with pool.Fori(TILE_WO // 4 + 1, TILES // 4) as g:
                for r in range(4):
                    low(r, w_hi[r][:, :], w_lo[r][:, :], g * 4 + (r + 1))
            for n in range(TILES // 4 * 4, TILES):
                low(n, w_hi[n % 4][:, :], w_lo[n % 4][:, :], n + 1)

        @block.scalar
        def _(act):
            def high(n, turn=0):
                if isinstance(turn, int):
                    n, turn = n + 4 * turn, 0
                if n >= TILES:
                    return
                act.wait_ge(S(f"raw_in{n % 2}"), turn * 32 + 16 * (n // 2 + 1))
                if TILE_WO <= n < TILE_WO + 4:
                    if n == TILE_WO:
                        for u in range(3):
                            act.wait_ge(S(f"s_stored{u}"), 16 * ((7 - u) // 3 + 1))
                        act.wait_ge(S("state_stored"), 16)
                    dst = wo_hi[:, n - TILE_WO, :]
                else:
                    if n >= 4:
                        act.wait_ge(S("ring_free"), turn * 4 + (freed(n) - 4))
                    dst = w_hi[n % 4][:, :]
                act.activation(dst, raw[n % 2][:, :], ACT.Copy).then_inc(S("w_hi_done"), 1)

            act.dma_start(rows_c[0:8, :], a["c_prompt"].rearrange("b (j p) -> (b j) p", p=P)).then_inc(S("c_in"), 16)
            act.dma_start(rows_c[8:72, :], a["c_sample"].rearrange("b (j p) -> (b j) p", p=P)).then_inc(S("c_in"), 16)
            act.wait_ge(S("c_tr"), 1)
            act.activation(c_sig[:, :], one_bank(2)[:, 0:72], ACT.Sigmoid).then_inc(S("c_sig"), 1)
            act.wait_ge(S("p_set"), 6)
            for t in range(TT):
                n = ROWS[t]
                act.wait_ge(S(f"x_in{t}"), 16)
                if t > 0:
                    act.wait_ge(S("x_sq"), t)
                act.activation(sq0[0:n, :], x_tok[0:n, t, :], ACT.Square, accum_out=st_x[0:n, 0, t:t + 1]) \
                   .then_inc(S("x_sq"), 1)
            for t in range(TT):
                n = ROWS[t]
                act.wait_ge(S("x_sq"), t + 1)
                act.activation(st_x[0:n, 1, t:t + 1], st_x[0:n, 0, t:t + 1], ACT.Sqrt, bias=eps[0:n, :],
                               scale=1.0 / D).then_inc(S("x_root"), 1)
            for i in range(KT):
                act.wait_ge(S(f"ada_in{i}"), 16)
                if i >= 2:
                    act.wait_ge(S("ada0_mm"), i - 1)
                act.activation(ada_hi[i % 2][:, :], ada_first[:, i, :], ACT.Copy).then_inc(S("ada_hi_done"), 1)
                t = i - 2
                if 0 <= t < TT:
                    n = ROWS[t]
                    act.wait_ge(S("x_tr"), t + 1)
                    src = bank[2 + t % 2][:, :, :].rearrange("p a (k t) -> p (a k) t", t=P)[:, :, 0:n]
                    act.activation(h32[:, :, P * t:P * t + n], src, ACT.Copy).then_inc(S("x_ch"), 1)
            act.wait_ge(S("ada0_mm"), KT)
            for g in range(2):
                act.activation(rows_ada0[:, g, :], one_bank(g)[0:18, :], ACT.Copy).then_inc(S("rows0_done"), 1)
            for n in range(3):
                high(n)
            for i in range(KT):
                act.wait_ge(S("h32_done"), i + 1)
                act.activation(h_hi[:, i, :], h32[:, i, :], ACT.Copy).then_inc(S("h_hi_done"), 1)
            act.wait_ge(S("lr_mm"), 1)
            act.activation(halves(lr[:, :]), bank[3][0:RANK, :, 0:HALF], ACT.Copy).then_inc(S("lr_done"), 1)
            for n in range(8):
                high(n + 3)
                dst = (k if n < 4 else q)[:, n % 4, :]
                act.wait_ge(S("ring_free"), n + 1)
                act.activation(halves(dst), out2(n % 3), ACT.Copy, scale=1.0 if n < 4 else DK ** -0.5) \
                   .then_inc(S("kq_done"), 1)
                if n < 4:
                    act.wait_ge(S("z_mm"), n + 1)
                    act.activation(halves(suf[:, n, :]), out2(3), ACT.Abs, bias=prm[:, B_A + n:B_A + n + 1]) \
                       .then_inc(S("z_abs"), 1)
            act.wait_ge(S("z_abs"), 4)
            act.activation(suf[:, :, :], suf[:, :, :], ACT.Exp, scale=-1.0).then_inc(S("z_exp"), 1)
            act.wait_ge(S("z_exp"), 1)
            act.activation(suf[:, :, :], suf[:, :, :], ACT.Ln, bias=one[:, :]).then_inc(S("z_ln"), 1)
            for n in range(TILE_V, TILE_C1):
                high(n + 3)
                if n % 4 == 3:
                    for t in range(TT):
                        m, c = ROWS[t], (n - TILE_V) // 4
                        if t < TT - 1:
                            act.wait_ge(S("v_mm"), (TT - 1) * c + t + 1)
                        else:
                            act.wait_ge(S("ring_free"), n + 1)
                        act.activation(v_tok[0:m, t, 512 * c:512 * c + 512], one_bank((TT * c + t) % 8)[0:m, :], ACT.Copy) \
                           .then_inc(S("v_done"), 1)
            for j in range(KT):
                n = TILE_C1 + 8 * j
                high(n + 3)
                act.wait_ge(S("ring_free"), n + 1)
                if j > 0:
                    act.wait_ge(S("u_done"), 3 * j)
                act.activation(halves(buf_a[:, :]), out2(c1_pair(j, 0)), ACT.Copy).then_inc(S("cg_done"), 1)
                for m in range(n + 4, n + 9):
                    high(m)
                if j + 1 < KT:
                    qd_exp(act, j + 1)
                high(n + 9)
                if 0 < j < KT - 1:
                    kd_exp(act, j + 1)
                high(n + 10)
                act.wait_ge(S("ring_free"), n + 7)
                if j > 0:
                    act.wait_ge(S("ya_done"), j)
                act.activation(halves(buf_b[:, :]), out2(c1_pair(j, 3)), ACT.Sigmoid).then_inc(S("sga_done"), 1)
            act.wait_ge(S("level_set"), 8)
            act.activation(suf[:, :, :], suf[:, :, :], ACT.Exp, scale=TAU_INV).then_inc(S("exps"), 1)
            act.activation(pre[:, :, :], pre[:, :, :], ACT.Exp, scale=TAU_INV).then_inc(S("exps"), 1)
            act.wait_ge(S("tails_tr"), 1)
            act.activation(tails_out[0:16, 0, :], one_bank(6)[0:16, 0:P], ACT.Copy).then_inc(S("tails_out"), 1)
            act.activation(tails_out[:, 1, :], one_bank(6)[:, P:2 * P], ACT.Copy).then_inc(S("tails_out"), 1)
            for c in range(NCH):
                act.wait_ge(S("k_tr"), c + 1)
                if c == 0:
                    act.wait_ge(S("decayed"), 1)
                if c >= 2:
                    act.wait_ge(S("delta_mm"), c - 1)
                act.activation(k_tok[c % 2][:, :], one_bank(0)[:, :], ACT.Copy).then_inc(S("k_tok_done"), 1)
                act.wait_ge(S("o_mm"), c + 1)
                act.activation(o[:, :, P * c:P * c + P], bank[2][:, :, :].rearrange("p a (m t) -> p (a m) t", t=P),
                               ACT.Copy).then_inc(S("o_done"), 1)
            act.wait_ge(S("ds_mm"), 8)
            for half in range(2):
                dst = o[:, :, SEQ:T].rearrange("p (h e) t -> p h e t", e=2)[:, :, half, :]
                act.activation(dst, bank[3][:, half, 0:256].rearrange("p (h t) -> p h t", t=64), ACT.Copy) \
                   .then_inc(S("o_done"), 1)
            def gates_b(i):
                for e in range(2):
                    if e == 1:
                        act.wait_ge(S("ssq_mm"), i * 2 + 1)
                    elif not isinstance(i, int) or i > 0:
                        act.wait_ge(S("silu_r"), i * 2)
                    act.activation(buf_a[:, :], row(o, i * 2 + e), ACT.Square).then_inc(S("o_sq"), 1)
                act.wait_ge(S("ssq_mm"), i * 2 + 2)
                if not isinstance(i, int) or i > 0:
                    act.wait_ge(S("gb_used"), i * 2)
                act.activation(halves(buf_b[:, :]), out2(3), ACT.Sqrt, bias=eps[:, :], scale=1.0 / DV) \
                   .then_inc(S("o_root"), 1)
                for e in range(2):
                    n = TILE_C2 + 2 * e
                    high(n + 3, i)
                    act.wait_ge(S("ring_free"), i * 4 + (n + 1))
                    if e == 1:
                        act.wait_ge(S("silu_r"), i * 2 + 1)
                    act.activation(halves(buf_a[:, :]), out2(C2_PAIR[2 * e]), ACT.Sigmoid).then_inc(S("sr_done"), 1)
                    high(n + 4, i)
                    act.wait_ge(S("ring_free"), i * 4 + (n + 2))
                    if e == 0:
                        act.wait_ge(S("o_recip"), i + 1)
                    else:
                        act.wait_ge(S("gb_used"), i * 2 + 1)
                    act.activation(halves(buf_b[:, :]), out2(C2_PAIR[2 * e + 1]), ACT.Sigmoid).then_inc(S("sgb_done"), 1)
                    act.wait_ge(S("m_done"), i * 2 + (e + 1))
                    act.activation(row(m_hi, i * 2 + e), cv[:, 0:T], ACT.Copy).then_inc(S("m_hi_done"), 1)

            act.wait_ge(S("o_done"), NCH + 2)
            gates_b(0)
            with act.Fori(1, HEADS - 1) as i:
                gates_b(i)
            gates_b(HEADS - 1)
            for n in range(TILE_WO + 3, TILE_UP):
                high(n)
            act_out(act)
            for n in range(TILE_UP, TILE_UP + 3):
                high(n)
            def ffn_up(i):
                for e in range(2):
                    n = TILE_UP + 2 * e
                    high(n + 3, i)
                    act.wait_ge(S("ring_free"), i * 4 + freed(n))
                    if e == 1 or not isinstance(i, int) or i > 0:
                        act.wait_ge(S("ftail_done"), i * 4 + 2 * e)
                    for src, dst, _, _ in conv_pieces(2 * e, ext, 2, TS + 2, 2):
                        act.activation(dst, src, ACT.Copy).then_inc(S("a_done"), 1)
                    high(n + 4, i)
                    act.wait_ge(S("fconv"), i * 6 + (3 * e + 3))
                    act.activation(cv[:, :], cv[:, :], ACT.Gelu_apprx_tanh).then_inc(S("gelu_done"), 1)
                    act.wait_ge(S("f_done"), i * 6 + (3 * e + 3))
                    act.activation(row(f_hi, i * 2 + e), buf_b[:, :], ACT.Copy).then_inc(S("f_hi_done"), 1)

            act.wait_ge(S("ext_zero"), 2)
            ffn_up(0)
            with act.Fori(1, FT // 2) as i:
                ffn_up(i)
            for n in range(TILE_DN, TILES):
                high(n + 3)
                if n == TILE_DN + 2:
                    act.wait_ge(S("ftails_tr"), 1)
                    for i in range(4):
                        m = (P, P, 96, 44)[i]
                        act.activation(ftails_out[0:m, i, :], one_bank(5)[0:m, P * i:P * i + P], ACT.Copy) \
                           .then_inc(S("ftails_out"), 1)
                if n == TILE_DN + 10:
                    for t in range(TT):
                        m = ROWS[t]
                        if t < TT - 1:
                            act.wait_ge(S("dn_mm"), t + 1)
                        else:
                            act.wait_ge(S("ring_free"), freed(n))
                        if t > 0:
                            act.wait_ge(S("f_sq"), t)
                        act.activation(sq_half[0:m, :], one_bank(t)[0:m, :], ACT.Square, accum_out=st_f[0:m, 0, t:t + 1]) \
                           .then_inc(S("f_sq"), 1)
                        act.activation(y_half[0:m, t, :], one_bank(t)[0:m, :], ACT.Copy).then_inc(S("yh_done"), 1)
            for t in range(TT):
                m = ROWS[t]
                if t < TT - 1:
                    act.wait_ge(S("dn_mm"), TT - 1 + t + 1)
                else:
                    act.wait_ge(S("ring_free"), freed(TILES - 1))
                act.wait_ge(S("f_sq"), TT + t)
                act.activation(sq_half[0:m, :], one_bank((TT + t) % 8)[0:m, :], ACT.Square, accum_out=st_f[0:m, 1, t:t + 1]) \
                   .then_inc(S("f_sq"), 1)
                act.wait_ge(S("f_sum"), t + 1)
                act.activation(st_f[0:m, 3, t:t + 1], st_f[0:m, 2, t:t + 1], ACT.Sqrt, bias=eps[0:m, :], scale=1.0 / D) \
                   .then_inc(S("f_root"), 1)

        @block.vector
        def _(dve):
            dve.wait_ge(S("c_sig"), 1)
            dve.tensor_tensor(c_t[:, :].rearrange("p (j s) -> p s j", j=KT), one_bank(2)[:, 0:72].rearrange("p (s j) -> p s j", j=KT),
                              c_sig[:, :].rearrange("p (s j) -> p s j", j=KT), ALU.mult).then_inc(S("c_done"), 1)
            c_view = c_t[:, :].rearrange("p (j s) -> p j s", j=KT)
            dve.wait_ge(S("c_done"), 1)
            dve.tensor_copy(c_hl[:, :, 0:9], c_view).then_inc(S("c_split"), 1)
            dve.wait_ge(S("c_split"), 1)
            dve.tensor_tensor(c_hl[:, :, 9:18], c_view, c_hl[:, :, 0:9].bitcast(F32), ALU.subtract).then_inc(S("c_split"), 1)
            dve.wait_ge(S("consts"), 9)
            dve.tensor_tensor(fold[:, :], ident[0:18, 0:9], ident[0:18, 9:18], ALU.add).then_inc(S("c_split"), 1)
            for t in range(TT):
                n = ROWS[t]
                dve.wait_ge(S("x_root"), t + 1)
                dve.reciprocal(st_x[0:n, 2, t:t + 1], st_x[0:n, 1, t:t + 1]).then_inc(S("x_rstd"), 1)
                dve.wait_ge(S("x_rstd"), t + 1)
                dve.tensor_scalar(x_tok[0:n, t, :], x_tok[0:n, t, :], st_x[0:n, 2, t:t + 1], None, ALU.mult) \
                   .then_inc(S("xn_done"), 1)
            for i in range(KT):
                dve.wait_ge(S("ada_hi_done"), i + 1)
                if i >= 2:
                    dve.wait_ge(S("ada0_mm"), i - 1)
                dve.tensor_tensor(ada_lo[i % 2][:, :], ada_first[:, i, :], ada_hi[i % 2][:, :].bitcast(F32), ALU.subtract) \
                   .then_inc(S("ada_lo_done"), 1)
                if i == KT - 2:
                    dve.wait_ge(S("rows_tr"), 1)
                    dve.tensor_copy(prm[:, :], one_bank(6)[:, 0:124]).then_inc(S("prm_done"), 1)
                    dve.tensor_copy(ffp[:, :], one_bank(6)[:, P:P + 88]).then_inc(S("prm_done"), 1)
                    dve.tensor_copy(mix0[:, :, :].rearrange("p a j -> p (a j)"), one_bank(7)[:, 0:P]).then_inc(S("prm_done"), 1)
                    dve.tensor_copy(ff0[:, :, :].rearrange("p a j -> p (a j)"), one_bank(7)[:, P:P + 352]) \
                       .then_inc(S("prm_done"), 1)
            dve.wait_ge(S("ada0_mm"), KT)
            for g in range(2, 4):
                dve.tensor_copy(rows_ada0[:, g, :], one_bank(g)[0:18, :]).then_inc(S("rows0_done"), 1)
            dve.wait_ge(S("back0"), 1)
            dve.wait_ge(S("prm_done"), 4)
            dve.tensor_tensor(mod[:, 0:16, :], one_bank(4)[:, 0:144].rearrange("p (m s) -> p m s", s=9),
                              spread(prm[:, 0:16], 9),
                              ALU.add).then_inc(S("mod_done"), 1)
            dve.wait_ge(S("mod_done"), 1)
            dve.scalar_tensor_tensor(mul1[:, :, :], mod[:, 8:16, :], 1.0, spread(prm[:, PRE1:PRE1 + 8], 9),
                                     ALU.add, ALU.mult).then_inc(S("mul1_done"), 1)
            dve.wait_ge(S("mul1_done"), 1)
            def h_low(i):
                dve.wait_ge(S("h32_done"), i + 1)
                dve.wait_ge(S("h_hi_done"), i + 1)
                dve.tensor_tensor(h_lo[:, i, :], h32[:, i, :], h_hi[:, i, :].bitcast(F32), ALU.subtract) \
                   .then_inc(S("h_lo_done"), 1)

            dve.wait_ge(S("x_ch"), TT)
            for i in range(KT):
                smp = h32[:, i, SEQ:T].rearrange("p (s t) -> p s t", t=TS)
                dve.tensor_scalar(h32[:, i, 0:SEQ], h32[:, i, 0:SEQ], mul1[:, i, 0:1], mod[:, i, 0:1], ALU.mult, ALU.add) \
                   .then_inc(S("h_prompt"), 1)
                dve.tensor_tensor(smp, smp, spread(mul1[:, i, 1:9], TS), ALU.mult) \
                   .then_inc(S("h_smp"), 1)
                if i >= 2:
                    h_low(i - 2)
                dve.wait_ge(S("h_smp"), i + 1)
                dve.wait_ge(S("h_prompt"), i + 1)
                dve.tensor_tensor(smp, smp, spread(mod[:, i, 1:9], TS), ALU.add) \
                   .then_inc(S("h32_done"), 1)
            for i in (KT - 2, KT - 1):
                h_low(i)
            for h in range(HEADS):
                dve.wait_ge(S("z_mm"), h + 1)
                dve.wait_ge(S("z_abs"), h + 1)
                dve.tensor_scalar(halves(pre[:, h, :]), out2(3), prm[:, B_A + h:B_A + h + 1], 0.0, ALU.add, ALU.min) \
                   .then_inc(S("z_min"), 1)
            dve.memset(score[:, :, :], 0.0).then_inc(S("score_zero"), 1)
            dve.wait_ge(S("z_ln"), 1)
            dve.wait_ge(S("z_min"), 4)
            dve.tensor_tensor(pre[:, :, :], pre[:, :, :], suf[:, :, :], ALU.subtract).then_inc(S("log_a"), 1)
            dve.wait_ge(S("log_a"), 1)
            dve.memset(suf[:, :, :], 0.0).then_inc(S("level_set"), 1)
            dve.memset(ext[:, 0:2], 0.0).then_inc(S("ext_zero"), 1)
            dve.wait_ge(S("ext_zero"), 1)
            dve.wait_ge(S("level_set"), 1)
            dve.wait_ge(S("score_zero"), 1)
            dve.wait_ge(S("consts"), 9)
            for j in range(KT):
                n = TILE_C1 + 8 * j
                for i in after_tile(j, 0):
                    take_item(dve, i)
                if j > 0:
                    dve.wait_ge(S("tail_done"), 2 * j)
                    dve.wait_ge(S("conv"), 3 * j)
                hist = ext[:, S0E:EXT].rearrange("p (s w) -> p s w", w=TS + 2)[:, :, 0:2]
                dve.tensor_copy(hist, mix0[:, :, j].rearrange("p (s w) -> p s w", w=2)).then_inc(S("hist"), 1)
                dve.wait_ge(S("cg_done"), j + 1)
                dve.wait_ge(S("ring_free"), n + 3)
                for src, dst, lo, hi in conv_pieces(c1_pair(j, 1), ext, 2, TS + 2, 2):
                    dve.tensor_tensor(dst, src, piece(buf_a, lo, hi), ALU.mult).then_inc(S("u_done"), 1)
                for i in after_tile(j, 2):
                    take_item(dve, i)
                dve.wait_ge(S("u_done"), 3 * (j + 1))
                dve.wait_ge(S("hist"), j + 1)
                if j > 0:
                    dve.wait_ge(S("t_done"), 3 * j)
                conv(dve, ext, cv, [prm[:, CW + 8 * w + j:CW + 8 * w + j + 1] for w in range(3)],
                     prm[:, CB + j:CB + j + 1], "conv", 3 * j)
                tails(dve, tail_mix[:, :, j], "tail_done")
                for i in after_tile(j, 4):
                    take_item(dve, i)
                dve.wait_ge(S("conv"), 3 * j + 3)
                dve.wait_ge(S("ring_free"), n + 5)
                for src, cvp, lo, hi in conv_pieces(c1_pair(j, 2), cv, 0, TS + 2, 2):
                    dve.tensor_tensor(piece(y_a[:, j, :], lo, hi), src, cvp, ALU.mult).then_inc(S("t_done"), 1)
                if j + 1 < KT:
                    dve_level(dve, j + 1)
                for i in after_tile(j, 6):
                    take_item(dve, i)
                if j > 0:
                    take_mod(dve, j - 1)
                dve.wait_ge(S("t_done"), 3 * (j + 1))
                dve.wait_ge(S("sga_done"), j + 1)
                dve.tensor_tensor(y_a[:, j, :], y_a[:, j, :], buf_b[:, :], ALU.mult).then_inc(S("ya_done"), 1)
                for i in after_tile(j, 7):
                    take_item(dve, i)
                dve.wait_ge(S("ring_free"), n + 8)
                if j > 0:
                    dve.wait_ge(S("back"), j)
                dve.tensor_copy(rows_ada[:, :], one_bank(6)[0:18, :]).then_inc(S("rows_ada"), 1)
            take_mod(dve, KT - 1)
            dve.wait_ge(S("mod_done"), 9)
            dve.scalar_tensor_tensor(mul2[:, :, :], mod[:, 32:40, :], 1.0, spread(prm[:, PRE2:PRE2 + 8], 9),
                                     ALU.add, ALU.mult).then_inc(S("scales"), 1)
            dve.tensor_tensor(g1n[:, :, :], mod[:, 16:24, :], spread(prm[:, POST1:POST1 + 8], 9),
                              ALU.mult).then_inc(S("scales"), 1)
            dve.tensor_tensor(g2n[:, :, :], mod[:, 40:48, :], spread(prm[:, POST2:POST2 + 8], 9),
                              ALU.mult).then_inc(S("scales"), 1)
            dve.wait_ge(S("scales"), 3)
            dve.tensor_copy(gx[:, :, :].rearrange("p k (s t) -> p k s t", t=TS), spread(g1n[:, :, 1:9], TS)) \
               .then_inc(S("gx_done"), 1)
            dve.wait_ge(S("exps"), 1)
            dve.wait_ge(S("item"), len(items))
            dve.tensor_tensor(k[:, :, :], k[:, :, :], suf[:, :, :], ALU.mult).then_inc(S("decayed"), 1)
            dve.wait_ge(S("exps"), 2)
            dve.tensor_tensor(q[:, :, :], q[:, :, :], pre[:, :, :], ALU.mult).then_inc(S("decayed"), 1)
            for c in range(NCH):
                dve.wait_ge(S("delta_mm"), c + 1)
                if c >= 2:
                    dve.wait_ge(S("o_mm"), c)
                new, old = state[c % 2], state[(c - 1) % 2]
                for h in range(HEADS):
                    delta = bank[1][:, :, :].rearrange("p a (h v) -> p (a h) v", v=DV)[:, h, :]
                    if c == 0:
                        ins = dve.tensor_copy(new[:, h, :], delta)
                    else:
                        if h == 0:
                            dve.wait_ge(S("state_done"), c)
                        ins = dve.scalar_tensor_tensor(new[:, h, :], old[:, h, :], pre[:, h, P * c + P - 1:P * c + P],
                                                       delta, ALU.mult, ALU.add)
                    if h == HEADS - 1:
                        ins.then_inc(S("state_done"), 1)
            for u in range(8):
                h, g = u // 2, u % 2
                if g == 0:
                    dve.wait_ge(S("ks_tr"), 1)
                    if h > 0:
                        dve.wait_ge(S("ds_mm"), 2 * h)
                    src = one_bank(1)[0:64, DK * h:DK * h + DK].rearrange("p (o d) -> p o d", o=1)
                    dve.tensor_tensor(k_own[:, :, :], src.to_broadcast([64, NS, DK]),
                                      spread(own[:, :], DK), ALU.mult).then_inc(S("k_own"), 1)
                dve.wait_ge(S("ds_mm"), u + 1)
                dve.wait_ge(S(f"s_in{u % 3}"), 16 * (u // 3 + 1))
                for s in range(4):
                    tok = SEQ + (4 * g + s) * TS + TS - 1
                    delta = bank[1 + u % 2][:, :, :].rearrange("p a (s v) -> p (a s) v", v=DV)[:, s, :]
                    dve.scalar_tensor_tensor(s_in[u % 3][:, s, :], s_in[u % 3][:, s, :], pre[:, h, tok:tok + 1], delta,
                                             ALU.mult, ALU.add).then_inc(S("s_done"), 1)
            dve.wait_ge(S("o_done"), NCH + 2)
            dve.wait_ge(S("tails_stored"), 32)
            dve.wait_ge(S("t_done"), 3 * KT)

            def merge(i):
                dve.wait_ge(S("o_root"), i + 1)
                dve.reciprocal(ext[:, 0:T], buf_b[:, :]).then_inc(S("o_recip"), 1)
                for e in range(2):
                    j = i * 2 + e
                    if e == 0:
                        dve.wait_ge(S("o_recip"), i + 1)
                    dve.tensor_tensor(row(o, j), row(o, j), ext[:, 0:T], ALU.mult).then_inc(S("o_norm"), 1)
                    dve.wait_ge(S("sr_done"), i * 2 + (e + 1))
                    if e == 1 or not isinstance(i, int) or i > 0:
                        dve.wait_ge(S("m_hi_done"), i * 2 + e)
                        dve.wait_ge(S("m_lo_done"), i * 2 + e)
                    dve.tensor_tensor(halves(cv[:, 0:T]), out2(C2_PAIR[2 * e]), halves(buf_a[:, :]), ALU.mult) \
                       .then_inc(S("silu_r"), 1)
                    dve.wait_ge(S("silu_r"), i * 2 + (e + 1))
                    dve.wait_ge(S("sgb_done"), i * 2 + (e + 1))
                    dve.tensor_tensor(cv[:, 0:T], cv[:, 0:T], buf_b[:, :], ALU.mult).then_inc(S("gb_used"), 1)
                    dve.wait_ge(S("gb_used"), i * 2 + (e + 1))
                    dve.wait_ge(S("o_norm"), i * 2 + (e + 1))
                    norm = prm[:, GN + j:GN + j + 1] if isinstance(j, int) else prm[:, bass.ds(j + GN, 1)]
                    dve.scalar_tensor_tensor(row(o, j), row(o, j), norm, cv[:, 0:T], ALU.mult, ALU.mult) \
                       .then_inc(S("y_b"), 1)
                    dve.wait_ge(S("y_b"), i * 2 + (e + 1))
                    dve.tensor_tensor(cv[:, 0:T], row(o, j), row(y_a, j), ALU.add).then_inc(S("m_done"), 1)
                    dve.wait_ge(S("m_done"), i * 2 + (e + 1))
                    dve.wait_ge(S("m_hi_done"), i * 2 + (e + 1))
                    dve.tensor_tensor(row(m_lo, j), cv[:, 0:T], row(m_hi, j).bitcast(F32), ALU.subtract) \
                       .then_inc(S("m_lo_done"), 1)

            merge(0)
            with dve.Fori(1, HEADS) as i:
                merge(i)
            dve.memset(ext[:, 0:2], 0.0).then_inc(S("ext_zero"), 1)
            for g in range(2):
                dve.wait_ge(S("gate1_mm"), g + 1)
                dve.wait_ge(S("m_lo_done"), KT)
                m = P if g == 0 else 64
                dve.tensor_copy(gate1[0:m, g, :], bank[3][0:m, :, :].rearrange("p a c -> p (a c)")) \
                   .then_inc(S("gate1_done"), 1)
            dve.wait_ge(S("x_back"), 32)
            dve.wait_ge(S("gate1_done"), 2)
            for t in range(TT):
                dve_out(dve, t)
            def ffn_mid(i):
                for e in range(2):
                    j = i * 2 + e
                    col = (lambda x: ffp[:, j + x:j + x + 1]) if isinstance(i, int) else (lambda x: ffp[:, bass.ds(j + x, 1)])
                    n = TILE_UP + 2 * e
                    later = e == 1 or not isinstance(i, int) or i > 0
                    if later:
                        dve.wait_ge(S("ftail_done"), i * 4 + 2 * e)
                    hist = ext[:, S0E:EXT].rearrange("p (s w) -> p s w", w=TS + 2)[:, :, 0:2]
                    if isinstance(i, int):
                        old = ff0[:, :, j].rearrange("p (s w) -> p s w", w=2)
                        new = tail_ff[:, :, j]
                    else:
                        old = ff0[:, :, bass.ds(j, 1)].rearrange("p (s w) o -> p s (w o)", w=2)
                        new = tail_ff[:, :, bass.ds(j, 1)].rearrange("p a o -> p (a o)")
                    dve.tensor_copy(hist, old).then_inc(S("fhist"), 1)
                    dve.wait_ge(S("a_done"), i * 6 + (3 * e + 3))
                    dve.wait_ge(S("fhist"), i * 2 + (e + 1))
                    if later:
                        dve.wait_ge(S("f_done"), i * 6 + 3 * e)
                    conv(dve, ext, cv, [col(FW + FT * w) for w in range(3)], col(FB), "fconv", i * 6 + 3 * e)
                    tails(dve, new, "ftail_done")
                    dve.wait_ge(S("gelu_done"), i * 2 + (e + 1))
                    dve.wait_ge(S("ring_free"), i * 4 + freed(n + 1))
                    for src, cvp, lo, hi in conv_pieces(2 * e + 1, cv, 0, TS + 2, 2):
                        dve.tensor_tensor(piece(buf_b, lo, hi), src, cvp, ALU.mult).then_inc(S("f_done"), 1)
                    dve.wait_ge(S("f_done"), i * 6 + (3 * e + 3))
                    dve.wait_ge(S("f_hi_done"), i * 2 + (e + 1))
                    dve.tensor_tensor(row(f_lo, j), buf_b[:, :], row(f_hi, j).bitcast(F32), ALU.subtract) \
                       .then_inc(S("f_lo_done"), 1)

            dve.wait_ge(S("ext_zero"), 2)
            ffn_mid(0)
            with dve.Fori(1, FT // 2) as i:
                ffn_mid(i)
            dve.tensor_copy(gx[:, :, :].rearrange("p k (s t) -> p k s t", t=TS), spread(g2n[:, :, 1:9], TS)) \
               .then_inc(S("gx_done"), 1)
            for g in range(2):
                dve.wait_ge(S("gate2_mm"), g + 1)
                m = P if g == 0 else 64
                dve.tensor_copy(gate2[0:m, g, :], bank[3][0:m, :, :].rearrange("p a c -> p (a c)")) \
                   .then_inc(S("gate2_done"), 1)
            for t in range(TT):
                m, g = ROWS[t], t // 4
                dve.wait_ge(S("f_sq"), TT + t + 1)
                dve.wait_ge(S("gate2_done"), 2)
                dve.tensor_tensor(st_f[0:m, 2, t:t + 1], st_f[0:m, 0, t:t + 1], st_f[0:m, 1, t:t + 1], ALU.add) \
                   .then_inc(S("f_sum"), 1)
                dve.wait_ge(S("f_root"), t + 1)
                dve.reciprocal(st_f[0:m, 2, t:t + 1], st_f[0:m, 3, t:t + 1]).then_inc(S("f_rstd"), 1)
                dve.wait_ge(S("f_rstd"), t + 1)
                dve.wait_ge(S("yh_done"), t + 1)
                dve.scalar_tensor_tensor(y_half[0:m, t, :], y_half[0:m, t, :], st_f[0:m, 2, t:t + 1],
                                         gate2[0:m, g, 0:512], ALU.mult, ALU.mult).then_inc(S("fin_a"), 1)
                if t > 0:
                    dve.wait_ge(S("y_out"), t)
                dve.scalar_tensor_tensor(buf_fin[0:m, :], one_bank((TT + t) % 8)[0:m, :], st_f[0:m, 2, t:t + 1],
                                         gate2[0:m, g, 512:1024], ALU.mult, ALU.mult).then_inc(S("fin_a"), 1)
                dve.wait_ge(S("fin_a"), 2 * t + 1)
                dve.tensor_tensor(x_tok[0:m, t, 0:512], x_tok[0:m, t, 0:512], y_half[0:m, t, :], ALU.add)
                dve.wait_ge(S("fin_a"), 2 * t + 2)
                dve.tensor_tensor(x_tok[0:m, t, 512:1024], x_tok[0:m, t, 512:1024], buf_fin[0:m, :], ALU.add) \
                   .then_inc(S("y_out"), 1)

        @block.tensor
        def _(pe):
            pe.wait_ge(S("consts"), 9)
            pe.wait_ge(S("c_in"), 32)
            pe.transpose(one_bank(2)[:, 0:72], rows_c[0:72, :], ident[0:72, 0:72]).then_inc(S("c_tr"), 1)

            def parameters():
                pe.wait_ge(S("rows_in"), 16 * 15)
                pe.wait_ge(S("x_ch"), 4)
                pe.transpose(one_bank(6)[:, 0:124], rows[0:124, :], ident[0:124, 0:124])
                pe.transpose(one_bank(6)[:, P:P + 88], rows_ffn[0:88, :], ident[0:88, 0:88])
                pe.transpose(one_bank(7)[:, 0:P], rows_mix[:, :], ident[:, :])
                for i in range(3):
                    n = min(P, 352 - P * i)
                    ins = pe.transpose(one_bank(7)[:, P + P * i:P + P * i + n], rows_ff0[0:n, i, :], ident[0:n, 0:n])
                ins.then_inc(S("rows_tr"), 1)

            def ada(dst, i, hi, lo, first, last):
                for p, w in enumerate((hi, lo)):
                    ins = pe.matmul(dst, c_hl[:, i, :], w, start=first and p == 0, stop=last and p == 1)
                return ins

            def ada_first_rows(i):
                pe.wait_ge(S("ada_lo_done"), i + 1)
                for g in range(4):
                    ins = ada(one_bank(g)[0:18, :], i, ada_hi[i % 2][:, 512 * g:512 * g + 512],
                              ada_lo[i % 2][:, 512 * g:512 * g + 512], i == 0, i == KT - 1)
                ins.then_inc(S("ada0_mm"), 1)

            pe.wait_ge(S("c_split"), 3)
            for i in range(KT):
                if i < TT:
                    n = ROWS[i]
                    pe.wait_ge(S("xn_done"), i + 1)
                    if i >= 2:
                        pe.wait_ge(S("x_ch"), i - 1)
                    for m in range(KT):
                        dst = bank[2 + i % 2][:, m // 4, P * (m % 4):P * (m % 4) + n]
                        ins = pe.transpose(dst, x_tok[0:n, i, P * m:P * m + P], ident[0:n, 0:n])
                    ins.then_inc(S("x_tr"), 1)
                ada_first_rows(i)
                if i == TT:
                    parameters()
            pe.wait_ge(S("rows0_done"), 4)
            pe.wait_ge(S("x_ch"), TT)
            for m in range(16):
                ins = pe.matmul(one_bank(4)[:, 9 * m:9 * m + 9], rows_ada0[:, m // 4, P * (m % 4):P * (m % 4) + P],
                                fold[:, :], start=True, stop=True)
            ins.then_inc(S("back0"), 1)

            def lr_rows(i):
                pe.wait_ge(S("h32_done"), i + 1)
                for half in range(2):
                    ins = pe.matmul(bank[3][0:RANK, half, 0:HALF], w_lr[:, i, :],
                                    h32[:, i, HALF * half:HALF * half + HALF], start=i == 0, stop=i == KT - 1)
                if i == KT - 1:
                    ins.then_inc(S("lr_mm"), 1)

            def channel_tile(hi, lo, pair, xs, first=False):
                x_hi, x_lo = xs
                for i in range(KT):
                    if first:
                        lr_rows(i)
                        pe.wait_ge(S("h_lo_done"), i + 1)
                    for w, x, p in ((hi, x_hi, 0), (hi, x_lo, 1), (lo, x_hi, 2)):
                        for half in range(2):
                            ins = pe.matmul(bank[pair][:, half, 0:HALF], w[:, i, :],
                                            x[:, i, HALF * half:HALF * half + HALF],
                                            start=i == 0 and p == 0, stop=i == KT - 1 and p == 2)
                ins.then_inc(S("ring_free"), 1)

            pe.wait_ge(S("lr_in"), 32)
            for n in range(8):
                pe.wait_ge(S("w_lo_done"), n + 1)
                if n >= 3:
                    pe.wait_ge(S("kq_done"), n - 2)
                channel_tile(kc(w_hi[n % 4]), kc(w_lo[n % 4]), n % 3, (h_hi, h_lo), first=n == 0)
                if n < 4:
                    pe.wait_ge(S("lr_done"), 1)
                    if n > 0:
                        pe.wait_ge(S("z_min"), n)
                    for half in range(2):
                        ins = pe.matmul(bank[3][:, half, 0:HALF], w_a2[:, DK * n:DK * n + DK],
                                        lr[:, HALF * half:HALF * half + HALF], start=True, stop=True)
                    ins.then_inc(S("z_mm"), 1)

            def token_tiles(n, g, banks, x_hi, x_lo, first, last, done):
                wh, wl = k2(w_hi[n % 4]), k2(w_lo[n % 4])
                for t in range(TT):
                    m = ROWS[t]
                    for i in range(2):
                        xh = x_hi[:, 2 * g + i, P * t:P * t + m]
                        xl = x_lo[:, 2 * g + i, P * t:P * t + m]
                        for p, (x, w) in enumerate(((xh, wh), (xh, wl), (xl, wh))):
                            ins = pe.matmul(one_bank(banks[t])[0:m, :], x, w[:, i, :],
                                            start=first and i == 0 and p == 0, stop=last and i == 1 and p == 2)
                    if last and t < TT - 1:
                        ins.then_inc(S(done), 1)
                return ins

            for n in range(8):
                c = n // 4
                pe.wait_ge(S("w_lo_done"), TILE_V + n + 1)
                if n == 0:
                    pe.wait_ge(S("kq_done"), 8)
                if n == 4:
                    pe.wait_ge(S("z_min"), 4)
                    pe.wait_ge(S("v_done"), 2)
                ins = token_tiles(TILE_V + n, n % 4, [(TT * c + t) % 8 for t in range(TT)], h_hi, h_lo,
                                  n % 4 == 0, n % 4 == 3, "v_mm")
                ins.then_inc(S("ring_free"), 1)
            pe.wait_ge(S("v_done"), 2 * TT)

            def score_item(i):
                lv, chunks = items[i]
                B = LEVELS[lv]
                dst = one_bank(7)
                if B:
                    pe.wait_ge(S("qd_done"), lv)
                    if B > 1:
                        pe.wait_ge(S("kd_done"), lv - 1)
                if i > 0:
                    pe.wait_ge(S("item_taken"), i)
                if lv >= 2:
                    pe.wait_ge(S("mod_done"), lv)
                kk = kd if B > 1 else k
                col = 0
                for c in chunks:
                    w = ROWS[c]
                    for h in range(HEADS):
                        lhs = kk[:, h, P * c:P * c + w]
                        if B == 0:
                            rhs, n = q[:, h, P * c:P * c + w], w
                        else:
                            at_ = (h * T + P * c) // 2 if B < 8 else (h * SEQ + P * c) // 2
                            rhs, n = qd[:, at_:at_ + w // 2], w // 2
                        ins = pe.matmul(dst[0:w, col:col + n], lhs, rhs, start=True, stop=True)
                        col += n
                ins.then_inc(S("item"), 1)

            def mod_back(j):
                pe.wait_ge(S("rows_ada"), j + 1)
                pe.wait_ge(S("item_taken"), items_to(min(j + 1, KT - 1)))
                if j > 0:
                    pe.wait_ge(S("mod_done"), j + 1)
                for m in range(4):
                    ins = pe.matmul(one_bank(7)[:, 9 * m:9 * m + 9], rows_ada[:, P * m:P * m + P], fold[:, :],
                                    start=True, stop=True)
                ins.then_inc(S("back"), 1)

            for j in range(KT):
                for e in range(8):
                    n = TILE_C1 + 8 * j + e
                    pe.wait_ge(S("w_lo_done"), n + 1)
                    if e % 2 == 0:
                        before = 4 * j + e // 2 - 3
                        if before >= 0:
                            name, count = (("cg_done", 1), ("u_done", 3), ("t_done", 3), ("sga_done", 1))[before % 4]
                            pe.wait_ge(S(name), count * (before // 4 + 1))
                        channel_tile(kc(w_hi[n % 4]), kc(w_lo[n % 4]), c1_pair(j, e // 2), (h_hi, h_lo))
                    else:
                        if e == 1 and j > 0:
                            pe.wait_ge(S("rows_ada"), j)
                        for i in range(2):
                            ins = ada(one_bank(6)[0:18, :], e // 2 * 2 + i, k2(w_hi[n % 4])[:, i, :], k2(w_lo[n % 4])[:, i, :],
                                      e == 1 and i == 0, e == 7 and i == 1)
                        ins.then_inc(S("ring_free"), 1)
                    for i in after_tile(j, e):
                        score_item(i)
                    if e == 6 and j > 0:
                        mod_back(j - 1)
            mod_back(KT - 1)
            pe.wait_ge(S("tail_done"), 2 * KT)
            pe.wait_ge(S("mod_done"), 9)
            pe.wait_ge(S("item_taken"), len(items))
            pe.transpose(one_bank(6)[0:16, 0:P], tail_mix[:, 0:2, :].rearrange("p a j -> p (a j)"), ident[:, :])
            pe.transpose(one_bank(6)[:, P:2 * P], tail_mix[:, 2:18, :].rearrange("p a j -> p (a j)"), ident[:, :]) \
              .then_inc(S("tails_tr"), 1)
            pe.wait_ge(S("decayed"), 1)
            pe.wait_ge(S("cg_done"), KT)
            pe.wait_ge(S("u_done"), 3 * KT)
            pe.wait_ge(S("t_done"), 3 * KT)
            pe.wait_ge(S("sga_done"), KT)
            for h in range(HEADS):
                ins = pe.transpose(one_bank(1)[0:64, DK * h:DK * h + DK], k[:, h, SEQ:T], ident[:, :])
            ins.then_inc(S("ks_tr"), 1)
            for c in range(NCH):
                if c >= 1:
                    pe.wait_ge(S("k_tok_done"), c)
                for h in range(HEADS):
                    ins = pe.transpose(one_bank(0)[:, DK * h:DK * h + DK], k[:, h, P * c:P * c + P], ident[:, :])
                ins.then_inc(S("k_tr"), 1)
                if c == 0:
                    pe.wait_ge(S("item_taken"), len(items))
                    pe.wait_ge(S("decayed"), 2)
                else:
                    pe.wait_ge(S("o_done"), c)
                    pe.wait_ge(S("state_done"), c)
                for h in range(HEADS):
                    for e in range(2):
                        mt = 2 * h + e
                        dst = bank[2][:, mt // 4, P * (mt % 4):P * (mt % 4) + P]
                        cols = DV * h + P * e
                        ins = pe.matmul(dst, v_tok[:, c, cols:cols + P], score[:, HEADS * c + h, :], start=True, stop=c == 0)
                        if c > 0:
                            ins = pe.matmul(dst, state[(c - 1) % 2][:, h, P * e:P * e + P], q[:, h, P * c:P * c + P],
                                            start=False, stop=True)
                ins.then_inc(S("o_mm"), 1)
                pe.wait_ge(S("k_tok_done"), c + 1)
                if c >= 1:
                    pe.wait_ge(S("state_done"), c)
                for h in range(HEADS):
                    dst = bank[1][:, h // 2, DV * (h % 2):DV * (h % 2) + DV]
                    ins = pe.matmul(dst, k_tok[c % 2][:, DK * h:DK * h + DK], v_tok[:, c, DV * h:DV * h + DV],
                                    start=True, stop=True)
                ins.then_inc(S("delta_mm"), 1)
            pe.wait_ge(S("tails_out"), 2)
            pe.wait_ge(S("o_done"), NCH)
            pe.wait_ge(S("state_done"), NCH)
            for u in range(8):
                h, g = u // 2, u % 2
                if g == 0:
                    for e in range(2):
                        pe.matmul(bank[3][:, e, 64 * h:64 * h + 64], v_tok[0:64, 4, DV * h + P * e:DV * h + P * e + P],
                                  score[0:64, HEADS * NCH + h, 0:64], start=True, stop=True)
                pe.wait_ge(S(f"s_in{u % 3}"), 16 * (u // 3 + 1))
                for e in range(2):
                    for s in range(4):
                        tok = (4 * g + s) * TS
                        pe.matmul(bank[3][:, e, 64 * h + tok:64 * h + tok + TS], s_in[u % 3][:, s, P * e:P * e + P],
                                  q[:, h, SEQ + tok:SEQ + tok + TS], start=False, stop=True,
                                  skip_group_check=True)
                pe.wait_ge(S("k_own"), h + 1)
                if u >= 2:
                    pe.wait_ge(S("s_done"), 4 * (u - 1))
                for s in range(4):
                    dst = bank[1 + u % 2][:, s // 2, DV * (s % 2):DV * (s % 2) + DV]
                    ins = pe.matmul(dst, k_own[:, 4 * g + s, :], v_tok[0:64, 4, DV * h:DV * h + DV], start=True, stop=True)
                ins.then_inc(S("ds_mm"), 1)
            pe.wait_ge(S("s_done"), 32)
            pe.wait_ge(S("o_done"), NCH + 2)
            def branch_b(i):
                later = not isinstance(i, int) or i > 0
                if later:
                    pe.wait_ge(S("o_root"), i)
                for e in range(2):
                    pe.wait_ge(S("o_sq"), i * 2 + (e + 1))
                    for half in range(2):
                        ins = pe.matmul(bank[3][:, half, 0:HALF], ones[:, :], buf_a[:, HALF * half:HALF * half + HALF],
                                        start=e == 0, stop=e == 1)
                    ins.then_inc(S("ssq_mm"), 1)
                for e in range(4):
                    n = TILE_C2 + e
                    pe.wait_ge(S("w_lo_done"), i * 4 + (n + 1))
                    if e == 3:
                        pe.wait_ge(S("silu_r"), i * 2 + 1)
                    elif later:
                        pe.wait_ge(S("silu_r" if e == 2 else "sgb_done"), i * 2)
                    channel_tile(kc(w_hi[n % 4]), kc(w_lo[n % 4]), C2_PAIR[e], (h_hi, h_lo))

            branch_b(0)
            with pe.Fori(1, HEADS) as i:
                branch_b(i)

            def gate_rows(src, g, done, name):
                m = P if g == 0 else 64
                if g == 1:
                    pe.wait_ge(S(done), 1)
                    pe.wait_ge(S("gx_done"), 1 if src is g1n else 2)
                for i in range(KT):
                    lhs = src[:, i, 0:1].to_broadcast([P, P]) if g == 0 else gx[:, i, :]
                    ins = pe.matmul(bank[3][0:m, i // 4, P * (i % 4):P * (i % 4) + P], lhs, ident[:, :],
                                    start=True, stop=True)
                ins.then_inc(S(name), 1)

            pe.wait_ge(S("scales"), 3)
            pe.wait_ge(S("o_root"), HEADS)
            for g in range(2):
                gate_rows(g1n, g, "gate1_done", "gate1_mm")
            pe.wait_ge(S("w_lo_done"), TILE_UP)
            pe.wait_ge(S("m_lo_done"), KT)
            pe.wait_ge(S("sgb_done"), KT)
            pe.wait_ge(S("silu_r"), KT)
            pe.wait_ge(S("gate1_done"), 2)

            def to_channels(t):
                m = ROWS[t]
                pe.wait_ge(S("xn2_done"), t + 1)
                if t > 0:
                    pe.wait_ge(S("h2_mul"), t)
                for i in range(KT):
                    ins = pe.transpose(bank[3][:, i // 4, P * (i % 4):P * (i % 4) + m], xn[0:m, P * i:P * i + P],
                                       ident[0:m, 0:m])
                ins.then_inc(S("h_tr"), 1)

            for t in range(TT):
                m = ROWS[t]
                if t >= 3:
                    pe.wait_ge(S("y_scaled"), t - 2)
                order = list(range(KT)) if t < TT - 1 else list(range(4, 8)) + list(range(4))
                for x, i in enumerate(order):
                    wh, wl = (wo_hi[:, i, :], wo_lo[:, i, :]) if i < 4 else (w_hi[i - 4][:, :], w_lo[i - 4][:, :])
                    xh, xl = m_hi[:, i, P * t:P * t + m], m_lo[:, i, P * t:P * t + m]
                    for c in range(2):
                        for p, (xx, w) in enumerate(((xh, wh), (xh, wl), (xl, wh))):
                            ins = pe.matmul(bank[t % 3][0:m, c, :], xx, w[:, 512 * c:512 * c + 512],
                                            start=x == 0 and p == 0, stop=x == KT - 1 and p == 2)
                    if t == TT - 1 and i >= 4:
                        ins.then_inc(S("ring_free"), 1)
                ins.then_inc(S("wo_mm"), 1)
                if t > 0:
                    to_channels(t - 1)
            to_channels(TT - 1)
            pe.wait_ge(S("h2_lo_done"), TT)
            def ffn_up(i):
                for e in range(4):
                    n = TILE_UP + e
                    pe.wait_ge(S("w_lo_done"), i * 4 + (n + 1))
                    if not isinstance(i, int) or i > 0:
                        if e < 2:
                            pe.wait_ge(S("f_done" if e % 2 else "a_done"), i * 6 - 3)
                        else:
                            pe.wait_ge(S("f_done" if e % 2 else "a_done"), i * 6)
                    channel_tile(kc(w_hi[n % 4]), kc(w_lo[n % 4]), e, (h_hi, h_lo))

            ffn_up(0)
            with pe.Fori(1, FT // 2) as i:
                ffn_up(i)
            pe.wait_ge(S("f_done"), 3 * FT)
            pe.wait_ge(S("a_done"), 3 * FT)
            pe.wait_ge(S("ftail_done"), 2 * FT)
            for i in range(4):
                lo, m = ((P * i, (P, P, 96)[i]) if i < 3 else (0, 44))
                src = (tail_ff[:, 2:18, :] if i < 3 else tail_ff[:, 0:2, :]).rearrange("p a j -> p (a j)")
                ins = pe.transpose(one_bank(5)[0:m, P * i:P * i + P], src[:, lo:lo + m], ident[:, :])
            ins.then_inc(S("ftails_tr"), 1)
            for n in range(FT):
                c, g = n // 11, n % 11
                pe.wait_ge(S("w_lo_done"), TILE_DN + n + 1)
                if c == 0:
                    pe.wait_ge(S("f_lo_done"), 2 * g + 2)
                if n == 0:
                    gate_rows(g2n, 0, "gate2_done", "gate2_mm")
                if n == 1:
                    gate_rows(g2n, 1, "gate2_done", "gate2_mm")
                if n == 11:
                    pe.wait_ge(S("ftails_out"), 4)
                    pe.wait_ge(S("gate2_done"), 2)
                    pe.wait_ge(S("yh_done"), 2)
                token_tiles(TILE_DN + n, g, [(TT * c + t) % 8 for t in range(TT)], f_hi, f_lo, g == 0, g == 10, "dn_mm") \
                    .then_inc(S("ring_free"), 1)


_INS = ["x_prompt", "x_sample", "c_prompt", "c_sample", "state_conv_mix", "state_gla", "state_conv_ffn",
        "w_ada", "b_ada", "norm_pre1", "norm_post1", "norm_pre2", "norm_post2", "w_in", "conv_w", "conv_b",
        "w_a2", "b_a", "gla_norm", "w_out", "w_up", "ffn_conv_w", "ffn_conv_b", "w_down"]
_OUTS = [("y_prompt", (1, SEQ, D)), ("y_sample", (NS, TS, D)),
         ("new_conv_mix_prompt", (1, 1, 2, D)), ("new_gla_prompt", (1, 1, HEADS, DK, DV)),
         ("new_conv_ffn_prompt", (1, 1, 2, FF)),
         ("new_conv_mix_sample", (1, NS, 2, D)), ("new_gla_sample", (1, NS, HEADS, DK, DV)),
         ("new_conv_ffn_sample", (1, NS, 2, FF))]


def kernel(**inputs):
    import concourse.bacc as _bacc
    from concourse.bass_utils import run_bass_kernel_spmd as _run

    nc = _bacc.Bacc("TRN2", target_bir_lowering=False, num_devices=1, dynamic_dma_scratch_size=1024)
    arrays, aps = {}, {}
    for name in _INS:
        arr = np.ascontiguousarray(inputs[name])
        arrays[f"in_{name}"] = arr
        aps[name] = nc.dram_tensor(f"in_{name}", arr.shape, mybir.dt.from_np(arr.dtype), kind="ExternalInput").ap()
    for name, shape in _OUTS:
        aps[name] = nc.dram_tensor(f"out_{name}", shape, F32, kind="ExternalOutput").ap()
    layer_program(nc, aps)
    r = _run(nc, [arrays], core_ids=[0])
    return tuple(r.results[0][f"out_{name}"] for name, _ in _OUTS)
```

```python
import numpy as np
import concourse.bass as bass
from concourse import mybir

F32 = mybir.dt.float32
F32R = mybir.dt.float32r
I32 = mybir.dt.int32
ALU = mybir.AluOpType
ACT = mybir.ActivationFunctionType

P = 128
D = 1024
KT = D // P
SEQ = 512
NS, TS = 8, 8
T = SEQ + NS * TS
HALF = T // 2
TT = 5
ROWS = [P, P, P, P, NS * TS]
HEADS, DK, DV = 4, 128, 256
RANK = 16
FF = 2816
FT = FF // P
EPS = 1e-6
TAU_INV = 1.0 / 16.0
NCH = SEQ // P
EXT = 2 + SEQ + NS * (2 + TS)
S0E = 2 + SEQ
CONV = EXT - 2

IN_BG, IN_CG, IN_UA = 0, D, 2 * D
IN_Q, IN_K, IN_V = 3 * D, 3 * D + HEADS * DK, 3 * D + 2 * HEADS * DK
IN_R = IN_V + HEADS * DV
IN_LR = IN_R + HEADS * DV
IN_GA = IN_LR + RANK
IN_GB = IN_GA + D

TILE_K, TILE_Q, TILE_V = 0, HEADS, 2 * HEADS
TILE_C1 = TILE_V + 8
TILE_C2 = TILE_C1 + 8 * KT
TILE_WO = TILE_C2 + 2 * KT
TILE_UP = TILE_WO + KT
TILE_DN = TILE_UP + 2 * FT
TILES = TILE_DN + FT
LEVELS = [0, 1, 2, 4, 8, 16, 32, 64]


WO_SLOT = [None, None, 0, 1, 2, None, None, 3]


def freed(n):
    return n + 1 if n < TILE_WO else n - 3


def layer_program(nc, a):
    base = 1152
    at = base

    def place(name, shape, dtype=F32, offset=None):
        nonlocal at
        size = int(np.prod(shape[1:])) * 4
        if offset is None:
            offset = at
            at += -(-size // 32) * 32
        return nc.alloc_sbuf_tensor_at(name, shape, dtype, offset=offset)

    raw = [place(f"raw{i}", [P, 1024]) for i in range(2)]
    w_hi = [place(f"w_hi{i}", [P, 1024], F32R) for i in range(4)]
    w_lo = [place(f"w_lo{i}", [P, 1024], F32R) for i in range(4)]
    x_at = at
    x_tok = place("x_tok", [P, TT, D])
    v_tok = place("v_tok", [P, TT, D], offset=x_at)
    h_at = at
    h_hi = place("h_hi", [P, KT, T], F32R)
    h_lo = place("h_lo", [P, KT, T], F32R)
    g_at = at
    at += 106496
    ada_first = place("ada_first", [P, KT, 2 * D], offset=g_at)
    q = place("q", [P, HEADS, T], offset=g_at)
    k = place("k", [P, HEADS, T], offset=g_at + 9216)
    pre = place("pre", [P, HEADS, T], offset=g_at + 18432)
    suf = place("suf", [P, HEADS, T], offset=g_at + 27648)
    kd = place("kd", [P, HEADS, T], offset=g_at + 36864)
    qd = place("qd", [P, HEADS * T // 2], offset=g_at + 46080)
    score = place("score", [P, TT * HEADS, P], offset=g_at + 50688)
    state = place("state", [P, NCH, DV], offset=g_at + 60928)
    y_a = place("y_a", [P, KT, T], offset=g_at + 69632)
    h32 = place("h32", [P, KT, T], offset=g_at + 69632)
    o_tok = place("o_tok", [P, TT, DV], offset=g_at + 88064)
    k_own = place("k_own", [NS * TS, NS, DK], offset=g_at + 93184)
    sq_o = place("sq_o", [P, DV], offset=g_at + 97280)
    tails_out = place("tails_out", [P, 2, P], offset=g_at + 49152)
    rows_ada = place("rows_ada", [18, 512], offset=g_at + 88064)
    rows_ada0 = place("rows_ada0", [18, 4, 512], offset=g_at + 96256)
    ada_hi = [place(f"ada_hi{i}", [P, 2 * D], F32R, offset=h_at + 8192 * i) for i in range(2)]
    ada_lo = [place(f"ada_lo{i}", [P, 2 * D], F32R, offset=h_at + 16384 + 8192 * i) for i in range(2)]
    k_tok = place("k_tok", [P, TT, DK], offset=g_at + 27648)
    q_own = place("q_own", [P, NS * (NS * TS + TS)], offset=g_at + 30208)
    s_in = [place(f"s_in{i}", [P, 4, DV], offset=g_at + 36864 + 4096 * i) for i in range(3)]
    m_hi = place("m_hi", [P, KT, T], F32R, offset=g_at + 69632)
    m_lo = place("m_lo", [P, KT, T], F32R, offset=g_at)
    wo_own = {i: (place(f"wo_hi{i}", [P, D], F32R, offset=g_at + hi), place(f"wo_lo{i}", [P, D], F32R, offset=g_at + lo))
              for i, hi, lo in ((0, 32512, 65024), (1, 98304, 102400), (5, 60928, 50688), (6, 54784, 45056))}
    gate1 = place("gate1", [P, 2, D], offset=g_at + 18432)
    xn = place("xn", [P, D], offset=g_at + 26624)
    y_tmp = place("y_tmp", [P, D], offset=g_at + 36864)
    h2_32 = place("h2_32", [P, KT, P], offset=g_at + 88064)
    sq_tok = place("sq_tok", [P, D], offset=g_at + 92160)
    f_hi = place("f_hi", [P, FT, SEQ], F32R, offset=g_at)
    f_lo = place("f_lo", [P, FT, SEQ], F32R, offset=g_at + FT * SEQ * 4)
    f_smp = place("f_smp", [P, FT, P], F32R, offset=g_at + 2 * FT * SEQ * 4)
    gate2 = place("gate2", [P, 2, D], offset=h_at)
    y_half = place("y_half", [P, TT, 512], offset=h_at + 8192)
    sq_half = place("sq_half", [P, 512], offset=h_at + 18432)
    smp_low = place("smp_low", [NS * TS, 2, 512], offset=h_at + 22528)
    t_at = at
    ext = place("ext", [P, EXT])
    cv = place("cv", [P, CONV])
    buf_a = place("buf_a", [P, T])
    buf_b = place("buf_b", [P, T])
    rows = place("rows", [P, P], offset=t_at)
    rows_ffn = place("rows_ffn", [P, P], offset=t_at + 512)
    rows_c = place("rows_c", [P, P], offset=t_at + 1024)
    rows_mix = place("rows_mix", [P, P], offset=t_at + 1536)
    rows_ff0 = place("rows_ff0", [P, 3, P], offset=t_at + 2048)
    w_lr = place("w_lr", [P, KT, RANK], offset=t_at + 3584)
    w_a2 = place("w_a2", [RANK, HEADS * DK], offset=t_at + 4096)
    lr = place("lr", [RANK, T], offset=t_at + 6144)
    sq0 = place("sq0", [P, D], offset=g_at + 90112)
    ftails_out = place("ftails_out", [P, 4, P], offset=h_at + 20480)
    buf_fin = place("buf_fin", [P, 512], offset=t_at)
    prm = place("prm", [P, 124])
    ffp = place("ffp", [P, 88])
    c_t = place("c_t", [P, 72], offset=t_at + 8736)
    c_sig = place("c_sig", [P, 72], offset=t_at + 8448)
    c_hl = place("c_hl", [P, KT, 18], F32R)
    fold = place("fold", [18, 9])
    mix0 = place("mix0", [P, 16, KT])
    ff0 = place("ff0", [P, 16, FT])
    mod = place("mod", [P, 48, 9])
    ident = place("ident", [P, P])
    ones = place("ones", [P, P])
    mask = place("mask", [P, 7, 64])
    own = place("own", [NS * TS, NS])
    mul1 = place("mul1", [P, KT, 9])
    mul2 = place("mul2", [P, KT, 9])
    g1n = place("g1n", [P, KT, 9])
    g2n = place("g2n", [P, KT, 9])
    gx = place("gx", [P, KT, NS * TS])
    eps = place("eps", [P, 1])
    one = place("one", [P, 1])
    st_x = place("st_x", [P, 3, TT])
    st_o = place("st_o", [P, 3, TT])
    st_y = place("st_y", [P, 3, TT])
    st_h = place("st_h", [P, 3, TT])
    st_f = place("st_f", [P, 4, TT])
    tail_mix = place("tail_mix", [P, 18, KT])
    tail_ff = place("tail_ff", [P, 18, FT])
    assert at <= 229368, at
    bank = [nc.alloc_psum_tensor(f"pair{i}", [P, 2, 512], F32) for i in range(4)]

    def one_bank(b):
        return bank[b // 2][:, b % 2, :]

    B_ADA, PRE1, POST1, PRE2, POST2, CW, CB, B_A, GN = 0, 48, 56, 64, 72, 80, 104, 112, 116
    FW, FB = 0, 66

    sems = {}

    def S(name):
        if name not in sems:
            sems[name] = nc.alloc_semaphore(name)
        return sems[name]

    w_in, w_up, w_down, w_out, w_ada = (a[n][0] for n in ("w_in", "w_up", "w_down", "w_out", "w_ada"))

    def in_cols(c0):
        return w_in[:, c0:c0 + P].rearrange("(k p) c -> p k c", p=P)

    def spread(v, n):
        if len(v.shape) == 2:
            return v.rearrange("p (m o) -> p m o", o=1).to_broadcast([v.shape[0], v.shape[1], n])
        return v.rearrange("p k (m o) -> p k m o", o=1).to_broadcast([v.shape[0], v.shape[1], v.shape[2], n])

    def row(buf, j):
        if isinstance(j, int):
            return buf[:, j, :]
        return buf[:, bass.ds(j, 1), :].rearrange("p o n -> p (o n)")

    def kc(tile):
        return tile[:, :].rearrange("p (k c) -> p k c", c=P)

    def k2(tile):
        return tile[:, :].rearrange("p (k c) -> p k c", c=512)

    gated = [cv[:, 0:T], ext[:, 0:T]]

    def halves(buf):
        return buf.rearrange("p (a t) -> p a t", a=2)

    def out2(pair):
        return bank[pair][:, :, 0:HALF]

    def conv_pieces(pair, buf, first, s_step, s_skip):
        s_at = first + SEQ
        smp = buf[:, s_at:s_at + NS * s_step].rearrange("p (s w) -> p s w", w=s_step)[:, :, s_skip:s_skip + TS]
        return [
            (bank[pair][:, 0, 0:HALF], buf[:, first:first + HALF], 0, HALF),
            (bank[pair][:, 1, 0:SEQ - HALF], buf[:, first + HALF:first + SEQ], HALF, SEQ),
            (bank[pair][:, 1, SEQ - HALF:HALF].rearrange("p (s w) -> p s w", w=TS), smp, SEQ, T),
        ]

    def piece(buf, lo, hi):
        v = buf[:, lo:hi]
        return v.rearrange("p (s w) -> p s w", w=TS) if lo == SEQ else v

    def c1_pair(j, i):
        return (4 * j + i) % 3

    def m_row(j):
        return j % 2 * HEADS + j // 2

    def wo_pair(t):
        return (2 * t + 2) % 3

    def w_pair(n):
        slot = n % 4
        if TILE_WO <= n < TILE_UP:
            slot = WO_SLOT[n - TILE_WO]
            if slot is None:
                return wo_own[n - TILE_WO]
        return w_hi[slot], w_lo[slot]

    def flat(pair):
        return bank[pair][:, :, :].rearrange("p a c -> p (a c)")

    items = []
    for lv, B in enumerate(LEVELS):
        items += [(lv, g) for g in ([[0], [1], [2], [3]] if B == 0 else [[0, 1], [2, 3]])]
        items += [(lv, [4])] if B < 8 else []

    def after_tile(j, e):
        level = [i for i, it in enumerate(items) if it[0] == j]
        slots = (0, 2, 4, 6, 7) if j == 0 else (0, 2, 4)
        return [i for i, slot in zip(level, slots) if slot == e]

    def items_to(lv):
        return sum(1 for it in items if it[0] <= lv)

    def block_view(buf, B, ch_tokens, side):
        return buf.rearrange("p (n s b) -> p n s b", s=2, b=B)[:, :, side, :]

    def store_state(sp, u):
        h, g = u // 2, u % 2
        sp.wait_ge(S("s_done"), 4 * (u + 1))
        sp.dma_start(a["new_gla_sample"][0, 4 * g:4 * g + 4, h].rearrange("s d v -> d s v"), s_in[u % 3][:, :, :]) \
          .then_inc(S(f"s_stored{u % 3}"), 16)

    def qd_exp(act, lv):
        B = LEVELS[lv]
        act.wait_ge(S("level_set"), lv)
        if lv > 1:
            act.wait_ge(S("item"), items_to(lv - 1))
        if B < 8:
            src = block_view(pre[:, :, :].rearrange("p h t -> p (h t)"), B, T, 1)
            dst = qd[:, :].rearrange("p (n b) -> p n b", b=B)
        else:
            src = pre[:, :, 0:SEQ].rearrange("p h (n s b) -> p h n s b", s=2, b=B)[:, :, :, 1, :]
            dst = qd[:, 0:HEADS * SEQ // 2].rearrange("p (h n b) -> p h n b", h=HEADS, b=B)
        act.activation(dst, src, ACT.Exp, scale=TAU_INV).then_inc(S("qd_exp"), 1)

    def kd_exp(act, lv):
        w = T if LEVELS[lv] < 8 else SEQ
        act.activation(kd[:, :, 0:w], suf[:, :, 0:w], ACT.Exp, scale=TAU_INV).then_inc(S("kd_exp"), 1)

    def act_out(act, high):
        for t in range(TT):
            m = ROWS[t]
            act.wait_ge(S("wo_mm"), t + 1)
            act.activation(sq_tok[0:m, :], flat(wo_pair(t))[0:m, :], ACT.Square,
                           accum_out=st_y[0:m, 0, t:t + 1]).then_inc(S("y_sq"), 1)
            act.wait_ge(S("y_sq"), t + 1)
            act.activation(st_y[0:m, 1, t:t + 1], st_y[0:m, 0, t:t + 1], ACT.Sqrt, bias=eps[0:m, :], scale=1.0 / D) \
               .then_inc(S("y_root"), 1)
            act.wait_ge(S("x1_done"), t + 1)
            act.activation(sq_tok[0:m, :], x_tok[0:m, t, :], ACT.Square, accum_out=st_h[0:m, 0, t:t + 1]) \
               .then_inc(S("x1_sq"), 1)
            act.wait_ge(S("x1_sq"), t + 1)
            act.activation(st_h[0:m, 1, t:t + 1], st_h[0:m, 0, t:t + 1], ACT.Sqrt, bias=eps[0:m, :], scale=1.0 / D) \
               .then_inc(S("x1_root"), 1)
            if t == TT - 2:
                high(TILE_UP)
                high(TILE_UP + 1)
            if t == TT - 1:
                high(TILE_UP + 2)
            act.wait_ge(S("h2_done"), t + 1)
            act.activation(h_hi[:, :, P * t:P * t + m], h2_32[:, :, 0:m], ACT.Copy).then_inc(S("h2_hi_done"), 1)

    def conv(dve, src, dst, w, b, name, count):
        dve.tensor_scalar(dst[:, :], src[:, 2:EXT], w[2], b, ALU.mult, ALU.add).then_inc(S(name), 1)
        for i, tap in enumerate((1, 0)):
            dve.wait_ge(S(name), count + (i + 1))
            dve.scalar_tensor_tensor(dst[:, :], src[:, tap:tap + CONV], w[tap], dst[:, :], ALU.mult, ALU.add) \
               .then_inc(S(name), 1)

    def tails(dve, dst, name):
        dve.tensor_copy(dst[:, 0:2], ext[:, SEQ:SEQ + 2]).then_inc(S(name), 1)
        last = ext[:, S0E:EXT].rearrange("p (s w) -> p s w", w=TS + 2)[:, :, TS:TS + 2]
        dve.tensor_copy(dst[:, 2:18].rearrange("p (s w) -> p s w", w=2), last).then_inc(S(name), 1)

    def dve_level(dve, lv):
        B = LEVELS[lv]
        if B:
            dve.wait_ge(S("level_set"), lv)
            dve.wait_ge(S("qd_exp"), lv)
            if B < 8:
                src = block_view(q[:, :, :].rearrange("p h t -> p (h t)"), B, T, 1)
                dst = qd[:, :].rearrange("p (n b) -> p n b", b=B)
            else:
                src = q[:, :, 0:SEQ].rearrange("p h (n s b) -> p h n s b", s=2, b=B)[:, :, :, 1, :]
                dst = qd[:, 0:HEADS * SEQ // 2].rearrange("p (h n b) -> p h n b", h=HEADS, b=B)
            dve.tensor_tensor(dst, dst, src, ALU.mult).then_inc(S("qd_done"), 1)
            if B > 1:
                w = T if B < 8 else SEQ
                dve.wait_ge(S("kd_exp"), lv - 1)
                dve.tensor_tensor(kd[:, :, 0:w], kd[:, :, 0:w], k[:, :, 0:w], ALU.mult).then_inc(S("kd_done"), 1)
            w = T if B < 8 else SEQ

            def side(buf, s, last=False):
                if B < 8:
                    v = buf[:, :, :].rearrange("p h t -> p (h t)").rearrange("p (n s b) -> p n s b", s=2, b=B)
                    v = v[:, :, s, B - 1:B] if last else v[:, :, s, :]
                    return v.to_broadcast([P, HEADS * T // (2 * B), B]) if last else v
                v = buf[:, :, 0:SEQ].rearrange("p h (n s b) -> p h n s b", s=2, b=B)
                v = v[:, :, :, s, B - 1:B] if last else v[:, :, :, s, :]
                return v.to_broadcast([P, HEADS, SEQ // (2 * B), B]) if last else v

            dve.tensor_tensor(side(suf, 0), side(suf, 0), side(pre, 1, True), ALU.add).then_inc(S("suf_add"), 1)
            dve.wait_ge(S("suf_add"), lv)
            dve.tensor_tensor(side(pre, 1), side(pre, 1), side(pre, 0, True), ALU.add).then_inc(S("level_set"), 1)

    def take_item(dve, i):
        lv, chunks = items[i]
        B = LEVELS[lv]
        src = one_bank(7)
        ch, nch = chunks[0] * HEADS, len(chunks) * HEADS
        m = ROWS[chunks[0]]
        dve.wait_ge(S("item"), i + 1)
        if B == 0:
            dst = score[0:m, ch:ch + nch, 0:m]
            msk = ident[0:m, 0:m].bitcast(I32).rearrange("p (o t) -> p o t", o=1).to_broadcast([m, nch, m])
            data = src[0:m, 0:nch * m].rearrange("p (c t) -> p c t", t=m)
        else:
            dst = score[0:m, ch:ch + nch, 0:m].rearrange("p c (n s b) -> p c n s b", s=2, b=B)[:, :, :, 1, :]
            msk = mask[0:m, lv - 1, 0:m // 2].bitcast(I32).rearrange("p (o n b) -> p o n b", o=1, b=B) \
                .to_broadcast([m, nch, m // 2 // B, B])
            data = src[0:m, 0:nch * m // 2].rearrange("p (c n b) -> p c n b", c=nch, b=B)
        dve.copy_predicated(dst, msk, data).then_inc(S("item_taken"), 1)

    def take_mod(dve, j):
        dve.wait_ge(S("back"), j + 1)
        dve.tensor_tensor(mod[:, 16 + 4 * j:20 + 4 * j, :], one_bank(7)[:, 0:36].rearrange("p (m s) -> p m s", s=9),
                          spread(prm[:, 16 + 4 * j:20 + 4 * j], 9), ALU.add).then_inc(S("mod_done"), 1)

    def dve_out(dve, t):
        m, g = ROWS[t], t // 4
        dve.wait_ge(S("y_root"), t + 1)
        dve.reciprocal(st_y[0:m, 2, t:t + 1], st_y[0:m, 1, t:t + 1]).then_inc(S("y_rstd"), 1)
        dve.wait_ge(S("y_rstd"), t + 1)
        if t > 0:
            dve.wait_ge(S("x1_done"), t)
        dve.scalar_tensor_tensor(y_tmp[0:m, :], flat(wo_pair(t))[0:m, :],
                                 st_y[0:m, 2, t:t + 1], gate1[0:m, g, :], ALU.mult, ALU.mult).then_inc(S("y_scaled"), 1)
        dve.wait_ge(S("y_scaled"), t + 1)
        dve.tensor_tensor(x_tok[0:m, t, :], x_tok[0:m, t, :], y_tmp[0:m, :], ALU.add).then_inc(S("x1_done"), 1)
        dve.wait_ge(S("x1_root"), t + 1)
        dve.reciprocal(st_h[0:m, 2, t:t + 1], st_h[0:m, 1, t:t + 1]).then_inc(S("x1_rstd"), 1)
        dve.wait_ge(S("x1_rstd"), t + 1)
        if t > 0:
            dve.wait_ge(S("h_tr"), t)
        dve.tensor_scalar(xn[0:m, :], x_tok[0:m, t, :], st_h[0:m, 2, t:t + 1], None, ALU.mult).then_inc(S("xn2_done"), 1)
        dve.wait_ge(S("h_tr"), t + 1)
        if t > 0:
            dve.wait_ge(S("h2_hi_done"), t)
            dve.wait_ge(S("h2_lo_done"), t)
        src = bank[3][:, :, :].rearrange("p a (k t) -> p (a k) t", t=P)[:, :, 0:m]
        dst = h2_32[:, :, 0:m]
        if g == 0:
            mul, add = (v.to_broadcast([P, KT, P]) for v in (mul2[:, :, 0:1], mod[:, 24:32, 0:1]))
        else:
            src = src.rearrange("p k (s t) -> p k s t", t=TS)
            dst = dst.rearrange("p k (s t) -> p k s t", t=TS)
            mul, add = (spread(v, TS) for v in (mul2[:, :, 1:9], mod[:, 24:32, 1:9]))
        dve.tensor_tensor(dst, src, mul, ALU.mult).then_inc(S("h2_mul"), 1)
        dve.wait_ge(S("h2_mul"), t + 1)
        dve.tensor_tensor(dst, dst, add, ALU.add).then_inc(S("h2_done"), 1)
        dve.wait_ge(S("h2_hi_done"), t + 1)
        dve.tensor_tensor(h_lo[:, :, P * t:P * t + m], h2_32[:, :, 0:m], h_hi[:, :, P * t:P * t + m].bitcast(F32),
                          ALU.subtract).then_inc(S("h2_lo_done"), 1)

    with nc.Block() as block:

        @block.sync
        def _(sp):
            def load_raw(n, src):
                if n >= 2:
                    sp.wait_ge(S("w_lo_done"), n - 1)
                dst = raw[n % 2][:, :]
                if len(src.shape) == 3:
                    dst = dst.rearrange("p (k c) -> p k c", k=src.shape[1])
                sp.dma_start(dst, src).then_inc(S(f"raw_in{n % 2}"), 16)

            for t in range(NCH):
                sp.dma_start(x_tok[:, t, :], a["x_prompt"][0, P * t:P * t + P, :]).then_inc(S(f"x_in{t}"), 16)
            sp.dma_start(x_tok[0:64, 4, :], a["x_sample"].rearrange("b t d -> (b t) d")).then_inc(S(f"x_in{NCH}"), 16)
            small = []
            r = 0
            for name in ("b_ada", "norm_pre1", "norm_post1", "norm_pre2", "norm_post2"):
                n = a[name].shape[1] // P
                small.append((rows[r:r + n, :], a[name].rearrange("o (j p) -> (o j) p", p=P)))
                r += n
            small.append((rows[r:r + 24, :], a["conv_w"][0].rearrange("w (j p) -> (w j) p", p=P)))
            small.append((rows[r + 24:r + 32, :], a["conv_b"].rearrange("o (j p) -> (o j) p", p=P)))
            small.append((rows[r + 32:r + 36, :], a["b_a"].rearrange("o (j p) -> (o j) p", p=P)))
            small.append((rows[r + 36:r + 44, :], a["gla_norm"][0].rearrange("h (j p) -> (h j) p", p=P)))
            small.append((rows_ffn[0:66, :], a["ffn_conv_w"][0].rearrange("w (j p) -> (w j) p", p=P)))
            small.append((rows_ffn[66:88, :], a["ffn_conv_b"].rearrange("o (j p) -> (o j) p", p=P)))
            small.append((rows_mix[:, :], a["state_conv_mix"][0].rearrange("s w (j p) -> (s w j) p", p=P)))
            ffr = a["state_conv_ffn"][0].rearrange("s w (j p) -> (s w j) p", p=P)
            for i in range(3):
                n = min(P, 352 - P * i)
                small.append((rows_ff0[0:n, i, :], ffr[P * i:P * i + n, :]))
            for i in range(KT):
                sp.dma_start(ada_first[:, i, :], w_ada[P * i:P * i + P, 0:2 * D]).then_inc(S(f"ada_in{i}"), 16)
                for dst, src in small[3 * i:3 * i + 3]:
                    sp.dma_start(dst, src).then_inc(S("rows_in"), 16)
            sp.dma_start(w_lr[:, :, :], w_in[:, IN_LR:IN_LR + RANK].rearrange("(k p) c -> p k c", p=P)) \
              .then_inc(S("lr_in"), 16)
            sp.dma_start(w_a2[:, :], a["w_a2"][0]).then_inc(S("lr_in"), 16)
            for h in range(HEADS):
                load_raw(TILE_K + h, in_cols(IN_K + h * DK))
            for h in range(HEADS):
                load_raw(TILE_Q + h, in_cols(IN_Q + h * DK))
            v_w = w_in[:, IN_V:IN_V + D].rearrange("(g k p) c -> g p k c", p=P, k=2)
            for n in range(8):
                load_raw(TILE_V + n, v_w[n % 4, :, :, 512 * (n // 4):512 * (n // 4) + 512])
            def load_c2(n):
                load_raw(TILE_C2 + n, in_cols((IN_R, IN_GB)[n % 2] + P * (n // 2)))

            ada_v = w_ada.rearrange("(g k p) c -> g p k c", p=P, k=2)
            for j in range(KT):
                for i, c0 in enumerate((IN_CG, IN_UA, IN_BG, IN_GA)):
                    load_raw(TILE_C1 + 8 * j + 2 * i, in_cols(c0 + P * j))
                    load_raw(TILE_C1 + 8 * j + 2 * i + 1, ada_v[i, :, :, 2 * D + 512 * j:2 * D + 512 * j + 512])
            for n in range(4):
                load_c2(n)
            def load_state(u):
                h, g = u // 2, u % 2
                sp.dma_start(s_in[u % 3][:, :, :], a["state_gla"][0, 4 * g:4 * g + 4, h].rearrange("s d v -> d s v")) \
                  .then_inc(S(f"s_in{u % 3}"), 16)

            sp.wait_ge(S("item"), len(items))
            for u in range(3):
                load_state(u)
            for h in range(HEADS):
                if h < HEADS - 1:
                    for n in range(4 * h + 4, 4 * h + 8):
                        load_c2(n)
                else:
                    for n in range(6):
                        load_raw(TILE_WO + n, w_out[P * n:P * n + P, :])
                if h == 0:
                    sp.wait_ge(S("tails_out"), 2)
                    tm = a["new_conv_mix_prompt"][0, 0].rearrange("w (j p) -> (w j) p", p=P)
                    sp.dma_start(tm, tails_out[0:16, 0, :]).then_inc(S("tails_stored"), 16)
                    ts = a["new_conv_mix_sample"][0].rearrange("s w (j p) -> (s w j) p", p=P)
                    sp.dma_start(ts, tails_out[:, 1, :]).then_inc(S("tails_stored"), 16)
                sp.wait_ge(S("state_done"), NCH * (h + 1))
                sp.dma_start(a["new_gla_prompt"][0, 0, h], state[:, NCH - 1, :]).then_inc(S("state_stored"), 16)
                for u in (2 * h, 2 * h + 1):
                    store_state(sp, u)
                for u in (2 * h + 3, 2 * h + 4):
                    if u < 8:
                        sp.wait_ge(S(f"s_stored{u % 3}"), 16 * (u // 3))
                        load_state(u)
            for n in range(6, KT):
                load_raw(TILE_WO + n, w_out[P * n:P * n + P, :])
            sp.wait_ge(S("ds_mm"), 8)
            sp.wait_ge(S("o_mm"), HEADS)
            sp.dma_start(x_tok[:, 0:4, :], a["x_prompt"][0].rearrange("(t p) d -> p t d", p=P)).then_inc(S("x_back"), 16)
            sp.dma_start(x_tok[0:64, 4, :], a["x_sample"].rearrange("b t d -> (b t) d")).then_inc(S("x_back"), 16)
            with sp.Fori(0, FT) as j:
                for i in range(2):
                    sp.wait_ge(S("w_lo_done"), j * 2 + (TILE_UP + i - 1))
                    src = w_up[:, bass.ds(j * P + i * FF, P)].rearrange("(k p) c -> p k c", p=P)
                    sp.dma_start(kc(raw[i]), src).then_inc(S(f"raw_in{i}"), 16)
            dn = w_down.rearrange("(g k p) c -> g p k c", p=P, k=2)
            for n in range(FT):
                load_raw(TILE_DN + n, dn[n % 11, :, :, 512 * (n // 11):512 * (n // 11) + 512])
            sp.wait_ge(S("ftails_out"), 4)
            fp = a["new_conv_ffn_prompt"][0, 0].rearrange("w (j p) -> (w j) p", p=P)
            sp.dma_start(fp, ftails_out[0:44, 3, :]).then_inc(S("out_stored"), 16)
            fs = a["new_conv_ffn_sample"][0].rearrange("s w (j p) -> (s w j) p", p=P)
            for i in range(3):
                n = min(P, 352 - P * i)
                sp.dma_start(fs[P * i:P * i + n, :], ftails_out[0:n, i, :]).then_inc(S("out_stored"), 16)
            for t in range(TT):
                sp.wait_ge(S("y_out"), t + 1)
                if t < 4:
                    dst = a["y_prompt"][0, P * t:P * t + P, :]
                else:
                    dst = a["y_sample"].rearrange("b t d -> (b t) d")
                sp.dma_start(dst, x_tok[0:ROWS[t], t, :]).then_inc(S("out_stored"), 16)
            sp.wait_ge(S("out_stored"), 16 * (4 + TT))
            sp.wait_ge(S("state_stored"), 16 * HEADS)
            sp.wait_ge(S("tails_stored"), 32)
            for u in range(3):
                sp.wait_ge(S(f"s_stored{u}"), 16 * ((7 - u) // 3 + 1))

        @block.gpsimd
        def _(pool):
            pool.memset(ident[:, :], 0.0).then_inc(S("p_set"), 1)
            pool.memset(mask[:, :, :], 1.0).then_inc(S("p_set"), 1)
            pool.memset(own[:, :], 1.0).then_inc(S("p_set"), 1)
            pool.memset(ones[:, :], 1.0).then_inc(S("p_set"), 1)
            pool.memset(eps[:, :], EPS).then_inc(S("p_set"), 1)
            pool.memset(one[:, :], 1.0).then_inc(S("p_set"), 1)
            pool.wait_ge(S("p_set"), 6)
            pool.affine_select(out=ident[:, :], in_=ident[:, :], compare_op=ALU.not_equal, fill=1.0, base=0,
                               pattern=[[-1, P]], channel_multiplier=1).then_inc(S("consts"), 1)
            for i, B in enumerate(LEVELS[1:]):
                m = mask[:, i, :].rearrange("p (n b) -> p n b", b=B)
                pool.affine_select(out=m, in_=m, compare_op=ALU.is_ge, fill=0.0, base=0,
                                   pattern=[[-2 * B, 64 // B], [0, B]], channel_multiplier=1).then_inc(S("p_sel"), 1)
                pool.wait_ge(S("p_sel"), i + 1)
                pool.affine_select(out=m, in_=m, compare_op=ALU.is_ge, fill=0.0, base=B - 1,
                                   pattern=[[2 * B, 64 // B], [0, B]], channel_multiplier=-1).then_inc(S("consts"), 1)
            pool.affine_select(out=own[:, :], in_=own[:, :], compare_op=ALU.is_ge, fill=0.0, base=0,
                               pattern=[[-TS, NS]], channel_multiplier=1).then_inc(S("p_sel"), 1)
            pool.wait_ge(S("p_sel"), 8)
            pool.affine_select(out=own[:, :], in_=own[:, :], compare_op=ALU.is_ge, fill=0.0, base=TS - 1,
                               pattern=[[TS, NS]], channel_multiplier=-1).then_inc(S("consts"), 1)

            def low(r, hi, lo, done):
                pool.wait_ge(S("w_hi_done"), done)
                pool.tensor_tensor(lo, raw[r % 2][:, :], hi.bitcast(F32), ALU.subtract).then_inc(S("w_lo_done"), 1)

            with pool.Fori(0, TILE_C2 // 4 + 1) as g:
                for r in range(4):
                    low(r, w_hi[r][:, :], w_lo[r][:, :], g * 4 + (r + 1))
            pool.wait_ge(S("decayed"), 2)
            pool.memset(q_own[:, :], 0.0).then_inc(S("p_set"), 1)
            pool.wait_ge(S("p_set"), 7)
            pool.wait_ge(S("back"), KT)
            for h in range(HEADS):
                pool.wait_ge(S("k_tok_done"), 2 * h + 2)
                if h > 0:
                    pool.wait_ge(S("ds_mm"), 2 * h)
                    pool.wait_ge(S("os_mm"), h)
                pool.tensor_tensor(k_own[:, :, :], k_tok[0:64, NCH, :].rearrange("p (o d) -> p o d", o=1)
                                   .to_broadcast([64, NS, DK]), spread(own[:, :], DK), ALU.mult).then_inc(S("k_own"), 1)
                pool.tensor_copy(q_own[:, :].rearrange("p (s w) -> p s w", w=NS * TS + TS)[:, :, 0:TS],
                                 q[:, h, SEQ:T].rearrange("p (s w) -> p s w", w=TS)).then_inc(S("q_own"), 1)
                for r in range(4 if h < HEADS - 1 else KT):
                    n = TILE_C2 + 4 * h + 4 + r
                    hi, lo = w_pair(n)
                    low(r, hi[:, :], lo[:, :], n + 1)
            with pool.Fori(TILE_UP // 4, TILES // 4) as g:
                for r in range(4):
                    low(r, w_hi[r][:, :], w_lo[r][:, :], g * 4 + (r + 1))
            for n in range(TILES // 4 * 4, TILES):
                low(n, w_hi[n % 4][:, :], w_lo[n % 4][:, :], n + 1)

        @block.scalar
        def _(act):
            def high(n, turn=0):
                if isinstance(turn, int):
                    n, turn = n + 4 * turn, 0
                if n >= TILES:
                    return
                act.wait_ge(S(f"raw_in{n % 2}"), turn * 32 + 16 * (n // 2 + 1))
                dst = w_pair(n)[0][:, :]
                if not TILE_WO <= n < TILE_UP:
                    if n >= 4:
                        act.wait_ge(S("ring_free"), turn * 4 + (freed(n) - 4))
                elif WO_SLOT[n - TILE_WO] is not None:
                    act.wait_ge(S("ring_free"), TILE_C2 + 4 * (HEADS - 1) + WO_SLOT[n - TILE_WO] + 1)
                elif n == TILE_WO + 5:
                    act.wait_ge(S("os_mm"), HEADS)
                    act.wait_ge(S("state_stored"), 16 * HEADS)
                    act.wait_ge(S("s_stored2"), 32)
                act.activation(dst, raw[n % 2][:, :], ACT.Copy).then_inc(S("w_hi_done"), 1)

            act.dma_start(rows_c[0:8, :], a["c_prompt"].rearrange("b (j p) -> (b j) p", p=P)).then_inc(S("c_in"), 16)
            act.dma_start(rows_c[8:72, :], a["c_sample"].rearrange("b (j p) -> (b j) p", p=P)).then_inc(S("c_in"), 16)
            act.wait_ge(S("c_tr"), 1)
            act.activation(c_sig[:, :], one_bank(2)[:, 0:72], ACT.Sigmoid).then_inc(S("c_sig"), 1)
            act.wait_ge(S("p_set"), 6)
            for t in range(TT):
                n = ROWS[t]
                act.wait_ge(S(f"x_in{t}"), 16)
                if t > 0:
                    act.wait_ge(S("x_sq"), t)
                act.activation(sq0[0:n, :], x_tok[0:n, t, :], ACT.Square, accum_out=st_x[0:n, 0, t:t + 1]) \
                   .then_inc(S("x_sq"), 1)
            for t in range(TT):
                n = ROWS[t]
                act.wait_ge(S("x_sq"), t + 1)
                act.activation(st_x[0:n, 1, t:t + 1], st_x[0:n, 0, t:t + 1], ACT.Sqrt, bias=eps[0:n, :],
                               scale=1.0 / D).then_inc(S("x_root"), 1)
            for i in range(KT):
                act.wait_ge(S(f"ada_in{i}"), 16)
                if i >= 2:
                    act.wait_ge(S("ada0_mm"), i - 1)
                act.activation(ada_hi[i % 2][:, :], ada_first[:, i, :], ACT.Copy).then_inc(S("ada_hi_done"), 1)
                t = i - 2
                if 0 <= t < TT:
                    n = ROWS[t]
                    act.wait_ge(S("x_tr"), t + 1)
                    src = bank[2 + t % 2][:, :, :].rearrange("p a (k t) -> p (a k) t", t=P)[:, :, 0:n]
                    act.activation(h32[:, :, P * t:P * t + n], src, ACT.Copy).then_inc(S("x_ch"), 1)
            act.wait_ge(S("ada0_mm"), KT)
            for g in range(2):
                act.activation(rows_ada0[:, g, :], one_bank(g)[0:18, :], ACT.Copy).then_inc(S("rows0_done"), 1)
            for n in range(3):
                high(n)
            for i in range(KT):
                act.wait_ge(S("h32_done"), i + 1)
                act.activation(h_hi[:, i, :], h32[:, i, :], ACT.Copy).then_inc(S("h_hi_done"), 1)
            act.wait_ge(S("lr_mm"), 1)
            act.activation(halves(lr[:, :]), bank[3][0:RANK, :, 0:HALF], ACT.Copy).then_inc(S("lr_done"), 1)
            for n in range(8):
                high(n + 3)
                dst = (k if n < 4 else q)[:, n % 4, :]
                act.wait_ge(S("ring_free"), n + 1)
                act.activation(halves(dst), out2(n % 3), ACT.Copy, scale=1.0 if n < 4 else DK ** -0.5) \
                   .then_inc(S("kq_done"), 1)
                if n < 4:
                    act.wait_ge(S("z_mm"), n + 1)
                    act.activation(halves(suf[:, n, :]), out2(3), ACT.Abs, bias=prm[:, B_A + n:B_A + n + 1]) \
                       .then_inc(S("z_abs"), 1)
            act.wait_ge(S("z_abs"), 4)
            act.activation(suf[:, :, :], suf[:, :, :], ACT.Exp, scale=-1.0).then_inc(S("z_exp"), 1)
            act.wait_ge(S("z_exp"), 1)
            act.activation(suf[:, :, :], suf[:, :, :], ACT.Ln, bias=one[:, :]).then_inc(S("z_ln"), 1)
            for n in range(TILE_V, TILE_C1):
                high(n + 3)
                if n % 4 == 3:
                    for t in range(TT):
                        m, c = ROWS[t], (n - TILE_V) // 4
                        if t < TT - 1:
                            act.wait_ge(S("v_mm"), (TT - 1) * c + t + 1)
                        else:
                            act.wait_ge(S("ring_free"), n + 1)
                        act.activation(v_tok[0:m, t, 512 * c:512 * c + 512], one_bank((TT * c + t) % 8)[0:m, :], ACT.Copy) \
                           .then_inc(S("v_done"), 1)
            for j in range(KT):
                n = TILE_C1 + 8 * j
                high(n + 3)
                act.wait_ge(S("ring_free"), n + 1)
                if j > 0:
                    act.wait_ge(S("u_done"), 3 * j)
                act.activation(halves(buf_a[:, :]), out2(c1_pair(j, 0)), ACT.Copy).then_inc(S("cg_done"), 1)
                for m in range(n + 4, n + 9):
                    high(m)
                if j + 1 < KT:
                    qd_exp(act, j + 1)
                else:
                    act.wait_ge(S("level_set"), KT)
                    act.activation(suf[:, :, :], suf[:, :, :], ACT.Exp, scale=TAU_INV).then_inc(S("exps"), 1)
                high(n + 9)
                if j == KT - 1:
                    act.activation(pre[:, :, :], pre[:, :, :], ACT.Exp, scale=TAU_INV).then_inc(S("exps"), 1)
                if 0 < j < KT - 1:
                    kd_exp(act, j + 1)
                high(n + 10)
                act.wait_ge(S("ring_free"), n + 7)
                if j > 0:
                    act.wait_ge(S("ya_done"), j)
                act.activation(halves(buf_b[:, :]), out2(c1_pair(j, 3)), ACT.Sigmoid).then_inc(S("sga_done"), 1)
            def m_high(i):
                act.wait_ge(S("m_done"), i + 1)
                act.activation(m_hi[:, i, :], gated[i % 2], ACT.Copy).then_inc(S("m_hi_done"), 1)

            for h in range(HEADS):
                n = TILE_C2 + 4 * h
                last = h == HEADS - 1
                high(n + 3)
                if last:
                    high(TILE_WO)
                if h == 0:
                    act.wait_ge(S("tails_tr"), 1)
                    act.activation(tails_out[0:16, 0, :], one_bank(6)[0:16, 0:P], ACT.Copy).then_inc(S("tails_out"), 1)
                    act.activation(tails_out[:, 1, :], one_bank(6)[:, P:2 * P], ACT.Copy).then_inc(S("tails_out"), 1)
                else:
                    m_high(2 * h - 2)
                    m_high(2 * h - 1)

                def sigmoid_r(e):
                    act.wait_ge(S("ring_free"), n + 2 * e + 1)
                    if h > 0 or e > 0:
                        act.wait_ge(S("silu_r"), 2 * h + e)
                    else:
                        act.wait_ge(S("u_done"), 3 * KT)
                    act.activation(halves(buf_a[:, :]), out2(0), ACT.Sigmoid).then_inc(S("sr_done"), 1)

                def sigmoid_b(e):
                    act.wait_ge(S("ring_free"), n + 2 * e + 2)
                    if h > 0 or e > 0:
                        act.wait_ge(S("gb_used"), 2 * h + e)
                    else:
                        act.wait_ge(S("ya_done"), KT)
                    act.activation(halves(buf_b[:, :]), out2(1), ACT.Sigmoid).then_inc(S("sgb_done"), 1)

                sigmoid_r(0)
                act.wait_ge(S("k_tr"), h + 1)
                if h == 0:
                    act.wait_ge(S("decayed"), 1)
                else:
                    act.wait_ge(S("delta_mm"), h)
                    act.wait_ge(S("k_own"), h)
                act.activation(k_tok[:, 0:NCH, :], bank[2][:, 0, :].rearrange("p (c d) -> p c d", d=DK), ACT.Copy) \
                   .then_inc(S("k_tok_done"), 1)
                act.activation(k_tok[0:64, NCH, :], bank[2][0:64, 1, 0:DK], ACT.Copy).then_inc(S("k_tok_done"), 1)
                high(n + 4 if not last else TILE_WO + 1)
                sigmoid_b(0)
                if last:
                    high(TILE_WO + 2)
                act.wait_ge(S("o_mm"), h + 1)
                if h == 0:
                    act.wait_ge(S("back"), KT)
                else:
                    act.wait_ge(S("o_tr"), 2 * h)
                act.activation(o_tok[:, 0:NCH, :].rearrange("p c v -> p (c v)"), flat(2), ACT.Copy).then_inc(S("o_done"), 1)
                high(n + 5 if not last else TILE_WO + 3)
                act.wait_ge(S("o_done"), 2 * h + 1)
                for c in range(TT):
                    m = ROWS[c]
                    if c == NCH:
                        act.wait_ge(S("os_mm"), h + 1)
                        act.activation(o_tok[0:64, NCH, :], bank[2][0:64, 0, 0:DV], ACT.Copy).then_inc(S("o_done"), 1)
                        act.wait_ge(S("o_done"), 2 * h + 2)
                    if c + h > 0:
                        act.wait_ge(S("o_sq"), TT * h + c)
                    act.activation(sq_o[0:m, :], o_tok[0:m, c, :], ACT.Square, accum_out=st_o[0:m, 0, c:c + 1]) \
                       .then_inc(S("o_sq"), 1)
                sigmoid_r(1)
                if not last:
                    high(n + 6)
                act.wait_ge(S("o_sq"), TT * h + TT)
                act.activation(st_o[:, 1, 0:NCH], st_o[:, 0, 0:NCH], ACT.Sqrt, bias=eps[:, :], scale=1.0 / DV) \
                   .then_inc(S("o_root"), 1)
                act.activation(st_o[0:64, 1, NCH:TT], st_o[0:64, 0, NCH:TT], ACT.Sqrt, bias=eps[0:64, :], scale=1.0 / DV) \
                   .then_inc(S("o_root"), 1)
                if last:
                    high(TILE_WO + 4)
                    high(TILE_WO + 5)
                sigmoid_b(1)
            m_high(KT - 2)
            high(TILE_WO + 6)
            m_high(KT - 1)
            high(TILE_WO + 7)
            act_out(act, high)
            def ffn_up(i):
                for e in range(2):
                    n = TILE_UP + 2 * e
                    high(n + 3, i)
                    act.wait_ge(S("ring_free"), i * 4 + freed(n))
                    if e == 1 or not isinstance(i, int) or i > 0:
                        act.wait_ge(S("ftail_done"), i * 4 + 2 * e)
                    for src, dst, _, _ in conv_pieces(2 * e, ext, 2, TS + 2, 2):
                        act.activation(dst, src, ACT.Copy).then_inc(S("a_done"), 1)
                    high(n + 4, i)
                    act.wait_ge(S("fconv"), i * 6 + (3 * e + 3))
                    act.activation(cv[:, :], cv[:, :], ACT.Gelu_apprx_tanh).then_inc(S("gelu_done"), 1)
                    act.wait_ge(S("f_done"), i * 6 + (3 * e + 3))
                    act.activation(row(f_hi, i * 2 + e), buf_b[:, 0:SEQ], ACT.Copy).then_inc(S("f_hi_done"), 1)
                    act.activation(row(f_smp, i * 2 + e)[:, 0:64], buf_b[:, SEQ:T], ACT.Copy).then_inc(S("f_hi_done"), 1)

            act.wait_ge(S("ext_zero"), 2)
            ffn_up(0)
            with act.Fori(1, FT // 2) as i:
                ffn_up(i)
            for n in range(TILE_DN, TILES):
                high(n + 3)
                if n == TILE_DN + 2:
                    act.wait_ge(S("ftails_tr"), 1)
                    for i in range(4):
                        m = (P, P, 96, 44)[i]
                        act.activation(ftails_out[0:m, i, :], one_bank(5)[0:m, P * i:P * i + P], ACT.Copy) \
                           .then_inc(S("ftails_out"), 1)
                if n == TILE_DN + 10:
                    for t in range(TT):
                        m = ROWS[t]
                        if t < TT - 1:
                            act.wait_ge(S("dn_mm"), t + 1)
                        else:
                            act.wait_ge(S("ring_free"), freed(n))
                        if t > 0:
                            act.wait_ge(S("f_sq"), t)
                        if t == NCH:
                            act.activation(smp_low[:, 0, :], one_bank(t)[64:P, :], ACT.Copy).then_inc(S("smp_low"), 1)
                            act.wait_ge(S("yh_done"), TT)
                            act.activation(sq_half[0:m, :], y_half[0:m, t, :], ACT.Square, accum_out=st_f[0:m, 0, t:t + 1]) \
                               .then_inc(S("f_sq"), 1)
                            continue
                        act.activation(sq_half[0:m, :], one_bank(t)[0:m, :], ACT.Square, accum_out=st_f[0:m, 0, t:t + 1]) \
                           .then_inc(S("f_sq"), 1)
                        act.activation(y_half[0:m, t, :], one_bank(t)[0:m, :], ACT.Copy).then_inc(S("yh_done"), 1)
            for t in range(TT):
                m = ROWS[t]
                act.wait_ge(S("dn_mm"), TT - 1 + t + 1)
                src = one_bank((TT + t) % 8)[0:m, :]
                if t == NCH:
                    act.activation(smp_low[:, 1, :], one_bank((TT + t) % 8)[64:P, :], ACT.Copy).then_inc(S("smp_low"), 1)
                    act.wait_ge(S("smp_low"), 3)
                    src = smp_low[:, 1, :]
                act.wait_ge(S("f_sq"), TT + t)
                act.activation(sq_half[0:m, :], src, ACT.Square, accum_out=st_f[0:m, 1, t:t + 1]) \
                   .then_inc(S("f_sq"), 1)
                act.wait_ge(S("f_sum"), t + 1)
                act.activation(st_f[0:m, 3, t:t + 1], st_f[0:m, 2, t:t + 1], ACT.Sqrt, bias=eps[0:m, :], scale=1.0 / D) \
                   .then_inc(S("f_root"), 1)

        @block.vector
        def _(dve):
            dve.wait_ge(S("c_sig"), 1)
            dve.tensor_tensor(c_t[:, :].rearrange("p (j s) -> p s j", j=KT),
                              one_bank(2)[:, 0:72].rearrange("p (s j) -> p s j", j=KT),
                              c_sig[:, :].rearrange("p (s j) -> p s j", j=KT), ALU.mult).then_inc(S("c_done"), 1)
            c_view = c_t[:, :].rearrange("p (j s) -> p j s", j=KT)
            dve.wait_ge(S("c_done"), 1)
            dve.tensor_copy(c_hl[:, :, 0:9], c_view).then_inc(S("c_split"), 1)
            dve.wait_ge(S("c_split"), 1)
            dve.tensor_tensor(c_hl[:, :, 9:18], c_view, c_hl[:, :, 0:9].bitcast(F32), ALU.subtract).then_inc(S("c_split"), 1)
            dve.wait_ge(S("consts"), 1)
            dve.tensor_tensor(fold[:, :], ident[0:18, 0:9], ident[0:18, 9:18], ALU.add).then_inc(S("c_split"), 1)
            def normalise(t):
                n = ROWS[t]
                dve.wait_ge(S("x_root"), t + 1)
                dve.reciprocal(st_x[0:n, 2, t:t + 1], st_x[0:n, 1, t:t + 1]).then_inc(S("x_rstd"), 1)
                dve.wait_ge(S("x_rstd"), t + 1)
                dve.tensor_scalar(x_tok[0:n, t, :], x_tok[0:n, t, :], st_x[0:n, 2, t:t + 1], None, ALU.mult) \
                   .then_inc(S("xn_done"), 1)

            normalise(0)
            normalise(1)
            for i in range(KT):
                if i + 2 < TT:
                    normalise(i + 2)
                dve.wait_ge(S("ada_hi_done"), i + 1)
                if i >= 2:
                    dve.wait_ge(S("ada0_mm"), i - 1)
                dve.tensor_tensor(ada_lo[i % 2][:, :], ada_first[:, i, :], ada_hi[i % 2][:, :].bitcast(F32), ALU.subtract) \
                   .then_inc(S("ada_lo_done"), 1)
                if i == KT - 2:
                    dve.wait_ge(S("rows_tr"), 1)
                    dve.tensor_copy(prm[:, :], one_bank(6)[:, 0:124]).then_inc(S("prm_done"), 1)
                    dve.tensor_copy(ffp[:, :], one_bank(6)[:, P:P + 88]).then_inc(S("prm_done"), 1)
                    dve.tensor_copy(mix0[:, :, :].rearrange("p a j -> p (a j)"), one_bank(7)[:, 0:P]).then_inc(S("prm_done"), 1)
                    dve.tensor_copy(ff0[:, :, :].rearrange("p a j -> p (a j)"), one_bank(7)[:, P:P + 352]) \
                       .then_inc(S("prm_done"), 1)
            dve.wait_ge(S("ada0_mm"), KT)
            for g in range(2, 4):
                dve.tensor_copy(rows_ada0[:, g, :], one_bank(g)[0:18, :]).then_inc(S("rows0_done"), 1)
            dve.wait_ge(S("back0"), 1)
            dve.wait_ge(S("prm_done"), 4)
            dve.tensor_tensor(mod[:, 0:16, :], one_bank(4)[:, 0:144].rearrange("p (m s) -> p m s", s=9),
                              spread(prm[:, 0:16], 9),
                              ALU.add).then_inc(S("mod_done"), 1)
            dve.wait_ge(S("mod_done"), 1)
            dve.scalar_tensor_tensor(mul1[:, :, :], mod[:, 8:16, :], 1.0, spread(prm[:, PRE1:PRE1 + 8], 9),
                                     ALU.add, ALU.mult).then_inc(S("mul1_done"), 1)
            dve.wait_ge(S("mul1_done"), 1)
            def h_low(i):
                dve.wait_ge(S("h32_done"), i + 1)
                dve.wait_ge(S("h_hi_done"), i + 1)
                dve.tensor_tensor(h_lo[:, i, :], h32[:, i, :], h_hi[:, i, :].bitcast(F32), ALU.subtract) \
                   .then_inc(S("h_lo_done"), 1)

            dve.wait_ge(S("x_ch"), TT)
            for i in range(KT):
                smp = h32[:, i, SEQ:T].rearrange("p (s t) -> p s t", t=TS)
                dve.tensor_scalar(h32[:, i, 0:SEQ], h32[:, i, 0:SEQ], mul1[:, i, 0:1], mod[:, i, 0:1], ALU.mult, ALU.add) \
                   .then_inc(S("h_prompt"), 1)
                dve.tensor_tensor(smp, smp, spread(mul1[:, i, 1:9], TS), ALU.mult) \
                   .then_inc(S("h_smp"), 1)
                if i >= 2:
                    h_low(i - 2)
                dve.wait_ge(S("h_smp"), i + 1)
                dve.wait_ge(S("h_prompt"), i + 1)
                dve.tensor_tensor(smp, smp, spread(mod[:, i, 1:9], TS), ALU.add) \
                   .then_inc(S("h32_done"), 1)
            for i in (KT - 2, KT - 1):
                h_low(i)
            for h in range(HEADS):
                dve.wait_ge(S("z_mm"), h + 1)
                dve.wait_ge(S("z_abs"), h + 1)
                dve.tensor_scalar(halves(pre[:, h, :]), out2(3), prm[:, B_A + h:B_A + h + 1], 0.0, ALU.add, ALU.min) \
                   .then_inc(S("z_min"), 1)
            dve.memset(score[:, :, :], 0.0).then_inc(S("score_zero"), 1)
            dve.wait_ge(S("z_ln"), 1)
            dve.wait_ge(S("z_min"), 4)
            dve.tensor_tensor(pre[:, :, :], pre[:, :, :], suf[:, :, :], ALU.subtract).then_inc(S("log_a"), 1)
            dve.wait_ge(S("log_a"), 1)
            dve.memset(suf[:, :, :], 0.0).then_inc(S("level_set"), 1)
            dve.memset(ext[:, 0:2], 0.0).then_inc(S("ext_zero"), 1)
            dve.wait_ge(S("ext_zero"), 1)
            dve.wait_ge(S("level_set"), 1)
            dve.wait_ge(S("score_zero"), 1)
            dve.wait_ge(S("consts"), 9)
            for j in range(KT):
                n = TILE_C1 + 8 * j
                for i in after_tile(j, 0):
                    take_item(dve, i)
                if j > 0:
                    dve.wait_ge(S("tail_done"), 2 * j)
                    dve.wait_ge(S("conv"), 3 * j)
                hist = ext[:, S0E:EXT].rearrange("p (s w) -> p s w", w=TS + 2)[:, :, 0:2]
                dve.tensor_copy(hist, mix0[:, :, j].rearrange("p (s w) -> p s w", w=2)).then_inc(S("hist"), 1)
                dve.wait_ge(S("cg_done"), j + 1)
                dve.wait_ge(S("ring_free"), n + 3)
                for src, dst, lo, hi in conv_pieces(c1_pair(j, 1), ext, 2, TS + 2, 2):
                    dve.tensor_tensor(dst, src, piece(buf_a, lo, hi), ALU.mult).then_inc(S("u_done"), 1)
                for i in after_tile(j, 2):
                    take_item(dve, i)
                dve.wait_ge(S("u_done"), 3 * (j + 1))
                dve.wait_ge(S("hist"), j + 1)
                if j > 0:
                    dve.wait_ge(S("t_done"), 3 * j)
                conv(dve, ext, cv, [prm[:, CW + 8 * w + j:CW + 8 * w + j + 1] for w in range(3)],
                     prm[:, CB + j:CB + j + 1], "conv", 3 * j)
                tails(dve, tail_mix[:, :, j], "tail_done")
                for i in after_tile(j, 4):
                    take_item(dve, i)
                dve.wait_ge(S("conv"), 3 * j + 3)
                dve.wait_ge(S("ring_free"), n + 5)
                for src, cvp, lo, hi in conv_pieces(c1_pair(j, 2), cv, 0, TS + 2, 2):
                    dve.tensor_tensor(piece(y_a[:, j, :], lo, hi), src, cvp, ALU.mult).then_inc(S("t_done"), 1)
                if j + 1 < KT:
                    dve_level(dve, j + 1)
                else:
                    dve.wait_ge(S("exps"), 1)
                    dve.tensor_tensor(k[:, :, :], k[:, :, :], suf[:, :, :], ALU.mult).then_inc(S("decayed"), 1)
                    dve.wait_ge(S("exps"), 2)
                    dve.tensor_tensor(q[:, :, :], q[:, :, :], pre[:, :, :], ALU.mult).then_inc(S("decayed"), 1)
                for i in after_tile(j, 6):
                    take_item(dve, i)
                if j > 0:
                    take_mod(dve, j - 1)
                dve.wait_ge(S("t_done"), 3 * (j + 1))
                dve.wait_ge(S("sga_done"), j + 1)
                dve.tensor_tensor(y_a[:, j, :], y_a[:, j, :], buf_b[:, :], ALU.mult).then_inc(S("ya_done"), 1)
                for i in after_tile(j, 7):
                    take_item(dve, i)
                dve.wait_ge(S("ring_free"), n + 8)
                if j > 0:
                    dve.wait_ge(S("back"), j)
                dve.tensor_copy(rows_ada[:, :], one_bank(6)[0:18, :]).then_inc(S("rows_ada"), 1)
            take_mod(dve, KT - 1)
            dve.wait_ge(S("mod_done"), 9)
            dve.scalar_tensor_tensor(mul2[:, :, :], mod[:, 32:40, :], 1.0, spread(prm[:, PRE2:PRE2 + 8], 9),
                                     ALU.add, ALU.mult).then_inc(S("scales"), 1)
            dve.tensor_tensor(g1n[:, :, :], mod[:, 16:24, :], spread(prm[:, POST1:POST1 + 8], 9),
                              ALU.mult).then_inc(S("scales"), 1)
            dve.tensor_tensor(g2n[:, :, :], mod[:, 40:48, :], spread(prm[:, POST2:POST2 + 8], 9),
                              ALU.mult).then_inc(S("scales"), 1)
            dve.wait_ge(S("scales"), 3)
            dve.tensor_copy(gx[:, :, :].rearrange("p k (s t) -> p k s t", t=TS), spread(g1n[:, :, 1:9], TS)) \
               .then_inc(S("gx_done"), 1)
            def merge(j):
                g = gated[j % 2]
                dve.wait_ge(S("gb_used"), j + 1)
                dve.wait_ge(S("o_tr"), j + 1)
                dve.scalar_tensor_tensor(g, flat(2 + j % 2)[:, 0:T], prm[:, GN + j:GN + j + 1], g, ALU.mult, ALU.mult) \
                   .then_inc(S("y_b"), 1)
                dve.wait_ge(S("y_b"), j + 1)
                dve.tensor_tensor(g, g, y_a[:, j, :], ALU.add).then_inc(S("m_done"), 1)

            def m_low(j):
                dve.wait_ge(S("m_done"), j + 1)
                dve.wait_ge(S("m_hi_done"), j + 1)
                dve.tensor_tensor(m_lo[:, m_row(j), :], gated[j % 2], m_hi[:, j, :].bitcast(F32), ALU.subtract) \
                   .then_inc(S("m_lo_done"), 1)

            def gate_b(j):
                dve.wait_ge(S("silu_r"), j + 1)
                dve.wait_ge(S("sgb_done"), j + 1)
                dve.tensor_tensor(gated[j % 2], gated[j % 2], buf_b[:, :], ALU.mult).then_inc(S("gb_used"), 1)

            def finish_head(h):
                merge(2 * h)
                gate_b(2 * h + 1)
                merge(2 * h + 1)
                m_low(2 * h)
                m_low(2 * h + 1)

            for h in range(HEADS):
                if h > 0:
                    finish_head(h - 1)

                def silu(e):
                    j = 2 * h + e
                    dve.wait_ge(S("sr_done"), j + 1)
                    if j < 2:
                        dve.wait_ge(S("t_done"), 3 * KT)
                        dve.wait_ge(S("tail_done"), 2 * KT)
                    else:
                        dve.wait_ge(S("m_lo_done"), j - 1)
                    dve.tensor_tensor(halves(gated[e]), out2(0), halves(buf_a[:, :]), ALU.mult).then_inc(S("silu_r"), 1)

                silu(0)
                dve.wait_ge(S("delta_mm"), h + 1)
                if h > 0:
                    dve.wait_ge(S("state_stored"), 16 * h)
                    dve.wait_ge(S("o_mm"), h)
                for c in range(NCH):
                    delta = flat(3)[:, DV * c:DV * c + DV]
                    if c == 0:
                        dve.tensor_copy(state[:, 0, :], delta).then_inc(S("state_done"), 1)
                    else:
                        dve.wait_ge(S("state_done"), NCH * h + c)
                        dve.scalar_tensor_tensor(state[:, c, :], state[:, c - 1, :], pre[:, h, P * c + P - 1:P * c + P],
                                                 delta, ALU.mult, ALU.add).then_inc(S("state_done"), 1)
                gate_b(2 * h)

                def sample_states(u):
                    dve.wait_ge(S("ds_mm"), u + 1)
                    dve.wait_ge(S("os_mm"), h + 1)
                    for s in range(4):
                        tok = SEQ + (4 * (u % 2) + s) * TS + TS - 1
                        dve.scalar_tensor_tensor(s_in[u % 3][:, s, :], s_in[u % 3][:, s, :], pre[:, h, tok:tok + 1],
                                                 flat(3)[:, DV * s:DV * s + DV], ALU.mult, ALU.add).then_inc(S("s_done"), 1)

                sample_states(2 * h)
                silu(1)
                sample_states(2 * h + 1)
                dve.wait_ge(S("o_root"), 2 * h + 2)
                dve.reciprocal(st_o[:, 2, 0:NCH], st_o[:, 1, 0:NCH]).then_inc(S("o_rstd"), 1)
                dve.reciprocal(st_o[0:64, 2, NCH:TT], st_o[0:64, 1, NCH:TT]).then_inc(S("o_rstd"), 1)
                dve.wait_ge(S("o_rstd"), 2 * h + 2)
                for c in range(TT):
                    m = ROWS[c]
                    dve.tensor_scalar(o_tok[0:m, c, :], o_tok[0:m, c, :], st_o[0:m, 2, c:c + 1], None, ALU.mult) \
                       .then_inc(S("o_norm"), 1)
            finish_head(HEADS - 1)
            dve.wait_ge(S("m_lo_done"), KT)
            dve.memset(ext[:, 0:2], 0.0).then_inc(S("ext_zero"), 1)
            for g in range(2):
                dve.wait_ge(S("gate1_mm"), g + 1)
                dve.wait_ge(S("s_done"), 32)
                m = P if g == 0 else 64
                dve.tensor_copy(gate1[0:m, g, :], flat(g)[0:m, :]) \
                   .then_inc(S("gate1_done"), 1)
            dve.wait_ge(S("x_back"), 32)
            dve.wait_ge(S("s_stored0"), 48)
            dve.wait_ge(S("gate1_done"), 2)
            for t in range(TT):
                dve_out(dve, t)
            def ffn_mid(i):
                for e in range(2):
                    j = i * 2 + e
                    col = (lambda x: ffp[:, j + x:j + x + 1]) if isinstance(i, int) else (lambda x: ffp[:, bass.ds(j + x, 1)])
                    n = TILE_UP + 2 * e
                    later = e == 1 or not isinstance(i, int) or i > 0
                    if later:
                        dve.wait_ge(S("ftail_done"), i * 4 + 2 * e)
                    hist = ext[:, S0E:EXT].rearrange("p (s w) -> p s w", w=TS + 2)[:, :, 0:2]
                    if isinstance(i, int):
                        old = ff0[:, :, j].rearrange("p (s w) -> p s w", w=2)
                        new = tail_ff[:, :, j]
                    else:
                        old = ff0[:, :, bass.ds(j, 1)].rearrange("p (s w) o -> p s (w o)", w=2)
                        new = tail_ff[:, :, bass.ds(j, 1)].rearrange("p a o -> p (a o)")
                    dve.tensor_copy(hist, old).then_inc(S("fhist"), 1)
                    dve.wait_ge(S("a_done"), i * 6 + (3 * e + 3))
                    dve.wait_ge(S("fhist"), i * 2 + (e + 1))
                    if later:
                        dve.wait_ge(S("f_done"), i * 6 + 3 * e)
                    conv(dve, ext, cv, [col(FW + FT * w) for w in range(3)], col(FB), "fconv", i * 6 + 3 * e)
                    tails(dve, new, "ftail_done")
                    dve.wait_ge(S("gelu_done"), i * 2 + (e + 1))
                    dve.wait_ge(S("ring_free"), i * 4 + freed(n + 1))
                    for src, cvp, lo, hi in conv_pieces(2 * e + 1, cv, 0, TS + 2, 2):
                        dve.tensor_tensor(piece(buf_b, lo, hi), src, cvp, ALU.mult).then_inc(S("f_done"), 1)
                    dve.wait_ge(S("f_done"), i * 6 + (3 * e + 3))
                    dve.wait_ge(S("f_hi_done"), i * 4 + (2 * e + 2))
                    dve.tensor_tensor(row(f_lo, j), buf_b[:, 0:SEQ], row(f_hi, j).bitcast(F32), ALU.subtract) \
                       .then_inc(S("f_lo_done"), 1)
                    dve.tensor_tensor(row(f_smp, j)[:, 64:P], buf_b[:, SEQ:T], row(f_smp, j)[:, 0:64].bitcast(F32),
                                      ALU.subtract).then_inc(S("f_lo_done"), 1)

            dve.wait_ge(S("ext_zero"), 2)
            ffn_mid(0)
            with dve.Fori(1, FT // 2) as i:
                ffn_mid(i)
            dve.tensor_copy(gx[:, :, :].rearrange("p k (s t) -> p k s t", t=TS), spread(g2n[:, :, 1:9], TS)) \
               .then_inc(S("gx_done"), 1)
            for g in range(2):
                dve.wait_ge(S("gate2_mm"), g + 1)
                m = P if g == 0 else 64
                dve.tensor_copy(gate2[0:m, g, :], bank[3][0:m, :, :].rearrange("p a c -> p (a c)")) \
                   .then_inc(S("gate2_done"), 1)
            dve.wait_ge(S("smp_low"), 1)
            dve.wait_ge(S("yh_done"), NCH)
            dve.tensor_tensor(y_half[0:64, NCH, :], one_bank(NCH)[0:64, :], smp_low[:, 0, :], ALU.add).then_inc(S("yh_done"), 1)
            for t in range(TT):
                m, g = ROWS[t], t // 4
                y_last = one_bank((TT + t) % 8)[0:m, :]
                if t == NCH:
                    dve.wait_ge(S("smp_low"), 2)
                    dve.tensor_tensor(smp_low[:, 1, :], y_last, smp_low[:, 1, :], ALU.add).then_inc(S("smp_low"), 1)
                    dve.wait_ge(S("smp_low"), 3)
                    y_last = smp_low[:, 1, :]
                dve.wait_ge(S("f_sq"), TT + t + 1)
                dve.wait_ge(S("gate2_done"), 2)
                dve.tensor_tensor(st_f[0:m, 2, t:t + 1], st_f[0:m, 0, t:t + 1], st_f[0:m, 1, t:t + 1], ALU.add) \
                   .then_inc(S("f_sum"), 1)
                dve.wait_ge(S("f_root"), t + 1)
                dve.reciprocal(st_f[0:m, 2, t:t + 1], st_f[0:m, 3, t:t + 1]).then_inc(S("f_rstd"), 1)
                dve.wait_ge(S("f_rstd"), t + 1)
                dve.wait_ge(S("yh_done"), t + 1)
                dve.scalar_tensor_tensor(y_half[0:m, t, :], y_half[0:m, t, :], st_f[0:m, 2, t:t + 1],
                                         gate2[0:m, g, 0:512], ALU.mult, ALU.mult).then_inc(S("fin_a"), 1)
                if t > 0:
                    dve.wait_ge(S("y_out"), t)
                dve.scalar_tensor_tensor(buf_fin[0:m, :], y_last, st_f[0:m, 2, t:t + 1],
                                         gate2[0:m, g, 512:1024], ALU.mult, ALU.mult).then_inc(S("fin_a"), 1)
                dve.wait_ge(S("fin_a"), 2 * t + 1)
                dve.tensor_tensor(x_tok[0:m, t, 0:512], x_tok[0:m, t, 0:512], y_half[0:m, t, :], ALU.add)
                dve.wait_ge(S("fin_a"), 2 * t + 2)
                dve.tensor_tensor(x_tok[0:m, t, 512:1024], x_tok[0:m, t, 512:1024], buf_fin[0:m, :], ALU.add) \
                   .then_inc(S("y_out"), 1)

        @block.tensor
        def _(pe):
            pe.wait_ge(S("consts"), 1)
            pe.wait_ge(S("c_in"), 32)
            pe.transpose(one_bank(2)[:, 0:72], rows_c[0:72, :], ident[0:72, 0:72]).then_inc(S("c_tr"), 1)

            def parameters():
                pe.wait_ge(S("rows_in"), 16 * 15)
                pe.wait_ge(S("x_ch"), 4)
                pe.transpose(one_bank(6)[:, 0:124], rows[0:124, :], ident[0:124, 0:124])
                pe.transpose(one_bank(6)[:, P:P + 88], rows_ffn[0:88, :], ident[0:88, 0:88])
                pe.transpose(one_bank(7)[:, 0:P], rows_mix[:, :], ident[:, :])
                for i in range(3):
                    n = min(P, 352 - P * i)
                    ins = pe.transpose(one_bank(7)[:, P + P * i:P + P * i + n], rows_ff0[0:n, i, :], ident[0:n, 0:n])
                ins.then_inc(S("rows_tr"), 1)

            def ada(dst, i, hi, lo, first, last):
                for p, w in enumerate((hi, lo)):
                    ins = pe.matmul(dst, c_hl[:, i, :], w, start=first and p == 0, stop=last and p == 1)
                return ins

            def ada_first_rows(i):
                pe.wait_ge(S("ada_lo_done"), i + 1)
                for g in range(4):
                    ins = ada(one_bank(g)[0:18, :], i, ada_hi[i % 2][:, 512 * g:512 * g + 512],
                              ada_lo[i % 2][:, 512 * g:512 * g + 512], i == 0, i == KT - 1)
                ins.then_inc(S("ada0_mm"), 1)

            pe.wait_ge(S("c_split"), 3)
            for i in range(KT):
                if i < TT:
                    n = ROWS[i]
                    pe.wait_ge(S("xn_done"), i + 1)
                    if i >= 2:
                        pe.wait_ge(S("x_ch"), i - 1)
                    for m in range(KT):
                        dst = bank[2 + i % 2][:, m // 4, P * (m % 4):P * (m % 4) + n]
                        ins = pe.transpose(dst, x_tok[0:n, i, P * m:P * m + P], ident[0:n, 0:n])
                    ins.then_inc(S("x_tr"), 1)
                ada_first_rows(i)
                if i == TT:
                    parameters()
            pe.wait_ge(S("rows0_done"), 4)
            pe.wait_ge(S("x_ch"), TT)
            for m in range(16):
                ins = pe.matmul(one_bank(4)[:, 9 * m:9 * m + 9], rows_ada0[:, m // 4, P * (m % 4):P * (m % 4) + P],
                                fold[:, :], start=True, stop=True)
            ins.then_inc(S("back0"), 1)

            def lr_rows(i):
                pe.wait_ge(S("h32_done"), i + 1)
                for half in range(2):
                    ins = pe.matmul(bank[3][0:RANK, half, 0:HALF], w_lr[:, i, :],
                                    h32[:, i, HALF * half:HALF * half + HALF], start=i == 0, stop=i == KT - 1)
                if i == KT - 1:
                    ins.then_inc(S("lr_mm"), 1)

            def channel_tile(hi, lo, pair, xs, first=False, part=None, token_halves=(0, 1)):
                x_hi, x_lo = xs
                for i in range(KT) if part is None else range(4 * part, 4 * part + 4):
                    if first:
                        lr_rows(i)
                        pe.wait_ge(S("h_lo_done"), i + 1)
                    for w, x, p in ((hi, x_hi, 0), (hi, x_lo, 1), (lo, x_hi, 2)):
                        for half in token_halves:
                            ins = pe.matmul(bank[pair][:, half, 0:HALF], w[:, i, :],
                                            x[:, i, HALF * half:HALF * half + HALF],
                                            start=i == 0 and p == 0, stop=i == KT - 1 and p == 2)
                if part != 0 and token_halves[-1] == 1:
                    ins.then_inc(S("ring_free"), 1)

            pe.wait_ge(S("lr_in"), 32)
            for n in range(8):
                pe.wait_ge(S("w_lo_done"), n + 1)
                if n >= 3:
                    pe.wait_ge(S("kq_done"), n - 2)
                channel_tile(kc(w_hi[n % 4]), kc(w_lo[n % 4]), n % 3, (h_hi, h_lo), first=n == 0)
                if n < 4:
                    pe.wait_ge(S("lr_done"), 1)
                    if n > 0:
                        pe.wait_ge(S("z_min"), n)
                    for half in range(2):
                        ins = pe.matmul(bank[3][:, half, 0:HALF], w_a2[:, DK * n:DK * n + DK],
                                        lr[:, HALF * half:HALF * half + HALF], start=True, stop=True)
                    ins.then_inc(S("z_mm"), 1)

            def token_tiles(n, g, banks, x_hi, x_lo, first, last, done, tiles=range(TT), smp=None):
                wh, wl = k2(w_hi[n % 4]), k2(w_lo[n % 4])
                for t in tiles:
                    m = ROWS[t]
                    if smp is not None and t == NCH:
                        dst = one_bank(banks[t])
                        first_i, last_i = smp[:, 2 * g, :], smp[:, 2 * g + 1, :]
                        pe.matmul(dst, first_i, wh[:, 0, :], start=first, stop=False)
                        pe.matmul(dst[0:64, :], first_i[:, 0:64], wl[:, 0, :], start=False, stop=False)
                        pe.matmul(dst[0:64, :], last_i[:, 0:64], wl[:, 1, :], start=False, stop=False)
                        ins = pe.matmul(dst, last_i, wh[:, 1, :], start=False, stop=last)
                        continue
                    for i in range(2):
                        xh = x_hi[:, 2 * g + i, P * t:P * t + m]
                        xl = x_lo[:, 2 * g + i, P * t:P * t + m]
                        for p, (x, w) in enumerate(((xh, wh), (xh, wl), (xl, wh))):
                            ins = pe.matmul(one_bank(banks[t])[0:m, :], x, w[:, i, :],
                                            start=first and i == 0 and p == 0, stop=last and i == 1 and p == 2)
                    if last and done and t < TT - 1:
                        ins.then_inc(S(done), 1)
                return ins

            for n in range(8):
                c = n // 4
                pe.wait_ge(S("w_lo_done"), TILE_V + n + 1)
                if n == 0:
                    pe.wait_ge(S("kq_done"), 8)
                if n == 4:
                    pe.wait_ge(S("z_min"), 4)
                    pe.wait_ge(S("v_done"), 2)
                ins = token_tiles(TILE_V + n, n % 4, [(TT * c + t) % 8 for t in range(TT)], h_hi, h_lo,
                                  n % 4 == 0, n % 4 == 3, "v_mm")
                ins.then_inc(S("ring_free"), 1)
            pe.wait_ge(S("v_done"), 2 * TT)

            def score_item(i):
                lv, chunks = items[i]
                B = LEVELS[lv]
                dst = one_bank(7)
                if B:
                    pe.wait_ge(S("qd_done"), lv)
                    if B > 1:
                        pe.wait_ge(S("kd_done"), lv - 1)
                if i > 0:
                    pe.wait_ge(S("item_taken"), i)
                if lv >= 2:
                    pe.wait_ge(S("mod_done"), lv)
                kk = kd if B > 1 else k
                col = 0
                for c in chunks:
                    w = ROWS[c]
                    for h in range(HEADS):
                        lhs = kk[:, h, P * c:P * c + w]
                        if B == 0:
                            rhs, n = q[:, h, P * c:P * c + w], w
                        else:
                            at_ = (h * T + P * c) // 2 if B < 8 else (h * SEQ + P * c) // 2
                            rhs, n = qd[:, at_:at_ + w // 2], w // 2
                        ins = pe.matmul(dst[0:w, col:col + n], lhs, rhs, start=True, stop=True)
                        col += n
                ins.then_inc(S("item"), 1)

            def mod_back(j):
                pe.wait_ge(S("rows_ada"), j + 1)
                pe.wait_ge(S("item_taken"), items_to(min(j + 1, KT - 1)))
                if j > 0:
                    pe.wait_ge(S("mod_done"), j + 1)
                for m in range(4):
                    ins = pe.matmul(one_bank(7)[:, 9 * m:9 * m + 9], rows_ada[:, P * m:P * m + P], fold[:, :],
                                    start=True, stop=True)
                ins.then_inc(S("back"), 1)

            for j in range(KT):
                for e in range(8):
                    n = TILE_C1 + 8 * j + e
                    pe.wait_ge(S("w_lo_done"), n + 1)
                    if e % 2 == 0:
                        before = 4 * j + e // 2 - 3
                        if before >= 0:
                            name, count = (("cg_done", 1), ("u_done", 3), ("t_done", 3), ("sga_done", 1))[before % 4]
                            pe.wait_ge(S(name), count * (before // 4 + 1))
                        channel_tile(kc(w_hi[n % 4]), kc(w_lo[n % 4]), c1_pair(j, e // 2), (h_hi, h_lo))
                    else:
                        if e == 1 and j > 0:
                            pe.wait_ge(S("rows_ada"), j)
                        for i in range(2):
                            ins = ada(one_bank(6)[0:18, :], e // 2 * 2 + i, k2(w_hi[n % 4])[:, i, :], k2(w_lo[n % 4])[:, i, :],
                                      e == 1 and i == 0, e == 7 and i == 1)
                        ins.then_inc(S("ring_free"), 1)
                    for i in after_tile(j, e):
                        score_item(i)
                    if e == 6 and j > 0:
                        mod_back(j - 1)
            def tails_and_mod():
                mod_back(KT - 1)
                pe.wait_ge(S("tail_done"), 2 * KT)
                pe.transpose(one_bank(6)[0:16, 0:P], tail_mix[:, 0:2, :].rearrange("p a j -> p (a j)"), ident[:, :])
                pe.transpose(one_bank(6)[:, P:2 * P], tail_mix[:, 2:18, :].rearrange("p a j -> p (a j)"), ident[:, :]) \
                  .then_inc(S("tails_tr"), 1)

            def k_to_tokens(h):
                pe.wait_ge(S("decayed"), 1)
                if h == 0:
                    pe.wait_ge(S("u_done"), 3 * KT)
                    pe.wait_ge(S("t_done"), 3 * KT)
                else:
                    pe.wait_ge(S("y_b"), 2 * h - 1)
                for c in range(NCH):
                    pe.transpose(bank[2][:, 0, DK * c:DK * c + DK], k[:, h, P * c:P * c + P], ident[:, :])
                pe.transpose(bank[2][0:64, 1, 0:DK], k[:, h, SEQ:T], ident[:, :]).then_inc(S("k_tr"), 1)

            def state_deltas(h):
                pe.wait_ge(S("k_tok_done"), 2 * h + 1)
                if h == 0:
                    pe.wait_ge(S("mod_done"), 9)
                    pe.wait_ge(S("tails_out"), 2)
                else:
                    pe.wait_ge(S("y_b"), 2 * h)
                for c in range(NCH):
                    ins = pe.matmul(flat(3)[:, DV * c:DV * c + DV], k_tok[:, c, :], v_tok[:, c, DV * h:DV * h + DV],
                                    start=True, stop=True)
                ins.then_inc(S("delta_mm"), 1)

            def outputs(h):
                pe.wait_ge(S("k_tok_done"), 2 * h + 2)
                pe.wait_ge(S("decayed"), 2)
                pe.wait_ge(S("item_taken"), len(items))
                for c in range(NCH):
                    dst = flat(2)[:, DV * c:DV * c + DV]
                    ins = pe.matmul(dst, score[:, HEADS * c + h, :], v_tok[:, c, DV * h:DV * h + DV],
                                    start=True, stop=c == 0)
                    if c > 0:
                        pe.wait_ge(S("state_done"), NCH * h + c)
                        ins = pe.matmul(dst, q[:, h, P * c:P * c + P], state[:, c - 1, :], start=False, stop=True)
                ins.then_inc(S("o_mm"), 1)

            def sample_outputs(h):
                pe.wait_ge(S("o_done"), 2 * h + 1)
                pe.wait_ge(S("q_own"), h + 1)
                dst = bank[2][0:64, 0, 0:DV]
                pe.matmul(dst, score[0:64, HEADS * NCH + h, 0:64], v_tok[0:64, 4, DV * h:DV * h + DV], start=True, stop=False)
                for s in range(NS):
                    u = 2 * h + s // 4
                    if s % 4 == 0:
                        pe.wait_ge(S(f"s_in{u % 3}"), 16 * (u // 3 + 1))
                    ins = pe.matmul(dst, q_own[:, 64 * s:64 * s + 64], s_in[u % 3][:, s % 4, :],
                                    start=False, stop=s == NS - 1)
                ins.then_inc(S("os_mm"), 1)

            def sample_deltas(u):
                if u % 2 == 0:
                    pe.wait_ge(S("state_done"), NCH * (u // 2 + 1))
                    pe.wait_ge(S("k_own"), u // 2 + 1)
                else:
                    pe.wait_ge(S("s_done"), 4 * u)
                h, g = u // 2, u % 2
                for s in range(4):
                    ins = pe.matmul(flat(3)[:, DV * s:DV * s + DV], k_own[:, 4 * g + s, :],
                                    v_tok[0:64, 4, DV * h:DV * h + DV], start=True, stop=True)
                ins.then_inc(S("ds_mm"), 1)

            def outputs_back(h):
                pe.wait_ge(S("o_norm"), TT * (h + 1))
                pe.wait_ge(S("o_done"), 2 * h + 2)
                pe.wait_ge(S("s_done"), 8 * (h + 1))
                for e in range(2):
                    for c in range(TT):
                        m = ROWS[c]
                        ins = pe.transpose(flat(2 + e)[:, P * c:P * c + m], o_tok[0:m, c, P * e:P * e + P], ident[0:m, 0:m])
                    ins.then_inc(S("o_tr"), 1)

            for h in range(HEADS):
                for f in range(8):
                    e = f // 2
                    n = TILE_C2 + 4 * h + e
                    if f % 2 == 0:
                        pe.wait_ge(S("w_lo_done"), n + 1)
                        if h == 0 and e < 2:
                            pe.wait_ge(S("sga_done" if e else "t_done"), KT if e else 3 * KT)
                            pe.wait_ge(S("cg_done" if e else "u_done"), KT if e else 3 * KT)
                        elif e % 2 == 0:
                            pe.wait_ge(S("silu_r"), 2 * h + e // 2)
                        else:
                            pe.wait_ge(S("sgb_done"), 2 * h + e // 2)
                    channel_tile(kc(w_hi[n % 4]), kc(w_lo[n % 4]), e % 2, (h_hi, h_lo), part=f % 2)
                    if f == 0 and h == 0:
                        tails_and_mod()
                    elif f == 1:
                        k_to_tokens(h)
                    elif f == 2:
                        state_deltas(h)
                    elif f == 3:
                        outputs(h)
                    elif f == 4:
                        sample_outputs(h)
                        sample_deltas(2 * h)
                    elif f == 5:
                        sample_deltas(2 * h + 1)
                    elif f == 7:
                        outputs_back(h)

            def gate_rows(src, g, pair, done, name):
                m = P if g == 0 else 64
                if g == 1:
                    pe.wait_ge(S("gx_done"), 1 if src is g1n else 2)
                    if pair == 3:
                        pe.wait_ge(S(done), 1)
                for i in range(KT):
                    lhs = src[:, i, 0:1].to_broadcast([P, P]) if g == 0 else gx[:, i, :]
                    ins = pe.matmul(bank[pair][0:m, i // 4, P * (i % 4):P * (i % 4) + P], lhs, ident[:, :],
                                    start=True, stop=True)
                ins.then_inc(S(name), 1)

            pe.wait_ge(S("scales"), 3)
            pe.wait_ge(S("silu_r"), KT)
            gate_rows(g1n, 0, 0, "gate1_done", "gate1_mm")
            pe.wait_ge(S("sgb_done"), KT)
            gate_rows(g1n, 1, 1, "gate1_done", "gate1_mm")
            pe.wait_ge(S("m_lo_done"), KT)

            def to_channels(t):
                m = ROWS[t]
                pe.wait_ge(S("xn2_done"), t + 1)
                if t > 0:
                    pe.wait_ge(S("h2_mul"), t)
                for i in range(KT):
                    ins = pe.transpose(bank[3][:, i // 4, P * (i % 4):P * (i % 4) + m], xn[0:m, P * i:P * i + P],
                                       ident[0:m, 0:m])
                ins.then_inc(S("h_tr"), 1)

            for t in range(TT):
                m = ROWS[t]
                if t in (1, 2):
                    pe.wait_ge(S("gate1_done"), 2)
                elif t >= 3:
                    pe.wait_ge(S("y_scaled"), t - 2)
                order = range(KT) if t < TT - 1 else (2, 3, 4, 7, 0, 1, 5, 6)
                for x, i in enumerate(order):
                    wh, wl = w_pair(TILE_WO + i)
                    if t == 0:
                        pe.wait_ge(S("w_lo_done"), TILE_WO + i + 1)
                    xh, xl = m_hi[:, i, P * t:P * t + m], m_lo[:, m_row(i), P * t:P * t + m]
                    for c in range(2):
                        for p, (xx, w) in enumerate(((xh, wh), (xh, wl), (xl, wh))):
                            ins = pe.matmul(bank[wo_pair(t)][0:m, c, :], xx, w[:, 512 * c:512 * c + 512],
                                            start=x == 0 and p == 0, stop=x == KT - 1 and p == 2)
                    if t == TT - 1 and WO_SLOT[i] is not None:
                        ins.then_inc(S("ring_free"), 1)
                ins.then_inc(S("wo_mm"), 1)
                if t > 0:
                    to_channels(t - 1)
            def ffn_up(i):
                for e in range(4):
                    n = TILE_UP + e
                    pe.wait_ge(S("w_lo_done"), i * 4 + (n + 1))
                    if not isinstance(i, int) or i > 0:
                        if e < 2:
                            pe.wait_ge(S("f_done" if e % 2 else "a_done"), i * 6 - 3)
                        else:
                            pe.wait_ge(S("f_done" if e % 2 else "a_done"), i * 6)
                    channel_tile(kc(w_hi[n % 4]), kc(w_lo[n % 4]), e, (h_hi, h_lo))

            for e, half in ((0, 0), (1, 0), (2, 0), (0, 1), (1, 1), (2, 1), (3, 0), (3, 1)):
                if (e, half) == (2, 0):
                    to_channels(TT - 1)
                pe.wait_ge(S("h2_lo_done"), TT if half else 3)
                if half == 0:
                    pe.wait_ge(S("w_lo_done"), TILE_UP + e + 1)
                    if e == 3:
                        pe.wait_ge(S("h2_mul"), TT)
                    else:
                        pe.wait_ge(S("y_scaled"), (3, 5, 4)[e])
                channel_tile(kc(w_hi[e]), kc(w_lo[e]), e, (h_hi, h_lo), token_halves=(half,))
            with pe.Fori(1, FT // 2) as i:
                ffn_up(i)
            pe.wait_ge(S("f_done"), 3 * FT)
            pe.wait_ge(S("a_done"), 3 * FT)
            pe.wait_ge(S("ftail_done"), 2 * FT)
            for i in range(4):
                lo, m = ((P * i, (P, P, 96)[i]) if i < 3 else (0, 44))
                src = (tail_ff[:, 2:18, :] if i < 3 else tail_ff[:, 0:2, :]).rearrange("p a j -> p (a j)")
                ins = pe.transpose(one_bank(5)[0:m, P * i:P * i + P], src[:, lo:lo + m], ident[:, :])
            ins.then_inc(S("ftails_tr"), 1)
            for n in range(FT - 3):
                c, g = n // 11, n % 11
                pe.wait_ge(S("w_lo_done"), TILE_DN + n + 1)
                if c == 0:
                    pe.wait_ge(S("f_lo_done"), 2 * (2 * g + 2))
                if n < 2:
                    gate_rows(g2n, n, 3, "gate2_done", "gate2_mm")
                if n == 11:
                    pe.wait_ge(S("ftails_out"), 4)
                    pe.wait_ge(S("gate2_done"), 2)
                    pe.wait_ge(S("yh_done"), 2)
                token_tiles(TILE_DN + n, g, [(TT * c + t) % 8 for t in range(TT)], f_hi, f_lo, g == 0, g == 10, "dn_mm",
                            smp=f_smp) \
                    .then_inc(S("ring_free"), 1)
            pe.wait_ge(S("w_lo_done"), TILES)
            for t in range(TT):
                for n in range(FT - 3, FT):
                    ins = token_tiles(TILE_DN + n, n - 11, [(TT + x) % 8 for x in range(TT)], f_hi, f_lo, False,
                                      n == FT - 1, None, (t,), f_smp)
                ins.then_inc(S("dn_mm"), 1)


_INS = ["x_prompt", "x_sample", "c_prompt", "c_sample", "state_conv_mix", "state_gla", "state_conv_ffn",
        "w_ada", "b_ada", "norm_pre1", "norm_post1", "norm_pre2", "norm_post2", "w_in", "conv_w", "conv_b",
        "w_a2", "b_a", "gla_norm", "w_out", "w_up", "ffn_conv_w", "ffn_conv_b", "w_down"]
_OUTS = [("y_prompt", (1, SEQ, D)), ("y_sample", (NS, TS, D)),
         ("new_conv_mix_prompt", (1, 1, 2, D)), ("new_gla_prompt", (1, 1, HEADS, DK, DV)),
         ("new_conv_ffn_prompt", (1, 1, 2, FF)),
         ("new_conv_mix_sample", (1, NS, 2, D)), ("new_gla_sample", (1, NS, HEADS, DK, DV)),
         ("new_conv_ffn_sample", (1, NS, 2, FF))]


def kernel(**inputs):
    import concourse.bacc as _bacc
    from concourse.bass_utils import run_bass_kernel_spmd as _run

    nc = _bacc.Bacc("TRN2", target_bir_lowering=False, num_devices=1, dynamic_dma_scratch_size=1024)
    arrays, aps = {}, {}
    for name in _INS:
        arr = np.ascontiguousarray(inputs[name])
        arrays[f"in_{name}"] = arr
        aps[name] = nc.dram_tensor(f"in_{name}", arr.shape, mybir.dt.from_np(arr.dtype), kind="ExternalInput").ap()
    for name, shape in _OUTS:
        aps[name] = nc.dram_tensor(f"out_{name}", shape, F32, kind="ExternalOutput").ap()
    layer_program(nc, aps)
    r = _run(nc, [arrays], core_ids=[0])
    return tuple(r.results[0][f"out_{name}"] for name, _ in _OUTS)
```
